# Optimizing a Trainium2 kernel written in Bass

```python
import math
import jax, jax.numpy as jnp
from jax import lax
import numpy as np

D_MODEL = 1024
BATCH = 1
SEQ = 1024
DEPTH = 2
DEC_BATCH = 8
DEC_SEQ = 8
PAST_LEN = 1024
PAGE_SIZE = 128

HEAD_DIM = 64
BLK = 128
DILATED = ((128, 1), (512, 4), (2048, 16))
N_DIL = len(DILATED)
H_A = D_MODEL // (2 * HEAD_DIM)
D_A = H_A * HEAD_DIM
QKV_A = N_DIL * 3 * D_A
D_B = D_MODEL // 2
GROUP_CH = 16
G_B = D_B // GROUP_CH
N_STATE = 64
H_C = D_MODEL // HEAD_DIM
KV_C = H_C // 4
WIN_C = 128
D_FF = 4 * D_MODEL
D_PLE = 256
N_AB = (DEPTH + 1) // 2
N_C = DEPTH // 2
RMS_EPS = 1e-6
NEG_INF = -1e30

kernel_name = 'hybrid_dilated_s5_sinkswa_decoder_step'

def rmsnorm(x, g):
    x32 = x.astype(jnp.float32)
    y = x32 * lax.rsqrt(jnp.mean(x32 * x32, axis=-1, keepdims=True) + RMS_EPS)
    return (y * g.astype(jnp.float32)).astype(x.dtype)

def _masked_softmax_parts(s, valid):
    s = jnp.where(valid, s, NEG_INF)
    m = s.max(-1)
    pexp = jnp.exp(s - m[..., None])
    return pexp, m, pexp.sum(-1)

def banded_attn(q, k, v, n_steps):
    n, t, h, hd = q.shape
    kv = k.shape[2]
    rep = h // kv
    nb = -(-t // BLK)
    tp = nb * BLK
    pad = tp - t
    qb = jnp.pad(q, ((0, 0), (0, pad), (0, 0), (0, 0))).reshape(n, nb, BLK, kv, rep, hd)

    def key_blocks(a):
        ap = jnp.pad(a, ((0, 0), (BLK, pad), (0, 0), (0, 0)))
        prev = ap[:, :tp].reshape(n, nb, BLK, kv, hd)
        cur = ap[:, BLK:].reshape(n, nb, BLK, kv, hd)
        return jnp.concatenate([prev, cur], axis=2)

    kb, vb = key_blocks(k), key_blocks(v)
    s = jnp.einsum('nbqgrd,nbkgd->nbgrqk', qb, kb, preferred_element_type=jnp.float32) * (hd ** -0.5)
    qi = jnp.arange(BLK)[:, None]
    ki = jnp.arange(2 * BLK)[None, :]
    dist = qi + BLK - ki
    kabs = jnp.arange(nb)[:, None, None] * BLK - BLK + ki[None]
    valid = (dist >= 0) & (dist <= n_steps) & (kabs >= 0)
    pexp, m, l = _masked_softmax_parts(s, valid[None, :, None, None])
    o = jnp.einsum('nbgrqk,nbkgd->nbqgrd', pexp, vb.astype(jnp.float32))
    o = o.reshape(n, tp, h, hd)[:, :t]
    m = m.transpose(0, 1, 4, 2, 3).reshape(n, tp, h)[:, :t]
    l = l.transpose(0, 1, 4, 2, 3).reshape(n, tp, h)[:, :t]
    return o, m, l

def gathered_attn(q, kseq, vseq, n_past, dilation, n_steps):
    n, s_new, h, hd = q.shape
    kv = kseq.shape[2]
    rep = h // kv
    idx = n_past + jnp.arange(s_new)[:, None] - dilation * jnp.arange(n_steps + 1)[None, :]
    valid = idx >= 0
    idx = jnp.maximum(idx, 0)
    kg = kseq[:, idx]
    vg = vseq[:, idx]
    qg = q.reshape(n, s_new, kv, rep, hd)
    sc = jnp.einsum('nsgrd,nskgd->nsgrk', qg, kg, preferred_element_type=jnp.float32) * (hd ** -0.5)
    pexp, m, l = _masked_softmax_parts(sc, valid[None, :, None, None, :])
    o = jnp.einsum('nsgrk,nskgd->nsgrd', pexp, vg.astype(jnp.float32))
    return o.reshape(n, s_new, h, hd), m.reshape(n, s_new, h), l.reshape(n, s_new, h)

def dilated_prompt(q, k, v, dilation, n_steps):
    n, t, h, hd = q.shape
    ts = t // dilation

    def split(a):
        return a.reshape(n, ts, dilation, a.shape[2], hd).transpose(0, 2, 1, 3, 4).reshape(n * dilation, ts, a.shape[2], hd)

    o, m, l = banded_attn(split(q), split(k), split(v), n_steps)
    o = o.reshape(n, dilation, ts, h, hd).transpose(0, 2, 1, 3, 4).reshape(n, t, h, hd)
    m = m.reshape(n, dilation, ts, h).transpose(0, 2, 1, 3).reshape(n, t, h)
    l = l.reshape(n, dilation, ts, h).transpose(0, 2, 1, 3).reshape(n, t, h)
    return o, m, l

def s5_scan(u, a_re, a_im, log_dt, b_re, b_im, c_re, c_im, d_skip, h0):
    f32 = jnp.float32
    n, t, _ = u.shape
    lam = lax.complex(a_re.astype(f32), a_im.astype(f32))
    dt = jnp.exp(log_dt.astype(f32))[:, None]
    abar = jnp.exp(lam * dt)
    bbar = ((abar - 1.0) / lam)[..., None] * lax.complex(b_re.astype(f32), b_im.astype(f32))
    u32 = u.astype(f32)
    ug = u32.reshape(n, t, G_B, GROUP_CH).astype(jnp.complex64)
    bu = jnp.einsum('ntgc,gsc->ntgs', ug, bbar)
    if h0 is not None:
        bu = bu.at[:, 0].add(abar * h0)
    a = jnp.broadcast_to(abar, bu.shape)
    _, hs = lax.associative_scan(lambda e1, e2: (e1[0] * e2[0], e2[0] * e1[1] + e2[1]), (a, bu), axis=1)
    cmat = lax.complex(c_re.astype(f32), c_im.astype(f32))
    y = jnp.einsum('ntgs,gcs->ntgc', hs, cmat).real.reshape(n, t, D_B) + d_skip.astype(f32) * u32
    return y, hs[:, -1]

def mixer_ab(h, prm, j, kv_bufs, h0):
    n, t, _ = h.shape
    z = h @ prm['w_in_ab'][j]
    qkv = z[..., :QKV_A].reshape(n, t, N_DIL, 3, H_A, HEAD_DIM)
    u = z[..., QKV_A:]
    outs, ms, ls, new_bufs = [], [], [], []
    for g, (win, dil) in enumerate(DILATED):
        q, k, v = qkv[:, :, g, 0], qkv[:, :, g, 1], qkv[:, :, g, 2]
        if kv_bufs is None:
            o, m, l = dilated_prompt(q, k, v, dil, win // dil)
            keep = min(win, t)
            new_bufs.append(jnp.stack([k[:, t - keep:], v[:, t - keep:]], axis=1))
        else:
            buf = kv_bufs[g]
            n_past = buf.shape[2]
            kseq = jnp.concatenate([buf[:, 0].astype(k.dtype), k], axis=1)
            vseq = jnp.concatenate([buf[:, 1].astype(v.dtype), v], axis=1)
            o, m, l = gathered_attn(q, kseq, vseq, n_past, dil, win // dil)
            new_bufs.append(jnp.stack([kseq[:, -n_past:], vseq[:, -n_past:]], axis=1))
        outs.append(o)
        ms.append(m)
        ls.append(l)
    m_all = jnp.stack(ms)
    wts = jnp.exp(m_all - m_all.max(0))
    num = jnp.sum(wts[..., None] * jnp.stack(outs), axis=0)
    den = jnp.sum(wts * jnp.stack(ls), axis=0)
    out_a = (num / den[..., None]).reshape(n, t, D_A)
    y, h_last = s5_scan(u, prm['ssm_a_re'][j], prm['ssm_a_im'][j], prm['ssm_log_dt'][j], prm['ssm_b_re'][j],
                        prm['ssm_b_im'][j], prm['ssm_c_re'][j], prm['ssm_c_im'][j], prm['ssm_d'][j], h0)
    zb = jax.nn.gelu(y)
    out_b = zb * jax.nn.sigmoid(zb @ prm['w_glu'][j].astype(jnp.float32) + prm['b_glu'][j].astype(jnp.float32))
    mix = jnp.concatenate([out_a, out_b], axis=-1).astype(h.dtype) @ prm['w_out_ab'][j]
    return mix, new_bufs, h_last.real, h_last.imag

def mixer_c(h, w_in, w_out, sinks, kv_buf):
    n, t, _ = h.shape
    z = h @ w_in
    q = z[..., :H_C * HEAD_DIM].reshape(n, t, H_C, HEAD_DIM)
    k = z[..., H_C * HEAD_DIM:(H_C + KV_C) * HEAD_DIM].reshape(n, t, KV_C, HEAD_DIM)
    v = z[..., (H_C + KV_C) * HEAD_DIM:].reshape(n, t, KV_C, HEAD_DIM)
    if kv_buf is None:
        o, m, l = banded_attn(q, k, v, WIN_C)
        keep = min(WIN_C, t)
        new_buf = jnp.stack([k[:, t - keep:], v[:, t - keep:]], axis=1)
    else:
        n_past = kv_buf.shape[2]
        kseq = jnp.concatenate([kv_buf[:, 0].astype(k.dtype), k], axis=1)
        vseq = jnp.concatenate([kv_buf[:, 1].astype(v.dtype), v], axis=1)
        o, m, l = gathered_attn(q, kseq, vseq, n_past, 1, WIN_C)
        new_buf = jnp.stack([kseq[:, -n_past:], vseq[:, -n_past:]], axis=1)
    sk = sinks.astype(jnp.float32)
    mx = jnp.maximum(m, sk)
    sc = jnp.exp(m - mx)
    out = o * sc[..., None] / (l * sc + jnp.exp(sk - mx))[..., None]
    return out.reshape(n, t, H_C * HEAD_DIM).astype(h.dtype) @ w_out, new_buf

def trunk(x, p, caches, prm):
    new_a = [[] for _ in range(N_DIL)]
    new_re, new_im, new_c = [], [], []
    for i in range(DEPTH):
        j = i // 2
        h = rmsnorm(x, prm['g_pre_mix'][i])
        if i % 2 == 0:
            bufs = None if caches is None else [caches[g][j] for g in range(N_DIL)]
            h0 = None if caches is None else lax.complex(caches[N_DIL][j].astype(jnp.float32), caches[N_DIL + 1][j].astype(jnp.float32))
            mix, bufs_new, s_re, s_im = mixer_ab(h, prm, j, bufs, h0)
            for g in range(N_DIL):
                new_a[g].append(bufs_new[g])
            new_re.append(s_re)
            new_im.append(s_im)
        else:
            mix, c_new = mixer_c(h, prm['w_in_c'][j], prm['w_out_c'][j], prm['sinks_c'][j],
                                 None if caches is None else caches[N_DIL + 2][j])
            new_c.append(c_new)
        x = x + rmsnorm(mix, prm['g_post_mix'][i])
        hf = rmsnorm(x, prm['g_pre_ffn'][i])
        f = jnp.square(jax.nn.relu(hf @ prm['w_ff1'][i])) @ prm['w_ff2'][i]
        x = x + rmsnorm(f, prm['g_post_ffn'][i])
        gate = jax.nn.sigmoid(rmsnorm(x, prm['g_ple'][i]) @ prm['w_ple_gate'][i])
        x = x + (p[i] @ prm['w_ple'][i]) * gate
    return (x, jnp.stack(new_a[0]), jnp.stack(new_a[1]), jnp.stack(new_a[2]),
            jnp.stack(new_re), jnp.stack(new_im), jnp.stack(new_c))

def setup_inputs(seed: int = 0) -> dict:
    key = jax.random.key(seed)
    ks = iter(jax.random.split(key, 40))

    def nrm(shape, scale=1.0):
        return scale * jax.random.normal(next(ks), shape, jnp.float32)

    la = [min(w, PAST_LEN) for w, _ in DILATED]
    lc = min(WIN_C, PAST_LEN)
    d_in_c = (H_C + 2 * KV_C) * HEAD_DIM
    return {
        'x_prompt': nrm((BATCH, SEQ, D_MODEL)),
        'x_sample': nrm((DEC_BATCH, DEC_SEQ, D_MODEL)),
        'cache_a1_kv': nrm((N_AB, DEC_BATCH, 2, la[0], H_A, HEAD_DIM)),
        'cache_a2_kv': nrm((N_AB, DEC_BATCH, 2, la[1], H_A, HEAD_DIM)),
        'cache_a3_kv': nrm((N_AB, DEC_BATCH, 2, la[2], H_A, HEAD_DIM)),
        'state_b_re': nrm((N_AB, DEC_BATCH, G_B, N_STATE), 0.3),
        'state_b_im': nrm((N_AB, DEC_BATCH, G_B, N_STATE), 0.3),
        'cache_c_kv': nrm((N_C, DEC_BATCH, 2, lc, KV_C, HEAD_DIM)),
        'p_prompt': nrm((DEPTH, BATCH, SEQ, D_PLE)),
        'p_sample': nrm((DEPTH, DEC_BATCH, DEC_SEQ, D_PLE)),
        'w_in_ab': nrm((N_AB, D_MODEL, QKV_A + D_B), D_MODEL ** -0.5),
        'w_out_ab': nrm((N_AB, D_A + D_B, D_MODEL), (D_A + D_B) ** -0.5),
        'ssm_a_re': -0.5 + nrm((N_AB, G_B, N_STATE), 0.01),
        'ssm_a_im': math.pi * jnp.arange(N_STATE, dtype=jnp.float32) + nrm((N_AB, G_B, N_STATE), 0.01),
        'ssm_log_dt': jax.random.uniform(next(ks), (N_AB, G_B), jnp.float32, math.log(1e-3), math.log(1e-1)),
        'ssm_b_re': nrm((N_AB, G_B, N_STATE, GROUP_CH), (2 * GROUP_CH) ** -0.5),
        'ssm_b_im': nrm((N_AB, G_B, N_STATE, GROUP_CH), (2 * GROUP_CH) ** -0.5),
        'ssm_c_re': nrm((N_AB, G_B, GROUP_CH, N_STATE), N_STATE ** -0.5),
        'ssm_c_im': nrm((N_AB, G_B, GROUP_CH, N_STATE), N_STATE ** -0.5),
        'ssm_d': nrm((N_AB, D_B), 0.5),
        'w_glu': nrm((N_AB, D_B, D_B), D_B ** -0.5),
        'b_glu': nrm((N_AB, D_B), 0.01),
        'w_in_c': nrm((N_C, D_MODEL, d_in_c), D_MODEL ** -0.5),
        'sinks_c': nrm((N_C, H_C), 0.5),
        'w_out_c': nrm((N_C, H_C * HEAD_DIM, D_MODEL), (H_C * HEAD_DIM) ** -0.5),
        'g_pre_mix': 1.0 + nrm((DEPTH, D_MODEL), 0.01),
        'g_post_mix': 1.0 + nrm((DEPTH, D_MODEL), 0.01),
        'g_pre_ffn': 1.0 + nrm((DEPTH, D_MODEL), 0.01),
        'g_post_ffn': 1.0 + nrm((DEPTH, D_MODEL), 0.01),
        'g_ple': 1.0 + nrm((DEPTH, D_MODEL), 0.01),
        'w_ff1': nrm((DEPTH, D_MODEL, D_FF), D_MODEL ** -0.5),
        'w_ff2': nrm((DEPTH, D_FF, D_MODEL), D_FF ** -0.5),
        'w_ple': nrm((DEPTH, D_PLE, D_MODEL), D_PLE ** -0.5),
        'w_ple_gate': nrm((DEPTH, D_MODEL, D_MODEL), D_MODEL ** -0.5),
    }

def reference(x_prompt, x_sample, cache_a1_kv, cache_a2_kv, cache_a3_kv, state_b_re, state_b_im, cache_c_kv,
              p_prompt, p_sample, w_in_ab, w_out_ab, ssm_a_re, ssm_a_im, ssm_log_dt, ssm_b_re, ssm_b_im,
              ssm_c_re, ssm_c_im, ssm_d, w_glu, b_glu, w_in_c, sinks_c, w_out_c, g_pre_mix, g_post_mix,
              g_pre_ffn, g_post_ffn, g_ple, w_ff1, w_ff2, w_ple, w_ple_gate):
    prm = dict(w_in_ab=w_in_ab, w_out_ab=w_out_ab, ssm_a_re=ssm_a_re, ssm_a_im=ssm_a_im, ssm_log_dt=ssm_log_dt,
               ssm_b_re=ssm_b_re, ssm_b_im=ssm_b_im, ssm_c_re=ssm_c_re, ssm_c_im=ssm_c_im, ssm_d=ssm_d,
               w_glu=w_glu, b_glu=b_glu, w_in_c=w_in_c, sinks_c=sinks_c, w_out_c=w_out_c,
               g_pre_mix=g_pre_mix, g_post_mix=g_post_mix, g_pre_ffn=g_pre_ffn, g_post_ffn=g_post_ffn,
               g_ple=g_ple, w_ff1=w_ff1, w_ff2=w_ff2, w_ple=w_ple, w_ple_gate=w_ple_gate)
    y_prompt, a1_p, a2_p, a3_p, bre_p, bim_p, c_p = trunk(x_prompt, p_prompt, None, prm)
    caches = (cache_a1_kv, cache_a2_kv, cache_a3_kv, state_b_re, state_b_im, cache_c_kv)
    y_sample, a1_s, a2_s, a3_s, bre_s, bim_s, c_s = trunk(x_sample, p_sample, caches, prm)
    return (y_prompt, y_sample, a1_p, a1_s, a2_p, a2_s, a3_p, a3_s, bre_p, bre_s, bim_p, bim_s, c_p, c_s)


_drawn_inputs = setup_inputs


def setup_inputs(seed=0):
    import zlib

    import numpy as np

    out = dict(_drawn_inputs(seed))
    spreads = {}
    factors = {'ssm_a_re': 16.785,
     'b_glu': 24.682,
     'sinks_c': 64.0,
     'g_pre_mix': 4.034,
     'g_post_mix': 6.417,
     'g_pre_ffn': 7.064,
     'g_post_ffn': 7.204,
     'g_ple': 64.0}
    for name, (base, spread) in spreads.items():
        noise = np.random.default_rng([zlib.crc32(name.encode()), seed]).standard_normal(out[name].shape)
        drawn = base * np.exp(spread * noise) if base else spread * noise
        out[name] = __import__('jax').numpy.asarray(drawn.astype(out[name].dtype))
    for name, factor in factors.items():
        out[name] = (out[name] * factor).astype(out[name].dtype)
    return out
```

```python
from contextlib import ExitStack, contextmanager

import concourse.bass as bass
from concourse import mybir
from concourse.alu_op_type import AluOpType as ALU

F32 = mybir.dt.float32
F32R = mybir.dt.float32r
ACT = mybir.ActivationFunctionType
AX = mybir.AxisListType.X

P = 128
D_MODEL = 1024
KC = D_MODEL // P
HEAD_DIM = 64
N_STATE = 64
H_A = 8
H_C = 16
NB, NS = 8, 8
SAMPLE = NB * NS
SEQ = 1024
T = SAMPLE + SEQ + 4
CH = T // 3
PADS = SAMPLE + SEQ
DILATION = (1, 4, 16)
ROWS = (128, 512, 1024)
ROWS_C = 128
ST = 16
SLOT = 2 * T
FF_BLOCKS = 16
EPS = 1e-6
ROW = 528
GAINS = ("pre_mix", "post_mix", "pre_ffn", "post_ffn", "ple")
SK = 128 + 3 * SAMPLE + 512 + 512
SKC = ROWS_C + SAMPLE

S5_STEPS = 192
W_U, W_QKV, W_GLU, W_OUT = 0, 2, 20, (21, 69)
W_FF, W_PLE, W_GATE = (25, 73), (57, 105), (59, 107)
W_QC, W_KC, W_VC, N_SLOTS = 63, 67, 68, 111

C_GLU, C_D, C_SINK, C_SINKROW, C_EPS, N_PARAM = 80, 84, 88, 104, 105, 106

V_ARE, V_AIM, V_DT, V_X, V_R, V_TH, V_K, V_COS, V_SIN, V_ABR, V_ABI, V_CR, V_CI, V_T1, V_T2, V_T3 = range(16)
V_POW = 16
N_VEC = V_POW + 20


UNITS = ([2] * 2 + ([2] * 4 + [4] * 2) * 3 + [4] + [2] * 4 + [2] + [2, 8] * 15 + [8] + [0, 8] + [2] * 4
         + [2] * 5 + [4] + [2] * 4 + [2] + [2, 8] * 15 + [8] + [0, 8] + [2] * 4)
assert len(UNITS) == N_SLOTS
UNITS_AT = [sum(UNITS[:s]) for s in range(N_SLOTS + 1)]
LO_GLU = 8 + 4 + 4
LO_MIXED_A = LO_GLU + 9
LO_MIXED_C = LO_MIXED_A + 8 + 2 * FF_BLOCKS + 8 + 8 + 9


class Count:

    def __init__(self, sem):
        self.sem, self.base, self.extra = sem, 0, 0

    @property
    def at(self):
        return self.base + self.extra

    def add(self, n=1):
        self.extra += n
        return self.at


@contextmanager
def turns(eng, n, per):
    start = {c: c.at for c in per}
    with eng.Fori(0, n) as i:
        for c, k in per.items():
            c.base, c.extra = start[c] + i * k, 0
        yield i
    for c, k in per.items():
        assert c.extra == k, (c.sem, c.extra, k)
        c.base, c.extra = start[c] + n * k, 0


def build(nc, a):
    x_keep = nc.dram_tensor("x_keep", (P, KC, T), F32).ap()
    og = nc.dram_tensor("og", (3, SEQ, ROW), F32).ap()
    qk_keep = nc.dram_tensor("qk_keep", (P, 3, 8, SAMPLE), F32).ap()
    v_keep = nc.dram_tensor("v_keep", (SAMPLE, 3, 512), F32).ap()

    with ExitStack() as ctx:
        def region(name, cols, *stages):
            made = []
            for stage in stages:
                with ExitStack() as s:
                    for n, c, dt in stage:
                        made.append(s.enter_context(nc.sbuf_tensor(n, [P, c], dt)))
                    assert sum(c for _, c, _ in stage) <= cols, (name, stage)
            whole = ctx.enter_context(nc.sbuf_tensor(name, [P, cols], F32))
            return whole, *made

        def sb(name, cols, dt=F32):
            return ctx.enter_context(nc.sbuf_tensor(name, [P, cols], dt))

        def sem(name):
            return ctx.enter_context(nc.semaphore(name))

        w_raw = sb("w_raw", SLOT)
        w_hi = [sb(f"w_hi{i}", SLOT, F32R) for i in range(2)]
        w_lo = [sb(f"w_lo{i}", SLOT, F32R) for i in range(2)]
        ident, ones, mask, param = sb("ident", P), sb("ones", P), sb("mask", 3 * P), sb("param", N_PARAM)
        oas = sb("oas", 4 * SAMPLE)
        nsink = sb("nsink", 17)
        (_, tmp, rs, q_st, sm, pr, pt, o_st, stat, vs_new, ks_new, sstat, sc, scb, hs_re, hs_im, h0, bt,
         og_in, c_acc, c_w, ktc_sb, vc_in, cm_sb) = region(
            "region_e", 5680,
            [("tmp", 2 * T, F32), ("rs", T, F32)],
            [("q_st", 1024, F32), ("sm", 1024, F32), ("pr", 1024, F32), ("pt", 1024, F32),
             ("o_st", 2 * ROW, F32), ("stat", 128, F32)],
            [("vs_new", 3 * 512, F32), ("ks_new", 12 * SAMPLE, F32), ("sstat", 16, F32)],
            [("sc", N_VEC * ST, F32), ("scb", N_VEC * 4, F32), ("hs_re", 256, F32), ("hs_im", 256, F32),
             ("h0", 2 * ST * NB, F32), ("bt", 512, F32)],
            [("og_in", 2 * 3 * ROW, F32), ("c_acc", 1024, F32), ("c_w", 128, F32)],
            [("ktc_sb", 2048, F32), ("vc_in", 2048, F32), ("cm_sb", NB * SKC, F32)])
        (_, hid_hi0, hid_hi1, hid_lo0, hid_lo1, xd, v_sb, u_sb, zb_, kc_sb, vc_sb, qc_st, on_c) = region(
            "region_d", 9 * 512 + 4 * T,
            [("hid_hi0", 2 * T, F32R), ("hid_hi1", 2 * T, F32R), ("hid_lo0", 2 * T, F32R), ("hid_lo1", 2 * T, F32R)],
            [("xd", KC * T, F32)],
            [("v_sb", 9 * 512, F32), ("u_sb", 4 * T, F32)],
            [("zb", 4 * T, F32)],
            [("kc_sb", 2 * T, F32), ("vc_sb", 9 * 256, F32), ("qc_st", 2048, F32), ("on_c", 1024, F32)])
        hid_hi, hid_lo = (hid_hi0, hid_hi1), (hid_lo0, hid_lo1)
        (xa, z_hi, z_lo, va, sp_t, qb, qs, cs_s, cs_t, ocs, cstat) = region(
            "xa", KC * T,
            [("z_hi", 4 * T, F32R), ("z_lo", 4 * T, F32R)],
            [("va", 9 * 512, F32), ("sp_t", 12 * P, F32), ("qb", 960, F32), ("qs", 12 * SAMPLE, F32)],
            [("cs_s", NB * SKC, F32), ("cs_t", 2048, F32), ("ocs", 512, F32), ("cstat", 64, F32)])
        (_, h_hi, h_lo, kt_sb0, kt_sb1, s_sb, sm_sb, b_blk, c_blk, tr, ti, gr, gi, xt1, xt2, sr, si) = region(
            "region_bc", 2 * KC * T,
            [("h_hi", KC * T, F32R), ("h_lo", KC * T, F32R)],
            [("kt_sb0", 4 * sum(ROWS), F32), ("kt_sb1", 4 * sum(ROWS), F32), ("s_sb", SK, F32), ("sm_sb", SK, F32)],
            [("b_blk", 1024, F32), ("c_blk", 1024, F32)]
            + [(n, SEQ, F32) for n in ("tr", "ti", "gr", "gi", "xt1", "xt2", "sr", "si")])
        kt_sb = (kt_sb0, kt_sb1)
        psum = ctx.enter_context(nc.psum_tensor("psum", [P, 8, 512], F32))

        raw_in, hi_made, split, slot_done = sem("raw_in"), sem("hi_made"), sem("split"), sem("slot_done")
        full, free = sem("full"), (sem("free0"), sem("free1"))
        const_in, const_made = sem("const_in"), sem("const_made")
        x_in, x_out, x_made = sem("x_in"), sem("x_out"), sem("x_made")
        sq_made, sq_used, rms_made, inv_made = sem("sq_made"), sem("sq_used"), sem("rms_made"), sem("inv_made")
        scaled, hi_act, lo_made = sem("scaled"), sem("hi_act"), sem("lo_made")
        dve_own, act_own = sem("dve_own"), sem("act_own")
        q_ready, s_mm, s_masked, max_made, exp_made = (sem(n) for n in ("q_ready", "s_mm", "s_masked", "max_made", "exp_made"))
        pt_mm, pt_taken, pv_mm, o_made, o_out = (sem(n) for n in ("pt_mm", "pt_taken", "pv_mm", "o_made", "o_out"))
        turned, zeroed = sem("turned"), sem("zeroed")
        ss_max, vec_arg = sem("ss_max"), sem("vec_arg")
        out_done, kept = sem("out_done"), sem("kept")
        sx_in, kv_in, kv_used, mask_in = sem("sx_in"), (sem("kv_in0"), sem("kv_in1")), sem("kv_used"), sem("mask_in")
        qb_made, ss_mm, ss_masked, ss_exp, ss_norm = (sem(n) for n in ("qb_made", "ss_mm", "ss_masked", "ss_exp", "ss_norm"))
        st_mm, st_taken, spv_mm, spv_taken = (sem(n) for n in ("st_mm", "st_taken", "spv_mm", "spv_taken"))
        ssm_in, blk_in, blk_used, vec_act, vec_dve, bu_mm, bu_used = (
            sem(n) for n in ("ssm_in", "blk_in", "blk_used", "vec_act", "vec_dve", "bu_mm", "bu_used"))
        hs_made, ys_mm, h_made, h_used, y_mm, y_made, z_made, state_out = (
            sem(n) for n in ("hs_made", "ys_mm", "h_made", "h_used", "y_mm", "y_made", "z_made", "state_out"))
        w_dif, w_exp, comb_made = sem("w_dif"), sem("w_exp"), sem("comb_made")
        og_loaded, og_used = (sem("og_loaded0"), sem("og_loaded1")), sem("og_used")

        def tiles(t, n):
            return t[:, :].rearrange("p (n c) -> p n c", n=n)

        XA, XD, TMP = tiles(xa, KC), tiles(xd, KC), tiles(tmp, 2)
        HH, HL = tiles(h_hi, KC), tiles(h_lo, KC)
        HIDH, HIDL = [tiles(t, 2) for t in hid_hi], [tiles(t, 2) for t in hid_lo]
        U, ZB, ZH, ZL = tiles(u_sb, 4), tiles(zb_, 4), tiles(z_hi, 4), tiles(z_lo, 4)
        V, VC, KCT = tiles(v_sb, 9), tiles(vc_sb, 9), tiles(kc_sb, 2)
        G = param[:, 0:80].rearrange("p (l k c) -> p l k c", l=2, k=5)
        QST, QCST = tiles(q_st, 8), tiles(qc_st, 16)
        OST = tiles(o_st, 2)
        UNIT = [psum[:, 3 * s:3 * s + 3, 0:CH] for s in range(2)]

        def chunked(ap):
            return ap.rearrange("p (c n) -> p c n", c=3)


        def prompt_cols(g, i):
            if g == 0:
                return lambda x: x[:, :, bass.ds(SAMPLE + i * P, P)]
            if g == 1:
                return lambda x: x[:, :, bass.ds(SAMPLE + i[1] * 512 + i[0], P, 4)]
            return lambda x: x[:, :, bass.ds(SAMPLE + i, P, 8)]

        def key_cols(g, i, nk):
            if nk == 1:
                return prompt_cols(g, i)
            if g == 0:
                return lambda x: x[:, :, bass.ds(SAMPLE - P + i * P, 2 * P)]
            return lambda x: x[:, :, bass.ds(SAMPLE + i[0], 2 * P, 4)]

        def value_tile(g, i):
            return 2 * i[0] + i[1] if g == 1 else i

        def over_tiles(eng, g, per_tile, tile):
            if g == 0:
                tile(0, 1)
                with turns(eng, 7, per_tile) as i:
                    tile(i + 1, 2)
            elif g == 1:
                with turns(eng, 4, {c: 2 * k for c, k in per_tile.items()}) as i:
                    tile((i, 0), 1)
                    tile((i, 1), 2)
            else:
                with turns(eng, 8, per_tile) as i:
                    tile(i, 1)

        class Units:

            def __init__(self):
                self.full, self.done, self.free = Count(full), Count(slot_done), (Count(free[0]), Count(free[1]))

            def wait(self, eng, last):
                c = self.done if last else self.full
                eng.wait_ge(c.sem, c.add())

            def skip(self, *slots):
                for n in slots:
                    self.full.add(n - 1)
                    self.done.add()
                    self.free[0].add(n // 2)
                    self.free[1].add(n // 2)

            def skip_half(self, m):
                (self.done if m else self.full).add()
                self.free[m].add()

            def per(self, *slots):
                n = sum(slots)
                return {self.full: n - len(slots), self.done: len(slots), self.free[0]: n // 2, self.free[1]: n // 2}

            def all_free(self, eng):
                eng.wait_ge(free[0], self.free[0].at)
                eng.wait_ge(free[1], self.free[1].at)

        block = ctx.enter_context(nc.Block())
        N_A_STEPS, N_C_STEPS = 3 * 8 * 4, 8 * 8

        @block.sync
        def _(sp):
            spl, stored, units = Count(split), Count(out_done), Units()
            made, oout, keeps = Count(o_made), Count(o_out), Count(kept)
            xin, xout, xm = Count(x_in), Count(x_out), Count(x_made)
            fed = [0]

            def feed(slot, first=False):
                if not first:
                    sp.wait_ge(split, spl.add())
                src = a["wall"][bass.ds(slot, 1), :, :].rearrange("a p n -> p (a n)")
                sp.dma_start(w_raw[:, :], src).then_inc(raw_in, 16)

            def feed_to(end):
                n = end - fed[0]
                if not fed[0]:
                    feed(0, first=True)
                    n, fed[0] = n - 1, 1
                if n > 0:
                    with turns(sp, n, {spl: 1}) as i:
                        feed(i + fed[0])
                fed[0] = end

            def store(dst, src):
                sp.dma_start(dst, src).then_inc(out_done, 16)
                stored.add(16)

            c = a["consts"]
            sp.dma_start(ident[:, :], c[:, 0:P]).then_inc(const_in, 16)
            sp.dma_start(ones[:, :], c[:, P:2 * P]).then_inc(const_in, 16)
            sp.dma_start(mask[:, :], c[:, 2 * P:5 * P]).then_inc(const_in, 16)
            sp.dma_start(param[:, :], a["params"]).then_inc(const_in, 16)
            sp.dma_start(XA, a["xT"]).then_inc(x_in, 16)
            xin.add(16)
            feed_to(11)

            units.skip(2, 2)
            for g in range(3):
                units.skip(2, 2, 2, 2, 4, 4)
                units.all_free(sp)
                w = min(ROWS[g], SEQ)
                store(a["okp"][g], XA[:, 4:8, PADS - w:PADS])
                if g == 0:
                    store(a["ovp"][g], V[:, 7, :])
                elif g == 1:
                    for phase in range(4):
                        store(a["ovp"][g].rearrange("(n r) c -> r n c", r=4)[phase], V[:, 2 * phase + 1, :])
                else:
                    for t in range(8):
                        store(a["ovp"][g].rearrange("(n r) c -> r n c", r=8)[t], V[:, t, :])
                store(a["oks_new"][g], XA[:, 4:8, 0:SAMPLE])
                store(a["ovs_new"][g], V[0:SAMPLE, 8, :])
                sp.dma_start(qk_keep[:, g, :, :], XA[:, :, 0:SAMPLE]).then_inc(kept, 16)
                sp.dma_start(v_keep[:, g, :], V[0:SAMPLE, 8, :]).then_inc(kept, 16)
                keeps.add(32)

                def tile(i, nk, g=g):
                    sp.wait_ge(o_made, made.add())
                    row = og[g]
                    if g == 0:
                        sp.dma_start(row[bass.ds(i * P, P), :], o_st[:, 0:ROW]).then_inc(o_out, 16)
                        oout.add(16)
                    elif g == 1:
                        dst = row.rearrange("(h n r) c -> h r n c", h=2, r=4)[i[1], bass.ds(i[0], 1), :, :]
                        sp.dma_start(dst.rearrange("r n c -> (r n) c"), o_st[:, 0:ROW]).then_inc(o_out, 16)
                        oout.add(16)
                    else:
                        dst = row.rearrange("(n r) c -> r n c", r=8)[bass.ds(i, 1), :, :]
                        sp.dma_start(dst.rearrange("r n c -> (r n) c"), o_st[:, 0:ROW]).then_inc(o_out, 16)
                        oout.add(16)

                over_tiles(sp, g, {made: 1, oout: 16}, tile)
                sp.wait_ge(out_done, stored.at)
                feed_to((17, 23, 23)[g])

            sp.wait_ge(kept, keeps.at)
            sp.wait_ge(o_out, oout.at)
            sp.wait_ge(pv_mm, N_A_STEPS)
            sp.dma_start(tiles(qs, 3).rearrange("p g (j t) -> p g j t", j=4), qk_keep[:, :, 0:4, :]).then_inc(sx_in, 16)
            sp.dma_start(tiles(ks_new, 3).rearrange("p g (j t) -> p g j t", j=4),
                         qk_keep[:, :, 4:8, :]).then_inc(sx_in, 16)
            sp.dma_start(vs_new[0:SAMPLE, :], v_keep.rearrange("t g c -> t (g c)")).then_inc(sx_in, 16)
            used = Count(kv_used)

            def load_batch(n, b):
                o = 0
                for g in range(3):
                    c = 4 * ROWS[g]
                    sp.dma_start(kt_sb[b][:, o:o + c], a["kt"][g][bass.ds(n, 1), :, :].rearrange("n p c -> p (n c)"))\
                        .then_inc(kv_in[b], 16)
                    o += c
                vb = (va, v_sb)[b]
                sp.dma_start(vb[:, 0:512], a["v"][0][bass.ds(n, 1), :, :].rearrange("n p c -> p (n c)")).then_inc(kv_in[b], 16)
                for c in range(4):
                    sp.dma_start(vb[:, 512 * (1 + c):512 * (2 + c)],
                                 a["v"][1][bass.ds(n, 1), P * c:P * c + P, :].rearrange("n p c -> p (n c)"))\
                        .then_inc(kv_in[b], 16)
                    src = a["v"][2][bass.ds(n, 1), 256 * c:256 * c + 256, :].rearrange("n (i s) c -> (n i) s c", s=16)
                    sp.dma_start(vb[:, 512 * (5 + c):512 * (6 + c)], src[:, 0:8, :]).then_inc(kv_in[b], 16)

            def load_mask(z):
                sp.dma_start(sm_sb[:, :], a["smask"][bass.ds(z, 1), :, :].rearrange("z p c -> p (z c)")).then_inc(mask_in, 16)

            masked = Count(ss_masked)
            load_batch(0, 0)
            load_mask(0)
            load_batch(1, 1)
            with turns(sp, 3, {used: 2, masked: 1}) as z:
                sp.wait_ge(kv_used, used.add())
                load_batch(z * 2 + 2, 0)
                sp.wait_ge(ss_masked, masked.add())
                load_mask(z + 1)
                sp.wait_ge(kv_used, used.add())
                load_batch(z * 2 + 3, 1)

            sp.wait_ge(kv_used, 8)
            sp.wait_ge(ss_norm, 4)
            sp.wait_ge(spv_taken, 4)
            sp.dma_start(sc[:, 0:3 * ST], a["ssm"]).then_inc(ssm_in, 16)
            sp.dma_start(h0[:, :], a["h0"]).then_inc(ssm_in, 16)
            sp.dma_start(b_blk[:, :], a["bmat"][0]).then_inc(blk_in, 16)
            sp.dma_start(c_blk[:, :], a["cmat"][0]).then_inc(blk_in, 16)
            ymm = Count(y_mm)
            with turns(sp, 3, {ymm: 1}) as b:
                sp.wait_ge(y_mm, ymm.add())
                sp.dma_start(b_blk[:, :], a["bmat"][bass.ds(b + 1, 1)].rearrange("b p c -> p (b c)")).then_inc(blk_in, 16)
                sp.dma_start(c_blk[:, :], a["cmat"][bass.ds(b + 1, 1)].rearrange("b p c -> p (b c)")).then_inc(blk_in, 16)
            sp.wait_ge(state_out, 1)
            store(a["st_s"], h0[:, :])
            store(a["st_p"], sc[:, V_T1 * ST:(V_T2 + 1) * ST])

            sp.wait_ge(out_done, stored.at)
            sp.wait_ge(lo_made, LO_GLU)
            ogu = Count(og_used)
            for t in range(2):
                sp.dma_start(tiles(og_in, 2)[:, t, :].rearrange("p (g c) -> p g c", g=3),
                             og[:, P * t:P * t + P, :].rearrange("g p c -> p g c")).then_inc(og_loaded[t], 16)
            with turns(sp, 3, {ogu: 2}) as t:
                for b in range(2):
                    sp.wait_ge(og_used, ogu.add())
                    sp.dma_start(tiles(og_in, 2)[:, b, :].rearrange("p (g c) -> p g c", g=3),
                                 og[:, bass.ds(t * 256 + 256 + P * b, P), :].rearrange("g p c -> p g c"))\
                        .then_inc(og_loaded[b], 16)

            for layer in range(2):
                if layer == 0:
                    sp.wait_ge(lo_made, LO_MIXED_A)
                    sp.dma_start(XD, a["xT"]).then_inc(x_in, 16)
                else:
                    sp.wait_ge(lo_made, LO_MIXED_C)
                    sp.wait_ge(x_out, xout.at)
                    sp.dma_start(XD, x_keep).then_inc(x_in, 16)
                xin.add(16)
                feed_to(W_OUT[layer] + 7)
                sp.wait_ge(x_made, xm.add(8))
                sp.dma_start(x_keep, XA).then_inc(x_out, 16)
                xout.add(16)

                def copy_batch(n, layer=layer):
                    s = bass.ds(n, 1)
                    for g in ((2,) if layer == 0 else (0, 1)):
                        r = ROWS[g]
                        store(a["oks"][g][s, :, :, 0:r - NS], a["kt"][g].rearrange("n p (j r) -> n p j r", j=4)[s, :, :, NS:r])
                        store(a["ovs"][g][s, 0:r - NS, :], a["v"][g][s, NS:r, :])
                    if layer == 1:
                        store(a["okc_s"][s, :, :, 0:ROWS_C - NS],
                              a["ktc"].rearrange("n p (j r) -> n p j r", j=2)[s, :, :, NS:ROWS_C])
                        store(a["ovc_s"][s, 0:ROWS_C - NS, :], a["vc"][s, NS:ROWS_C, :])

                n_copies = 16 * (2 if layer == 0 else 6)
                base = fed[0]
                with turns(sp, 7, {spl: 4, stored: n_copies}) as i:
                    for k in range(4):
                        feed(i * 4 + base + k)
                    copy_batch(i)
                fed[0] += 28
                copy_batch(7)
                feed_to(W_PLE[layer] + 3)
                sp.wait_ge(slot_done, W_PLE[layer])
                sp.wait_ge(x_out, xout.at)
                sp.dma_start(XD, x_keep).then_inc(x_in, 16)
                xin.add(16)
                xm.add(8)
                if layer == 0:
                    feed_to(W_GATE[0] + 7)
                    sp.wait_ge(x_made, xm.add(8))
                    sp.dma_start(x_keep, XA).then_inc(x_out, 16)
                    xout.add(16)
                    feed_to(W_VC + 4)
                    sp.wait_ge(slot_done, W_VC + 1)
                    sp.wait_ge(free[0], UNITS_AT[W_VC + 1] // 2)
                    sp.wait_ge(free[1], UNITS_AT[W_VC + 1] // 2)
                    store(a["okc_p"], KCT[:, :, PADS - ROWS_C:PADS])
                    store(a["ovc_p"], VC[:, 7, :])
                    store(a["okc_new"], KCT[:, :, 0:SAMPLE])
                    store(a["ovc_new"], VC[0:SAMPLE, 8, :])
                    sp.wait_ge(o_made, made.add(8))
                    sp.dma_start(ktc_sb[:, :].rearrange("p (n c) -> p n c", n=NB), a["ktc"].rearrange("n p c -> p n c")).then_inc(sx_in, 16)
                    sp.dma_start(vc_in[:, :].rearrange("p (n c) -> p n c", n=NB), a["vc"].rearrange("n p c -> p n c")).then_inc(sx_in, 16)
                    sp.dma_start(cm_sb[:, :], a["cmask"]).then_inc(sx_in, 16)
                    sp.wait_ge(out_done, stored.at)
                else:
                    feed_to(N_SLOTS)
                    sp.wait_ge(x_made, xm.add(8))
                    store(a["yT"], XA)
            sp.wait_ge(out_done, stored.at)
            sp.wait_ge(x_out, xout.at)
            sp.wait_ge(o_out, oout.at)
            sp.wait_ge(kept, keeps.at)

        @block.gpsimd
        def _(pool):
            raw, hi, done = Count(raw_in), Count(hi_made), Count(slot_done)

            def split_slot(b, wait_free=True):
                pool.wait_ge(raw_in, raw.add(16))
                if wait_free:
                    pool.wait_ge(slot_done, done.add())
                pool.tensor_tensor(w_hi[b][:, :], w_raw[:, :], ones[:, 0:1].broadcast_to([P, SLOT]), ALU.mult).then_inc(hi_made, 1)
                pool.wait_ge(hi_made, hi.add())
                pool.tensor_tensor(w_lo[b][:, :], w_raw[:, :], w_hi[b][:, :].bitcast(F32), ALU.subtract).then_inc(split, 1)

            pool.wait_ge(const_in, 64)
            split_slot(0, wait_free=False)
            split_slot(1, wait_free=False)
            with turns(pool, (N_SLOTS - 3) // 2, {raw: 32, hi: 2, done: 2}):
                split_slot(0)
                split_slot(1)
            split_slot(0)

        @block.tensor
        def _(pe):
            u, spl = Units(), Count(split)
            sqm, rms, lo = Count(sq_made), Count(rms_made), Count(lo_made)
            n_q, n_s, n_mask, n_exp, n_ptt, n_pt, n_pv, n_o = (
                Count(s) for s in (q_ready, s_mm, s_masked, exp_made, pt_taken, pt_mm, pv_mm, o_made))

            def sums():
                pe.wait_ge(free[0], u.free[0].at)
                for kc in range(KC):
                    pe.wait_ge(sq_made, sqm.add())
                    for c in range(3):
                        mm = pe.matmul(UNIT[0][:, c, :], ones[:, :], TMP[:, kc % 2, c * CH:(c + 1) * CH],
                                       start=kc == 0, stop=kc == KC - 1)
                    mm.then_inc(sq_used, 1)
                pe.wait_ge(rms_made, rms.add())

            def halves(slot, kcs):
                return [t[slot % 2][:, 0:2048].rearrange("p (k c) -> p k c", k=kcs) for t in (w_hi, w_lo)]

            def slot_ready():
                pe.wait_ge(split, spl.add())

            def features(slot, XH, XL, kcs=KC, n_units=2, done=1):
                WH, WL = halves(slot, kcs)
                for m in range(n_units):
                    cols = slice(m * P, m * P + P)
                    s = m % 2
                    if not (isinstance(u.free[s].at, int) and u.free[s].at == 0):
                        pe.wait_ge(free[s], u.free[s].at)
                    u.free[s].add()
                    for kc in range(kcs):
                        for w, x in ((WH, XH), (WL, XH), (WH, XL)):
                            first, last = kc == 0 and w is WH and x is XH, kc == kcs - 1 and x is XL
                            for c in range(3):
                                mm = pe.matmul(UNIT[s][:, c, :], w[:, kc, cols], x[:, kc, c * CH:(c + 1) * CH],
                                               start=first, stop=last)
                    if m == n_units - 1:
                        mm.then_inc(slot_done, done)
                        u.done.add(done)
                    else:
                        mm.then_inc(full, 1)
                        u.full.add()

            def values(slot, g):
                WH, WL = halves(slot, KC)
                for n, tt in enumerate(((0, 1, 2), (3, 4, 5), (6, 7), (8,))):
                    s = n % 2
                    pe.wait_ge(free[s], u.free[s].at)
                    u.free[s].add()
                    for c, t in enumerate(tt):
                        pick = (lambda x: x[:, :, 0:P]) if t == 8 else prompt_cols(g, divmod(t, 2) if g == 1 else t)
                        XH, XL = pick(HH), pick(HL)
                        for kc in range(KC):
                            for x, w in ((XH, WH), (XH, WL), (XL, WH)):
                                mm = pe.matmul(psum[:, 3 * s + c, 0:256], x[:, kc], w[:, kc, :],
                                               start=kc == 0 and x is XH and w is WH, stop=kc == KC - 1 and x is XL)
                    if n == 3:
                        mm.then_inc(slot_done, 1)
                        u.done.add()
                    else:
                        mm.then_inc(full, 1)
                        u.full.add()

            def slot_pairs(n, first, XH, XL):
                with turns(pe, n, {spl: 2, **u.per(2, 2)}):
                    for k in range(2):
                        slot_ready()
                        features(first + k, XH, XL)

            def attend(g, heads, keys, vals):
                steps, per_kv = heads // 2, 1 if heads == H_A else 4
                staged = QST if heads == H_A else QCST

                def tile(i, nk):
                    K = key_cols(g, i, nk)(keys)
                    pe.wait_ge(q_ready, n_q.add())
                    base = n_mask.at

                    def scores(k):
                        m = n_mask.add()
                        if not (isinstance(m, int) and m <= 2):
                            pe.wait_ge(s_masked, m - 2)
                        for hh in range(2):
                            h = 2 * k + hh
                            kt = h // 2 if per_kv == 1 else h // 8
                            mm = pe.matmul(psum[:, k % 2, hh * 256:hh * 256 + nk * P], staged[:, h, :], K[:, kt],
                                           start=True, stop=True)
                        mm.then_inc(s_mm, 1)

                    def turn(k):
                        pe.wait_ge(exp_made, n_exp.add())
                        m = n_ptt.add()
                        if not (isinstance(m, int) and m <= 2):
                            pe.wait_ge(pt_taken, m - 2)
                        for hh in range(2):
                            for kb in range(nk):
                                o = (k % 2) * 512 + hh * 256 + kb * P
                                mm = pe.transpose(psum[:, 2 + k % 2, hh * 256 + kb * P:hh * 256 + kb * P + P],
                                                  pr[:, o:o + P], ident[:, :])
                        mm.then_inc(pt_mm, 1)

                    def weigh(k):
                        if k == 0:
                            m = n_o.add()
                            if not (isinstance(m, int) and m <= 1):
                                pe.wait_ge(o_made, m - 1)
                        pe.wait_ge(pt_taken, n_pv.add())
                        for hh in range(2):
                            h = 2 * k + hh
                            c = (h // per_kv) * HEAD_DIM
                            for kb in range(nk):
                                t = value_tile(g, i) - (nk - 1 - kb)
                                o = (k % 2) * 512 + hh * 256 + kb * P
                                mm = pe.matmul(psum[:, 4 + h // 8, (h % 8) * HEAD_DIM:(h % 8 + 1) * HEAD_DIM],
                                               pt[:, o:o + P], vals[:, bass.ds(t, 1), c:c + HEAD_DIM],
                                               start=kb == 0, stop=kb == nk - 1)
                        mm.then_inc(pv_mm, 1)

                    for k in range(steps + 2):
                        if k < steps:
                            scores(k)
                        if 1 <= k <= steps:
                            turn(k - 1)
                        if k >= 2:
                            weigh(k - 2)
                    if heads == H_C:
                        pe.wait_ge(o_made, n_o.at)
                        m = lo.at
                        pe.wait_ge(lo_made, m)
                        for k in range(KC):
                            mm = pe.transpose(psum[:, 6 + k // 4, (k % 4) * P:(k % 4 + 1) * P],
                                              on_c[:, k * P:(k + 1) * P], ident[:, :])
                        mm.then_inc(turned, 1)
                        lo.add()

                per = {n_q: 1, n_mask: steps, n_exp: steps, n_ptt: steps, n_pv: steps, n_o: 1}
                if heads == H_C:
                    per[lo] = 1
                over_tiles(pe, g, per, tile)
                pe.wait_ge(o_made, n_o.at)

            pe.wait_ge(const_in, 64)
            sums()
            pe.wait_ge(lo_made, lo.add(8))
            for k in range(2):
                slot_ready()
                features(W_U + k, HH, HL)
            for g in range(3):
                slot_pairs(2, W_QKV + 6 * g, HH, HL)
                for k in range(2):
                    slot_ready()
                    values(W_QKV + 6 * g + 4 + k, g)
                u.all_free(pe)
                attend(g, H_A, XA[:, 4:8, :], V)

            pe.wait_ge(sx_in, 48)
            pe.wait_ge(o_made, n_o.at)
            KSN, VSN = tiles(ks_new, 12), tiles(vs_new, 3)
            QB, PT = qb[:, :].rearrange("p (g c) -> p g c", g=3), tiles(sp_t, 12)
            qbm, kvi, ssm_, sse, stt_, spt_ = Count(qb_made), [Count(s) for s in kv_in], Count(ss_masked), Count(ss_norm), Count(st_taken), Count(spv_taken)
            with turns(pe, 4, {qbm: 2, kvi[0]: 16 * 12, kvi[1]: 16 * 12, ssm_: 1, sse: 1, stt_: 1, spt_: 1}):
                for b in range(2):
                    KT_ = kt_sb[b]
                    pe.wait_ge(qb_made, qbm.add())
                    pe.wait_ge(kv_in[b], kvi[b].add(16 * 12))
                    if b == 0:
                        pe.wait_ge(ss_masked, ssm_.add() - 1)
                    rows = slice(64 * b, 64 * b + 64)

                    def score(out, g, keys):
                        for j in range(4):
                            mm = pe.matmul(out, QB[:, g, j * 64:j * 64 + 64], keys[j], start=j == 0, stop=j == 3)
                        return mm

                    off = 0
                    for g in range(3):
                        kk = KT_[:, off:off + 4 * ROWS[g]].rearrange("p (j r) -> p j r", j=4)
                        off += 4 * ROWS[g]
                        if g == 2:
                            cached = [kk[:, j].rearrange("p (i s) -> p i s", s=16)[:, :, 0:8] for j in range(4)]
                        else:
                            cached = [kk[:, j, :] for j in range(4)]
                        score(psum[rows, g, 0:(P, 512, 512)[g]], g, cached)
                        mm = score(psum[rows, 0, P + 64 * g:P + 64 * g + 64], g, [KSN[:, 4 * g + j, :] for j in range(4)])
                    mm.then_inc(ss_mm, 1)
                pe.wait_ge(ss_norm, sse.add())
                pe.wait_ge(st_taken, stt_.add() - 1)
                for n in range(9):
                    o = 0 if n == 0 else 320 + (n - 1) * P
                    out = psum[:, 4 + n // 4, (n % 4) * P:(n % 4 + 1) * P] if n < 8 else psum[:, 3, 384:512]
                    pe.transpose(out, s_sb[:, o:o + P], ident[:, :])
                for g in range(3):
                    mm = pe.transpose(psum[0:64, 3, g * P:g * P + P], s_sb[:, P + 64 * g:P + 64 * g + 64], ident[:, :])
                mm.then_inc(st_mm, 1)
                pe.wait_ge(st_taken, stt_.at)
                pe.wait_ge(spv_taken, spt_.add() - 1)
                for b in range(2):
                    vb = tiles((va, v_sb)[b], 9)
                    for j in range(4):
                        out = psum[:, 6, b * 64 + j * 16:b * 64 + j * 16 + 16]
                        cols = slice(b * 64 + j * 16, b * 64 + j * 16 + 16)
                        for g in range(3):
                            pe.matmul(out, VSN[0:64, g, j * P:(j + 1) * P], PT[0:64, g, cols], start=g == 0, stop=False)
                        for n in range(9):
                            mm = pe.matmul(out, vb[:, n, j * P:(j + 1) * P], PT[:, 3 + n, cols], start=False, stop=n == 8)
                    mm.then_inc(kv_used, 1)

            pe.wait_ge(spv_taken, 4)
            bi, hsm, vd, ym, hm, bus = Count(blk_in), Count(hs_made), Count(vec_dve), Count(y_made), Count(h_made), Count(bu_used)
            BB = b_blk[:, :].rearrange("p (t c s) -> p t c s", t=4, c=2)
            CB = c_blk[:, :].rearrange("p (t c s) -> p t c s", t=4, c=2)
            HSR, HSI = tiles(hs_re, 4), tiles(hs_im, 4)
            with turns(pe, 4, {bi: 32, hsm: 1, vd: 1, ym: 1, hm: 4, bus: 5}) as b:
                ub = U[:, bass.ds(b, 1), :]
                pe.wait_ge(blk_in, bi.add(32))
                pe.wait_ge(bu_used, bus.add() - 1)
                for c in range(2):
                    for t in range(4):
                        mm = pe.matmul(psum[:, 7, c * 256 + t * 64:c * 256 + t * 64 + 64], BB[:, t, c, :],
                                       ub[:, :, 0:SAMPLE], start=True, stop=True)
                mm.then_inc(bu_mm, 1)
                pe.wait_ge(hs_made, hsm.add())
                pe.wait_ge(y_made, ym.add() - 1)
                for t in range(4):
                    for c, H in ((0, HSR), (1, HSI)):
                        mm = pe.matmul(psum[:, 6, 0:SAMPLE], CB[:, t, c, :], H[:, t, :],
                                       start=t == 0 and c == 0, stop=t == 3 and c == 1)
                mm.then_inc(ys_mm, 1)
                pe.wait_ge(vec_dve, vd.add())
                for t in range(4):
                    pe.wait_ge(bu_used, bus.add() - 1)
                    for c in range(2):
                        for n in range(2):
                            mm = pe.matmul(psum[:, 2 * c + n, :], BB[:, t, c, :],
                                           ub[:, :, SAMPLE + n * 512:SAMPLE + n * 512 + 512], start=True, stop=True)
                    mm.then_inc(bu_mm, 1)
                    pe.wait_ge(h_made, hm.add())
                    for n in range(2):
                        for c, H in ((0, sr), (1, si)):
                            mm = pe.matmul(psum[:, 4 + n, :], CB[:, t, c, :], H[:, n * 512:n * 512 + 512],
                                           start=t == 0 and c == 0, stop=t == 3 and c == 1, skip_group_check=True)
                    mm.then_inc(*((y_mm, 1) if t == 3 else (h_used, 1)))

            pe.wait_ge(lo_made, lo.add(4))
            slot_ready()
            features(W_GLU, ZH, ZL, kcs=4, n_units=4)
            lo.add(4)

            cmb = Count(comb_made)
            lo.add()
            with turns(pe, 4, {cmb: 2, lo: 2}):
                for b in range(2):
                    pe.wait_ge(comb_made, cmb.add())
                    m = lo.add()
                    pe.wait_ge(lo_made, m - 2)
                    for k in range(4):
                        mm = pe.transpose(psum[:, 6 + b, k * P:k * P + P], c_acc[:, b * 512 + k * P:b * 512 + k * P + P],
                                          ident[:, :])
                    mm.then_inc(turned, 1)

            for layer in range(2):
                if layer == 1:
                    slot_pairs(2, W_QC, HH, HL)
                    slot_ready()
                    features(W_KC, HH, HL)
                    slot_ready()
                    values(W_VC, 0)
                    u.all_free(pe)
                    attend(0, H_C, KCT, VC)
                    pe.wait_ge(sx_in, 48 + 48)
                    pe.wait_ge(qb_made, 9)
                    QS = qc_st[:, :].rearrange("p (n j c) -> p n j c", n=NB, j=2)
                    KS, VS = ktc_sb[:, :].rearrange("p (n j r) -> p n j r", n=NB, j=2), tiles(vc_in, NB)
                    for n in range(NB):
                        o = (n % 2) * SKC
                        for out, keys in ((psum[:, n // 2, o:o + P], [KS[:, n, j] for j in range(2)]),
                                          (psum[:, n // 2, o + P:o + SKC], [KCT[:, j, 0:SAMPLE] for j in range(2)])):
                            for j in range(2):
                                mm = pe.matmul(out, QS[:, n, j, :], keys[j], start=j == 0, stop=j == 1)
                    mm.then_inc(ss_mm, 1)
                    pe.wait_ge(ss_norm, 5)
                    pe.wait_ge(lo_made, lo.at)
                    S, PTC = tiles(cs_s, NB), tiles(cs_t, 16)
                    for n in range(NB):
                        pe.transpose(psum[:, 4 + n // 4, (n % 4) * P:(n % 4 + 1) * P], S[:, n, 0:P], ident[:, :])
                        mm = pe.transpose(psum[0:64, 6 + n // 4, (n % 4) * P:(n % 4 + 1) * P], S[:, n, P:SKC], ident[:, :])
                    mm.then_inc(st_mm, 1)
                    pe.wait_ge(st_taken, 5)
                    for n in range(NB):
                        for j in range(2):
                            out = psum[:, n // 4, (n % 4) * P + j * 64:(n % 4) * P + j * 64 + 64]
                            pe.matmul(out, VS[:, n, j * P:j * P + P], PTC[:, n, j * 64:j * 64 + 64], start=True, stop=False)
                            mm = pe.matmul(out, VC[0:SAMPLE, 8, j * P:j * P + P], PTC[0:64, 8 + n, j * 64:j * 64 + 64],
                                           start=False, stop=True)
                    mm.then_inc(spv_mm, 1)
                    lo.add()
                pe.wait_ge(lo_made, lo.at)
                slot_pairs(2, W_OUT[layer], HH, HL)
                sums()
                sums()
                pe.wait_ge(lo_made, lo.add(8))
                up = W_FF[layer]

                def ff_up(slot):
                    slot_ready()
                    features(slot, HH, HL)
                    lo.add(2)

                def ff_down(slot, h):
                    slot_ready()
                    pe.wait_ge(lo_made, lo.at - (0 if slot == up + 31 else 2))
                    features(slot, HIDH[h], HIDL[h], kcs=2, n_units=8)

                ff_up(up)
                with turns(pe, 7, {spl: 4, lo: 4, **u.per(2, 8, 2, 8)}):
                    ff_up(up + 1)
                    ff_down(up + 2, 0)
                    ff_up(up + 3)
                    ff_down(up + 4, 1)
                ff_up(up + 29)
                ff_down(up + 30, 0)
                ff_down(up + 31, 1)
                sums()
                slot_ready()
                slot_ready()
                s = W_PLE[layer] % 2
                PH, PL = (t[s][:, :].rearrange("p (k c) -> p k c", k=2) for t in (w_hi, w_lo))
                features(W_PLE[layer] + 1, PH, PL, kcs=2, n_units=8, done=2)
                sums()
                pe.wait_ge(lo_made, lo.add(8))
                slot_pairs(2, W_GATE[layer], HH, HL)
                if layer == 0:
                    sums()
                    pe.wait_ge(lo_made, lo.add(8))

        OUT_G = (64, 64 + 112, 64 + 112 + 176)
        OUT_S5 = OUT_G[2] + 32


        @block.scalar
        def _(act):
            u, squ, lo, scl = Units(), Count(sq_used), Count(lo_made), Count(scaled)
            xm, own = Count(x_made), Count(act_own)
            n_s, n_max, n_ptx, n_pt, n_pv, n_o, n_sc = (Count(s) for s in (s_mm, max_made, pt_mm, pt_mm, pv_mm, o_made, w_dif))
            n_turn, n_out = Count(turned), Count(o_out)

            def late(sem_, value):
                if not (isinstance(value, int) and value <= 0):
                    act.wait_ge(sem_, value)

            def squares(ready):
                for kc in range(KC):
                    ready(kc)
                    late(sq_used, squ.add() - 2)
                    act.activation(TMP[:, kc % 2, :], XA[:, kc, :], ACT.Square).then_inc(sq_made, 1)
                act.wait_ge(sq_used, squ.at)
                act.activation(chunked(rs[:, :]), UNIT[0], ACT.Sqrt, bias=param[:, C_EPS:C_EPS + 1],
                               scale=1.0 / D_MODEL).then_inc(rms_made, 1)

            def high(dst, src, ready, n):
                act.wait_ge(ready, n)
                act.activation(dst, src, ACT.Copy).then_inc(hi_act, 1)

            def norm_highs():
                for kc in range(KC):
                    high(HH[:, kc, :], TMP[:, kc % 2, :], scaled, scl.add())
                lo.add(8)

            def take(dst, m, last, func=ACT.Copy, **kw):
                u.wait(act, last)
                act.activation(chunked(dst), UNIT[m % 2], func, **kw).then_inc(free[m % 2], 1)
                u.free[m % 2].add()

            def take_pairs(n, buf, first=0):
                with turns(act, n, u.per(2, 2)) as i:
                    for k in range(4):
                        take(buf[:, bass.ds(i * 4 + k + first, 1), :].rearrange("p a t -> p (a t)"), k, k % 2 == 1)

            def take_values(buf, cols):
                for n, (t, k) in enumerate(((0, 3), (3, 3), (6, 2), (8, 1))):
                    rows = slice(0, SAMPLE) if n == 3 else slice(0, P)
                    u.wait(act, n == 3)
                    s = n % 2
                    act.activation(buf[rows, t:t + k, cols], psum[rows, 3 * s:3 * s + k, 0:256], ACT.Copy).then_inc(free[s], 1)
                    u.free[s].add()

            def attend(g, heads):
                steps = heads // 2
                src = XA if heads == H_C else XA[:, 0:4, :]

                def tile(i, nk):
                    late(s_mm, n_s.at)
                    n_s.add(steps)
                    for par in range(2):
                        rows = slice(64 * par, 64 * par + 64)
                        if heads == H_A:
                            q = prompt_cols(g, i)(src)[rows]
                            out = QST.rearrange("p (j h) c -> p h j c", h=2)[rows, par]
                            mm = act.activation(out, q, ACT.Copy, scale=HEAD_DIM ** -0.5)
                        else:
                            for o in range(2):
                                q = prompt_cols(g, i)(src)[rows].rearrange("p (k o y) c -> p k o y c", k=2, o=2)[:, :, o]
                                out = QCST.rearrange("p (k o y h) c -> p k o y h c", k=2, o=2, y=2)[64 * o:64 * o + 64, :, o, :, par]
                                mm = act.activation(out, q, ACT.Copy, scale=HEAD_DIM ** -0.5)
                    mm.then_inc(q_ready, 1)
                    late(o_made, n_o.at)
                    n_o.add()

                    def exps(k):
                        act.wait_ge(max_made, n_max.add())
                        late(pt_mm, n_ptx.add() - 2)
                        for hh in range(2):
                            h = 2 * k + hh
                            o = (k % 2) * 512 + hh * 256
                            mm = act.activation(pr[:, o:o + nk * P], sm[:, o:o + nk * P], ACT.Exp, bias=stat[:, h:h + 1],
                                                accum_out=stat[:, 16 + h:17 + h])
                        mm.then_inc(exp_made, 1)

                    def turned_out(k):
                        act.wait_ge(pt_mm, n_pt.add())
                        late(pv_mm, n_pv.add() - 2)
                        o = (k % 2) * 512
                        act.activation(pt[:, o:o + 512].rearrange("p (h c) -> p h c", h=2)[:, :, 0:nk * P],
                                       psum[:, 2 + k % 2, :].rearrange("p (h c) -> p h c", h=2)[:, :, 0:nk * P],
                                       ACT.Copy).then_inc(pt_taken, 1)

                    exps(0)
                    for k in range(steps):
                        if k + 1 < steps:
                            exps(k + 1)
                        turned_out(k)
                    if heads == H_C:
                        act.wait_ge(w_dif, n_sc.add())
                        act.activation(stat[:, 48:64], stat[:, 32:48], ACT.Exp).then_inc(w_exp, 1)
                        high(HH[:, :, bass.ds(i * P + SAMPLE, P)],
                             psum[:, 6:8, :].rearrange("p b (k c) -> p (b k) c", c=P), turned, n_turn.add())

                per = {n_s: steps, n_o: 1, n_max: steps, n_ptx: steps, n_pt: steps, n_pv: steps}
                if heads == H_C:
                    per |= {n_sc: 1, n_turn: 1}
                over_tiles(act, g, per, tile)

            act.wait_ge(const_in, 64)
            squares(lambda kc: act.wait_ge(x_in, 16))
            norm_highs()
            for m in range(4):
                take(U[:, m, :], m, m % 2 == 1)
            act.wait_ge(lo_made, lo.at)
            act.wait_ge(zeroed, 1)
            for g in range(3):
                if g:
                    act.wait_ge(out_done, OUT_G[g - 1])
                    act.wait_ge(kept, 32 * g)
                take_pairs(2, XA)
                for k in range(2):
                    take_values(V, slice(256 * k, 256 * k + 256))
                u.all_free(act)
                attend(g, H_A)

            smx, stm, kvu = Count(ss_max), Count(st_mm), Count(kv_used)
            PT = tiles(sp_t, 12)
            with turns(act, 4, {smx: 1, stm: 1, kvu: 2}):
                act.wait_ge(ss_max, smx.add())
                act.activation(s_sb[:, :], s_sb[:, :], ACT.Exp, bias=sstat[:, 0:1], accum_out=sstat[:, 1:2]).then_inc(ss_exp, 1)
                act.wait_ge(st_mm, stm.add())
                act.wait_ge(kv_used, kvu.at)
                kvu.add(2)
                act.activation(PT[0:64, 0:3, :], psum[0:64, 3, 0:384].rearrange("p (g c) -> p g c", g=3), ACT.Copy)
                act.activation(PT[:, 3:11, :], psum[:, 4:6, :].rearrange("p b (n c) -> p (b n) c", c=P), ACT.Copy)
                act.activation(PT[:, 11, :], psum[:, 3, 384:512], ACT.Copy).then_inc(st_taken, 1)

            def vec(v):
                return sc[:, v * ST:(v + 1) * ST]

            act.wait_ge(ssm_in, 32)
            act.activation(vec(V_DT), vec(V_DT), ACT.Exp).then_inc(vec_act, 1)
            act.wait_ge(vec_arg, 1)
            act.activation(vec(V_R), vec(V_X), ACT.Exp)
            act.activation(vec(V_SIN), vec(V_K), ACT.Sin)
            act.activation(vec(V_COS), vec(V_COS), ACT.Sin).then_inc(vec_act, 1)
            act.wait_ge(y_made, 4)
            act.wait_ge(zeroed, 2)
            for m in range(4):
                act.activation(ZB[:, m, :], ZB[:, m, :], ACT.Gelu_apprx_tanh).then_inc(act_own, 1)
                high(ZH[:, m, :], ZB[:, m, :], act_own, own.add())
            lo.add(4)
            act.wait_ge(out_done, OUT_S5)
            for m in range(4):
                act.wait_ge(lo_made, lo.at - (1 if m < 2 else 0) + (m - 2 if m >= 2 else 0))
                if m >= 2:
                    act.wait_ge(lo_made, lo.at + m - 1)
                take(TMP[:, m % 2, :], m, m == 3, ACT.Sigmoid, bias=param[:, C_GLU + m:C_GLU + m + 1])
                if m:
                    high(HH[:, 3 + m, :], TMP[:, (m - 1) % 2, :], scaled, scl.add())
            high(HH[:, 7, :], TMP[:, 1, :], scaled, scl.add())
            lo.add(4)

            high(HH[:, 0:4, 0:SAMPLE], tiles(oas, 4), spv_taken, 4)
            lo.add()
            with turns(act, 4, {n_sc: 2, n_turn: 2}) as t:
                for b in range(2):
                    act.wait_ge(w_dif, n_sc.add())
                    act.activation(c_w[:, b * 64 + 32:b * 64 + 56], c_w[:, b * 64 + 8:b * 64 + 32], ACT.Exp).then_inc(w_exp, 1)
                    high(HH[:, 0:4, bass.ds(t * 256 + SAMPLE + P * b, P)],
                         psum[:, 6 + b, :].rearrange("p (k c) -> p k c", c=P), turned, n_turn.add())
            lo.add(8)

            for layer in range(2):
                if layer == 1:
                    act.wait_ge(x_out, 32)
                    take_pairs(2, XA)
                    for m in range(2):
                        take(KCT[:, m, :], m, m == 1)
                    take_values(VC, slice(0, 256))
                    u.all_free(act)
                    act.wait_ge(zeroed, 3)
                    attend(0, H_C)
                    lo.add(8)
                    for n in range(NB):
                        act.wait_ge(ss_max, 5)
                        mm = act.activation(tiles(cs_s, NB)[:, n, :], tiles(cs_s, NB)[:, n, :], ACT.Exp,
                                            bias=cstat[:, n:n + 1], accum_out=cstat[:, 8 + n:9 + n])
                    act.activation(cstat[:, 16:24], cstat[:, 0:8], ACT.Exp,
                                   bias=param[:, C_SINKROW:C_SINKROW + 1]).then_inc(ss_exp, 1)
                    act.wait_ge(st_mm, 5)
                    PTC = tiles(cs_t, 16)
                    act.activation(PTC[:, 0:8, :], psum[:, 4:6, :].rearrange("p b (n c) -> p (b n) c", c=P), ACT.Copy)
                    act.activation(PTC[0:64, 8:16, :], psum[0:64, 6:8, :].rearrange("p b (n c) -> p (b n) c", c=P),
                                   ACT.Copy).then_inc(st_taken, 1)
                    high(HH[:, :, 0:SAMPLE], tiles(ocs, 8), spv_taken, 5)
                    lo.add()
                act.wait_ge(lo_made, lo.at)
                take_pairs(2, XA)

                def ready_r(kc):
                    act.wait_ge(free[kc % 2], u.free[kc % 2].at - 3 + kc // 2)

                def ready_x(kc):
                    act.wait_ge(x_made, xm.add())

                squares(ready_r)
                squares(ready_x)
                norm_highs()

                def ff_up(h):
                    for m in range(2):
                        act.wait_ge(lo_made, lo.at - 1 + m)
                        take(TMP[:, m, :], m, m == 1, ACT.Relu)
                    for m in range(2):
                        high(HIDH[h][:, m, :], TMP[:, m, :], scaled, scl.add())
                    lo.add(2)

                ff_up(0)
                with turns(act, 7, {lo: 4, scl: 4, **u.per(2, 8, 2, 8)}):
                    ff_up(1)
                    u.skip(8)
                    ff_up(0)
                    u.skip(8)
                ff_up(1)
                u.skip(8, 8)
                act.wait_ge(lo_made, lo.at)
                squares(ready_r)
                for m in range(8):
                    act.wait_ge(x_made, xm.at + m + 1)
                    if m < 7:
                        take(XD[:, m, :], m, m == 6 and False)
                    else:
                        u.done.add(1)
                        take(XD[:, m, :], m, True)
                squares(ready_x)
                norm_highs()
                act.wait_ge(lo_made, lo.at)
                for m in range(8):
                    if m >= 2:
                        act.wait_ge(x_made, xm.at + m - 1)
                    take(TMP[:, m % 2, :], m, m % 2 == 1, ACT.Sigmoid)
                if layer == 0:
                    act.wait_ge(x_made, xm.at + 8)
                    squares(ready_x)
                    norm_highs()

        @block.vector
        def _(dve):
            u, lo, hi, rms, own = Units(), Count(lo_made), Count(hi_act), Count(rms_made), Count(dve_own)
            xin = Count(x_in)
            xin.add(16)
            n_s, n_exp, n_pv, n_out, n_we, n_turn = (Count(s) for s in (s_mm, exp_made, pv_mm, o_out, w_exp, turned))

            def step(ins):
                ins.then_inc(dve_own, 1)
                dve.wait_ge(dve_own, own.add())

            def late(sem_, value):
                if not (isinstance(value, int) and value <= 0):
                    dve.wait_ge(sem_, value)

            def copy(dst, src):
                return dve.tensor_scalar(dst, src, 1.0, None, ALU.mult)

            def low(dst, src, high_):
                dve.wait_ge(hi_act, hi.add())
                dve.tensor_tensor(dst, src, high_.bitcast(F32), ALU.subtract).then_inc(lo_made, 1)
                lo.add()

            def inverse():
                dve.wait_ge(rms_made, rms.add())
                step(dve.reciprocal(rs[:, :], rs[:, :]))

            def normalise(layer, kind):
                inverse()
                first = lo.at
                for kc in range(KC + 1):
                    if kc < KC:
                        if kc >= 2:
                            dve.wait_ge(lo_made, first + kc - 1)
                        dve.scalar_tensor_tensor(TMP[:, kc % 2, :], XA[:, kc, :], G[:, layer, kind, kc:kc + 1], rs[:, :],
                                                 ALU.mult, ALU.mult).then_inc(scaled, 1)
                    if kc:
                        low(HL[:, kc - 1, :], TMP[:, (kc - 1) % 2, :], HH[:, kc - 1, :])

            def residual(layer, kind):
                inverse()
                dve.wait_ge(x_in, xin.add(16))
                for kc in range(KC + 1):
                    if kc < KC:
                        dve.scalar_tensor_tensor(XA[:, kc, :], XA[:, kc, :], G[:, layer, kind, kc:kc + 1], rs[:, :],
                                                 ALU.mult, ALU.mult).then_inc(dve_own, 1)
                        own.add()
                    if kc:
                        dve.wait_ge(dve_own, own.at - (1 if kc < KC else 0))
                        dve.tensor_tensor(XA[:, kc - 1, :], XA[:, kc - 1, :], XD[:, kc - 1, :], ALU.add).then_inc(x_made, 1)

            def attend(g, heads):
                steps = heads // 2

                def tile(i, nk):
                    for k in range(steps):
                        dve.wait_ge(s_mm, n_s.add())
                        late(exp_made, n_exp.add() - 2)
                        out = sm[:, (k % 2) * 512:(k % 2) * 512 + 512].rearrange("p (h c) -> p h c", h=2)[:, :, 0:nk * P]
                        m = mask[:, 2 * P:3 * P] if g == 2 else mask[:, 2 * P - nk * P:2 * P]
                        if k == 0:
                            late(o_out if heads == H_A else o_made, n_out.at if heads == H_A else n_om.at)
                        dve.tensor_tensor(out, psum[:, k % 2, :].rearrange("p (h c) -> p h c", h=2)[:, :, 0:nk * P],
                                          m.unsqueeze(1).broadcast_to([P, 2, nk * P]), ALU.add).then_inc(s_masked, 1)
                        dve.wait_ge(s_masked, n_mk.add())
                        red = dve.tensor_reduce(stat[:, 2 * k:2 * k + 2], out, AX, ALU.max, negate=True)
                        if heads == H_C:
                            step(red)
                            red = dve.tensor_tensor(stat[:, 2 * k:2 * k + 2], stat[:, 2 * k:2 * k + 2],
                                                    nsink[:, 2 * k:2 * k + 2], ALU.min)
                        red.then_inc(max_made, 1)
                    dve.wait_ge(exp_made, n_exp.at)
                    sums_ = stat[:, 16:16 + heads]
                    if heads == H_C:
                        dve.wait_ge(max_made, n_s.at - 0 * steps)
                        dve.tensor_tensor(stat[:, 32:48], param[:, C_SINK:C_SINK + 16], stat[:, 0:16], ALU.add).then_inc(w_dif, 1)
                        dve.wait_ge(w_exp, n_we.add())
                        step(dve.tensor_tensor(sums_, sums_, stat[:, 48:64], ALU.add))
                    step(dve.reciprocal(stat[:, 64:64 + heads], sums_))
                    dve.wait_ge(pv_mm, n_pv.add(steps))
                    inv = stat[:, 64:64 + heads].unsqueeze(2).broadcast_to([P, heads, HEAD_DIM])
                    if heads == H_A:
                        dve.tensor_copy(o_st[:, 512:520], sums_)
                        dve.tensor_copy(o_st[:, 520:528], stat[:, 0:8])
                        dve.tensor_tensor(o_st[:, 0:512].rearrange("p (h d) -> p h d", h=8),
                                          psum[:, 4, :].rearrange("p (h d) -> p h d", h=8), inv, ALU.mult).then_inc(o_made, 1)
                        n_out.add(16)
                        n_om.add()
                    else:
                        late(turned, n_turn.at)
                        dve.tensor_tensor(on_c[:, :].rearrange("p (h d) -> p h d", h=16),
                                          psum[:, 4:6, :].rearrange("p b (h d) -> p (b h) d", h=8), inv, ALU.mult)\
                            .then_inc(o_made, 1)
                        n_turn.add()
                        n_om.add()
                        low(HL[:, :, bass.ds(i * P + SAMPLE, P)], psum[:, 6:8, :].rearrange("p b (k c) -> p (b k) c", c=P),
                            HH[:, :, bass.ds(i * P + SAMPLE, P)])

                per = {n_s: steps, n_exp: steps, n_mk: steps, n_pv: steps, n_om: 1}
                if heads == H_A:
                    per[n_out] = 16
                else:
                    per |= {own: steps + 2, n_we: 1, n_turn: 1, hi: 1, lo: 1}
                if heads == H_A:
                    per[own] = 1
                over_tiles(dve, g, per, tile)

            n_mk, n_om = Count(s_masked), Count(o_made)

            dve.wait_ge(const_in, 64)
            dve.tensor_scalar(nsink[:, :], param[:, C_SINK:C_SINK + 17], -1.0, None, ALU.mult)
            normalise(0, 0)
            dve.wait_ge(lo_made, lo.at)
            dve.memset(QST, 0.0).then_inc(zeroed, 1)
            u.skip(2, 2)
            for g in range(3):
                u.skip(2, 2, 2, 2, 4, 4)
                attend(g, H_A)

            kvi, mi, ssm_, sse, spv, stt_ = (Count(ss_mm), Count(mask_in), Count(ss_mm), Count(ss_exp), Count(kv_used), Count(st_mm))
            QSF, QB = qs[:, :].rearrange("p (g j t) -> p g j t", g=3, j=4), qb[:, :].rearrange("p (g c) -> p g c", g=3)
            dve.wait_ge(sx_in, 48)
            dve.wait_ge(pv_mm, N_A_STEPS)
            step(dve.memset(qb[:, :], 0.0))
            OAS = tiles(oas, 4)
            with turns(dve, 4, {ssm_: 2, mi: 16, own: 3, sse: 1, spv: 2, stt_: 1}) as z:
                for b in range(2):
                    late(ss_mm, ssm_.at)
                    if b == 0:
                        pass
                    for par in range(2):
                        rows = slice(64 * par, 64 * par + 64)
                        out = QB[rows].rearrange("p g (j c) -> p g j c", c=80)[:, :, :, 8 * par:8 * par + 8]
                        ins = dve.tensor_scalar(out, QSF[rows, :, :, bass.ds(z * 16 + b * 8, 8)], HEAD_DIM ** -0.5, None, ALU.mult)
                    ins.then_inc(qb_made, 1)
                    ssm_.add()
                dve.wait_ge(ss_mm, ssm_.at)
                dve.wait_ge(mask_in, mi.add(16))
                dve.wait_ge(st_mm, stt_.at)
                stt_.add()
                dve.tensor_tensor(s_sb[:, 0:320], psum[:, 0, 0:320], sm_sb[:, 0:320], ALU.add)
                dve.tensor_tensor(s_sb[:, 320:SK].rearrange("p (b c) -> p b c", b=2), psum[:, 1:3, :],
                                  sm_sb[:, 320:SK].rearrange("p (b c) -> p b c", b=2), ALU.add).then_inc(ss_masked, 1)
                step(dve.tensor_copy(sstat[:, 4:5], nsink[:, 0:1]))
                dve.tensor_reduce(sstat[:, 0:1], s_sb[:, :], AX, ALU.max, negate=True).then_inc(ss_max, 1)
                dve.wait_ge(ss_exp, sse.add())
                step(dve.reciprocal(sstat[:, 2:3], sstat[:, 1:2]))
                dve.tensor_scalar(s_sb[:, :], s_sb[:, :], sstat[:, 2:3], None, ALU.mult).then_inc(ss_norm, 1)
                dve.wait_ge(kv_used, spv.add(2))
                for par in range(2):
                    rows = slice(64 * par, 64 * par + 64)
                    src = psum[rows, 6, 0:128].rearrange("p (b j c) -> p b j c", b=2, j=4)[:, :, :, 8 * par:8 * par + 8]
                    out = OAS[rows, :, bass.ds(z * 16, 16)].rearrange("p j (b q) -> p b j q", b=2)
                    ins = copy(out, src)
                    if par == 0:
                        step(ins)
                ins.then_inc(spv_taken, 1)

            def vec(v, n=1):
                return sc[:, v * ST:(v + n) * ST]

            def vv(out, x, y, op):
                step(dve.tensor_tensor(vec(out), vec(x), vec(y), op))

            def vs(out, x, s1, op0, s2=None, op1=None):
                step(dve.tensor_scalar(vec(out), vec(x), s1, s2, op0, op1) if op1 else
                     dve.tensor_scalar(vec(out), vec(x), s1, None, op0))

            PI, ROUND = 3.1415925, 12582912.0
            dve.wait_ge(ssm_in, 32)
            dve.wait_ge(vec_act, 1)
            vv(V_X, V_ARE, V_DT, ALU.mult)
            vv(V_TH, V_AIM, V_DT, ALU.mult)
            vs(V_T1, V_TH, 1 / 6.283185307179586, ALU.mult)
            vs(V_T1, V_T1, ROUND, ALU.add)
            vs(V_T1, V_T1, -ROUND, ALU.add)
            step(dve.scalar_tensor_tensor(vec(V_K), vec(V_T1), -6.28125, vec(V_TH), ALU.mult, ALU.add))
            step(dve.scalar_tensor_tensor(vec(V_K), vec(V_T1), -1.9353071795864769e-3, vec(V_K), ALU.mult, ALU.add))
            vs(V_COS, V_K, 1.5707963267948966, ALU.add)
            vs(V_T1, V_COS, PI, ALU.is_gt)
            step(dve.scalar_tensor_tensor(vec(V_COS), vec(V_T1), -6.283185307179586, vec(V_COS), ALU.mult, ALU.add))
            vs(V_COS, V_COS, -PI, ALU.max, PI, ALU.min)
            step(dve.tensor_scalar(vec(V_K), vec(V_K), -PI, PI, ALU.max, ALU.min))
            dve.tensor_copy(vec(V_T3), vec(V_K)).then_inc(vec_arg, 1)
            dve.wait_ge(vec_act, 2)
            vv(V_ABR, V_R, V_COS, ALU.mult)
            vv(V_ABI, V_R, V_SIN, ALU.mult)
            vv(V_T1, V_ARE, V_ARE, ALU.mult)
            vv(V_T2, V_AIM, V_AIM, ALU.mult)
            vv(V_T1, V_T1, V_T2, ALU.add)
            step(dve.reciprocal(vec(V_T1), vec(V_T1)))
            vs(V_T2, V_ABR, -1.0, ALU.add)
            vv(V_CR, V_T2, V_ARE, ALU.mult)
            vv(V_T3, V_ABI, V_AIM, ALU.mult)
            vv(V_CR, V_CR, V_T3, ALU.add)
            vv(V_CR, V_CR, V_T1, ALU.mult)
            vv(V_CI, V_ABI, V_ARE, ALU.mult)
            vv(V_T3, V_T2, V_AIM, ALU.mult)
            vv(V_CI, V_CI, V_T3, ALU.subtract)
            vv(V_CI, V_CI, V_T1, ALU.mult)
            step(dve.tensor_copy(vec(V_POW), vec(V_COS)))
            step(dve.tensor_copy(vec(V_POW + 1), vec(V_SIN)))
            for k in range(10):
                w = V_POW + 2 * k
                if k:
                    vv(V_T1, w - 2, w - 2, ALU.mult)
                    vv(V_T2, w - 1, w - 1, ALU.mult)
                    vv(w, V_T1, V_T2, ALU.subtract)
                    vv(w + 1, w - 2, w - 1, ALU.mult)
                    vs(w + 1, w + 1, 2.0, ALU.mult)
                vv(V_T1, w, w, ALU.mult)
                vv(V_T2, w + 1, w + 1, ALU.mult)
                vv(V_T1, V_T1, V_T2, ALU.add)
                vs(V_T1, V_T1, -0.5, ALU.mult, 1.5, ALU.add)
                vv(w, w, V_T1, ALU.mult)
                vv(w + 1, w + 1, V_T1, ALU.mult)

            bum, ysm, hus, ymm = Count(bu_mm), Count(ys_mm), Count(h_used), Count(y_mm)
            SC, SCB = tiles(sc, N_VEC), tiles(scb, N_VEC)
            HS = [t[:, :].rearrange("p (t n s) -> p t n s", t=4, n=NB) for t in (hs_re, hs_im)]
            HF = [t[:, :].rearrange("p (tn s) -> p tn s", s=NS) for t in (hs_re, hs_im)]
            H0 = h0[:, :].rearrange("p (c t n) -> p c t n", c=2, t=ST)
            CB = c_blk[:, :].rearrange("p (t c s) -> p t c s", t=4, c=2)
            BT = bt[:, :].rearrange("p (c t l) -> p c t l", c=2, t=4)

            def wide(v, n):
                return SCB[:, v, :].unsqueeze(2).broadcast_to([P, 4, n])

            def x4(t, n):
                return t[:, 0:4 * n].rearrange("p (t n) -> p t n", t=4)

            def tt(out, x, y, op):
                step(dve.tensor_tensor(out, x, y, op))

            own_at = own.at
            with turns(dve, 4, {own: S5_STEPS, bum: 5, ysm: 1, hus: 3, ymm: 1}) as b:
                step(copy(SCB, SC[:, :, bass.ds(b * 4, 4)]))
                dve.wait_ge(bu_mm, bum.add())
                br, bi_ = (psum[:, 7, 256 * c:256 * c + 256].rearrange("p (t n) -> p t n", t=4) for c in range(2))
                hr_, hi_ = tiles(hs_re, 4), tiles(hs_im, 4)
                tt(x4(xt1, 64), br, wide(V_CR, 64), ALU.mult)
                tt(x4(xt2, 64), bi_, wide(V_CI, 64), ALU.mult)
                tt(hr_, x4(xt1, 64), x4(xt2, 64), ALU.subtract)
                tt(x4(xt1, 64), br, wide(V_CI, 64), ALU.mult)
                dve.tensor_tensor(x4(xt2, 64), bi_, wide(V_CR, 64), ALU.mult).then_inc(bu_used, 1)
                dve.wait_ge(bu_used, b * 5 + 1)
                tt(hi_, x4(xt1, 64), x4(xt2, 64), ALU.add)
                AB = [x4(t, NB) for t in (gr, gi)]
                tt(AB[0], wide(V_ABR, NB), wide(V_ABR, NB), ALU.max)
                tt(AB[1], wide(V_ABI, NB), wide(V_ABI, NB), ALU.max)
                abr, abi = gr[:, 0:32], gi[:, 0:32]

                def advance(pr_, pi_, cr_, ci_):
                    tt(xt1[:, 0:32], pr_, abr, ALU.mult)
                    tt(xt1[:, 32:64], pi_, abi, ALU.mult)
                    tt(xt1[:, 0:32], xt1[:, 0:32], xt1[:, 32:64], ALU.subtract)
                    tt(cr_, cr_, xt1[:, 0:32], ALU.add)
                    tt(xt1[:, 0:32], pr_, abi, ALU.mult)
                    tt(xt1[:, 32:64], pi_, abr, ALU.mult)
                    tt(xt1[:, 0:32], xt1[:, 0:32], xt1[:, 32:64], ALU.add)
                    tt(ci_, ci_, xt1[:, 0:32], ALU.add)

                for c in range(2):
                    step(copy(x4(xt2, 8) if c == 0 else xt2[:, 32:64].rearrange("p (t n) -> p t n", t=4),
                              H0[:, c, bass.ds(b * 4, 4), :]))
                advance(xt2[:, 0:32], xt2[:, 32:64], HF[0][:, :, 0], HF[1][:, :, 0])
                for s in range(1, NS):
                    advance(HF[0][:, :, s - 1], HF[1][:, :, s - 1], HF[0][:, :, s], HF[1][:, :, s])
                for c in range(2):
                    step(copy(H0[:, c, bass.ds(b * 4, 4), :], HS[c][:, :, :, NS - 1]))
                dve.tensor_scalar(hs_im[:, :], hs_im[:, :], -1.0, None, ALU.mult).then_inc(hs_made, 1)
                dve.wait_ge(ys_mm, ysm.add())
                cre, cim = CB[:, :, 0, :], CB[:, :, 1, :]
                tt(x4(gr, P), cre, wide(V_CR, P), ALU.mult)
                tt(x4(gi, P), cim, wide(V_CI, P), ALU.mult)
                tt(x4(xt1, P), cre, wide(V_CI, P), ALU.mult)
                tt(x4(xt2, P), cim, wide(V_CR, P), ALU.mult)
                tt(cre, x4(gr, P), x4(gi, P), ALU.subtract)
                step(dve.scalar_tensor_tensor(cim, x4(xt1, P), -1.0, x4(xt2, P), ALU.mult, ALU.subtract))
                step(dve.memset(BT[:, 0, :, 0:1], 1.0))
                step(dve.memset(BT[:, 1, :, 0:1], 0.0))
                for k in range(6):
                    n = 1 << k
                    wr, wi = wide(V_POW + 2 * k, n), wide(V_POW + 2 * k + 1, n)
                    er, ei = BT[:, 0, :, 0:n], BT[:, 1, :, 0:n]
                    tt(x4(xt1, n), er, wr, ALU.mult)
                    tt(x4(xt2, n), ei, wi, ALU.mult)
                    tt(BT[:, 0, :, n:2 * n], x4(xt1, n), x4(xt2, n), ALU.subtract)
                    tt(x4(xt1, n), er, wi, ALU.mult)
                    tt(x4(xt2, n), ei, wr, ALU.mult)
                    tt(BT[:, 1, :, n:2 * n], x4(xt1, n), x4(xt2, n), ALU.add)
                dve.tensor_copy(xt1[:, 0:4], xt2[:, 0:4]).then_inc(vec_dve, 1)
                for t in range(4):
                    step(dve.tensor_copy(tr[:, 0:64], BT[:, 0, t, :]))
                    step(dve.tensor_copy(ti[:, 0:64], BT[:, 1, t, :]))
                    for k in range(6, 10):
                        n = 1 << k
                        wr, wi = SCB[:, V_POW + 2 * k, t:t + 1], SCB[:, V_POW + 2 * k + 1, t:t + 1]
                        dve.tensor_scalar(xt1[:, 0:n], ti[:, 0:n], wi, None, ALU.mult)
                        step(dve.tensor_scalar(xt2[:, 0:n], tr[:, 0:n], wi, None, ALU.mult))
                        dve.scalar_tensor_tensor(tr[:, n:2 * n], tr[:, 0:n], wr, xt1[:, 0:n], ALU.mult, ALU.subtract)
                        step(dve.scalar_tensor_tensor(ti[:, n:2 * n], ti[:, 0:n], wr, xt2[:, 0:n], ALU.mult, ALU.add))
                    dve.wait_ge(bu_mm, bum.add())
                    ur, ui = psum[:, 0:2, :].rearrange("p b c -> p (b c)"), psum[:, 2:4, :].rearrange("p b c -> p (b c)")
                    dve.tensor_tensor(xt1[:, :], ur, tr[:, :], ALU.mult)
                    step(dve.tensor_tensor(xt2[:, :], ui, ti[:, :], ALU.mult))
                    tt(gr[:, :], xt1[:, :], xt2[:, :], ALU.add)
                    dve.tensor_tensor(xt1[:, :], ui, tr[:, :], ALU.mult)
                    dve.tensor_tensor(xt2[:, :], ur, ti[:, :], ALU.mult).then_inc(bu_used, 1)
                    dve.wait_ge(bu_used, b * 5 + t + 2)
                    tt(gi[:, :], xt1[:, :], xt2[:, :], ALU.subtract)
                    if t:
                        dve.wait_ge(h_used, hus.add())
                    r = SCB[:, V_R, t:t + 1].broadcast_to([P, SEQ])
                    dve.tensor_tensor_scan(xt1[:, :], r, gr[:, :], 0.0, ALU.mult, ALU.add)
                    step(dve.tensor_tensor_scan(xt2[:, :], r, gi[:, :], 0.0, ALU.mult, ALU.add))
                    dve.tensor_tensor(gr[:, :], xt1[:, :], tr[:, :], ALU.mult)
                    step(dve.tensor_tensor(gi[:, :], xt2[:, :], ti[:, :], ALU.mult))
                    tt(sr[:, :], gr[:, :], gi[:, :], ALU.subtract)
                    dve.tensor_tensor(gr[:, :], xt1[:, :], ti[:, :], ALU.mult)
                    step(dve.tensor_tensor(gi[:, :], xt2[:, :], tr[:, :], ALU.mult))
                    dve.tensor_tensor(si[:, :], gr[:, :], gi[:, :], ALU.add).then_inc(h_made, 1)
                    dve.wait_ge(h_made, b * 4 + t + 1)
                    copy(SC[:, V_X, bass.ds(b * 4 + t, 1)], sr[:, SEQ - 1:SEQ])
                    step(copy(SC[:, V_TH, bass.ds(b * 4 + t, 1)], si[:, SEQ - 1:SEQ]))
                dve.wait_ge(y_mm, ymm.add())
                z, ub = ZB[:, bass.ds(b, 1), :], U[:, bass.ds(b, 1), :]
                d = param[:, bass.ds(b + C_D, 1)]
                dve.scalar_tensor_tensor(z[:, 0, 0:SAMPLE], ub[:, 0, 0:SAMPLE], d, psum[:, 6, 0:SAMPLE], ALU.mult, ALU.add)
                dve.scalar_tensor_tensor(z[:, 0, SAMPLE:PADS], ub[:, 0, SAMPLE:PADS], d,
                                         psum[:, 4:6, :].rearrange("p b c -> p (b c)"), ALU.mult, ALU.add).then_inc(y_made, 1)
            dve.memset(ZB[:, :, PADS:T], 0.0).then_inc(zeroed, 1)
            vv(V_T1, V_X, V_CR, ALU.mult)
            vv(V_T2, V_TH, V_CI, ALU.mult)
            vv(V_T1, V_T1, V_T2, ALU.subtract)
            vv(V_T2, V_X, V_CI, ALU.mult)
            vv(V_T3, V_TH, V_CR, ALU.mult)
            dve.tensor_tensor(vec(V_T2), vec(V_T2), vec(V_T3), ALU.add).then_inc(state_out, 1)
            for m in range(4):
                low(ZL[:, m, :], ZB[:, m, :], ZH[:, m, :])

            for m in range(4):
                dve.wait_ge(free[m % 2], UNITS_AT[W_GLU] // 2 + m // 2 + 1)
                dve.tensor_tensor(TMP[:, m % 2, :], TMP[:, m % 2, :], ZB[:, m, :], ALU.mult).then_inc(scaled, 1)
                low(HL[:, 4 + m, :], TMP[:, m % 2, :], HH[:, 4 + m, :])
            u.skip(4)

            dve.memset(HH[:, 0:4, PADS:T].bitcast(F32), 0.0)
            dve.memset(HL[:, 0:4, PADS:T].bitcast(F32), 0.0)
            low(HL[:, 0:4, 0:SAMPLE], tiles(oas, 4), HH[:, 0:4, 0:SAMPLE])
            ogl = [Count(s) for s in og_loaded]
            turn_ = Count(turned)
            with turns(dve, 4, {ogl[0]: 16, ogl[1]: 16, own: 20, n_we: 2, hi: 2, lo: 2}) as t:
                for b in range(2):
                    IN = og_in[:, b * 3 * ROW:(b + 1) * 3 * ROW].rearrange("p (g c) -> p g c", g=3)
                    W = c_w[:, b * 64:b * 64 + 64]
                    acc = c_acc[:, b * 512:b * 512 + 512].rearrange("p (h d) -> p h d", h=8)
                    og_o = [IN[:, g, 0:512].rearrange("p (h d) -> p h d", h=8) for g in range(3)]
                    dve.wait_ge(og_loaded[b], ogl[b].add(16))
                    nm, ls = IN[:, :, 520:528], IN[:, :, 512:520]
                    tt(W[:, 0:8], nm[:, 0], nm[:, 1], ALU.min)
                    tt(W[:, 0:8], W[:, 0:8], nm[:, 2], ALU.min)
                    E = W[:, 32:56].rearrange("p (g h) -> p g h", g=3)
                    D = W[:, 8:32].rearrange("p (g h) -> p g h", g=3)
                    dve.tensor_tensor(D, W[:, 0:8].unsqueeze(1).broadcast_to([P, 3, 8]), nm, ALU.subtract).then_inc(w_dif, 1)
                    dve.wait_ge(w_exp, n_we.add())
                    tt(E, E, ls, ALU.mult)
                    tt(W[:, 0:8], E[:, 0], E[:, 1], ALU.add)
                    tt(W[:, 0:8], W[:, 0:8], E[:, 2], ALU.add)
                    step(dve.reciprocal(W[:, 56:64], W[:, 0:8]))
                    tt(D, E, W[:, 56:64].unsqueeze(1).broadcast_to([P, 3, 8]), ALU.mult)
                    for g in range(3):
                        dve_in = og_o[g]
                        ins = dve.tensor_tensor(dve_in, dve_in, D[:, g].unsqueeze(2).broadcast_to([P, 8, HEAD_DIM]), ALU.mult)
                    step(ins)
                    step(dve.tensor_tensor(og_o[1], og_o[0], og_o[1], ALU.add))
                    dve.tensor_tensor(acc, og_o[1], og_o[2], ALU.add).then_inc(comb_made, 1)
                    dve.wait_ge(comb_made, t * 2 + b + 1)
                    step(dve.tensor_copy(W[:, 0:4], W[:, 4:8]))
                    dve.tensor_copy(W[:, 0:4], W[:, 4:8]).then_inc(og_used, 1)
                    cols = bass.ds(t * 256 + SAMPLE + P * b, P)
                    low(HL[:, 0:4, cols], psum[:, 6 + b, :].rearrange("p (k c) -> p k c", c=P), HH[:, 0:4, cols])

            for layer in range(2):
                if layer == 1:
                    u.skip(2, 2, 2, 2, 2, 4)
                    dve.wait_ge(x_made, 16 + 8)
                    dve.wait_ge(lo_made, lo.at)
                    dve.wait_ge(free[0], UNITS_AT[W_QC] // 2 + 1)
                    dve.memset(qc_st[:, :], 0.0).then_inc(zeroed, 1)
                    attend(0, H_C)
                    dve.memset(HH[:, :, PADS:T].bitcast(F32), 0.0)
                    dve.memset(HL[:, :, PADS:T].bitcast(F32), 0.0)
                    dve.wait_ge(s_mm, N_A_STEPS + N_C_STEPS)
                    step(dve.memset(qc_st[:, :], 0.0))
                    QS = qc_st[:, :].rearrange("p (n j h q) -> p n j h q", n=NB, j=2, h=16)
                    for j in range(2):
                        for o in range(2):
                            for par in range(2):
                                src = XA[64 * par:64 * par + 64, 4 * j + 2 * o:4 * j + 2 * o + 2, 0:SAMPLE]
                                h = 8 * j + 4 * o + par
                                out = QS[64 * o:64 * o + 64, :, j, h:h + 3:2, :]
                                ins = dve.tensor_scalar(out.rearrange("p n y q -> p y n q"), src.rearrange("p y (n q) -> p y n q", n=NB),
                                                        HEAD_DIM ** -0.5, None, ALU.mult)
                                if not (j and o and par):
                                    step(ins)
                    ins.then_inc(qb_made, 1)
                    dve.wait_ge(ss_mm, 9)
                    S = tiles(cs_s, 4)
                    step(dve.tensor_tensor(S, psum[:, 0:4, 0:2 * SKC], tiles(cm_sb, 4), ALU.add))
                    step(dve.tensor_reduce(cstat[:, 0:8], tiles(cs_s, NB), AX, ALU.max, negate=True))
                    dve.tensor_scalar(cstat[:, 0:8], cstat[:, 0:8], nsink[:, 16:17], None, ALU.min).then_inc(ss_max, 1)
                    dve.wait_ge(ss_exp, 5)
                    step(dve.tensor_tensor(cstat[:, 8:16], cstat[:, 8:16], cstat[:, 16:24], ALU.add))
                    step(dve.reciprocal(cstat[:, 24:32], cstat[:, 8:16]))
                    S8 = tiles(cs_s, NB)
                    dve.tensor_tensor(S8, S8, cstat[:, 24:32].unsqueeze(2).broadcast_to([P, NB, SKC]), ALU.mult).then_inc(ss_norm, 1)
                    dve.wait_ge(spv_mm, 1)
                    OC = tiles(ocs, 8)
                    O = psum[:, 0:2, :].rearrange("p b (n c) -> p (b n) c", n=4)
                    for j in range(2):
                        for o in range(2):
                            for par in range(2):
                                src = O[64 * o:64 * o + 64, :, j * 64 + o * 32 + par * 8:j * 64 + o * 32 + 32]
                                for y in range(2):
                                    ins = dve.tensor_copy(
                                        OC[64 * par:64 * par + 64, 4 * j + 2 * o + y, :].rearrange("p (n q) -> p n q", n=NB),
                                        src[:, :, y * 16:y * 16 + 8])
                                    if not (j and o and par and y):
                                        step(ins)
                    ins.then_inc(spv_taken, 1)
                    low(HL[:, :, 0:SAMPLE], OC, HH[:, :, 0:SAMPLE])
                u.skip(2, 2, 2, 2)
                residual(layer, 1)
                normalise(layer, 2)
                dve.wait_ge(x_out, 16 + 32 * layer)
                step(dve.memset(XA, 0.0))

                def ff_up(h):
                    for m in range(2):
                        u.skip_half(m)
                        dve.wait_ge(free[m], u.free[m].at)
                        dve.tensor_tensor(TMP[:, m, :], TMP[:, m, :], TMP[:, m, :], ALU.mult).then_inc(scaled, 1)
                    for m in range(2):
                        low(HIDL[h][:, m, :], TMP[:, m, :], HIDH[h][:, m, :])

                def ff_down():
                    for m in range(8):
                        if m < 2:
                            dve.wait_ge(free[m % 2], u.free[m % 2].at)
                        u.wait(dve, m == 7)
                        dve.tensor_tensor(chunked(XA[:, m, :]), chunked(XA[:, m, :]), UNIT[m % 2], ALU.add).then_inc(free[m % 2], 1)
                        u.free[m % 2].add()

                ff_up(0)
                with turns(dve, 7, {lo: 4, hi: 4, **u.per(2, 8, 2, 8)}):
                    ff_up(1)
                    ff_down()
                    ff_up(0)
                    ff_down()
                ff_up(1)
                ff_down()
                ff_down()
                residual(layer, 3)
                u.skip(0 + 8)
                u.done.add()
                normalise(layer, 4)
                for m in range(8):
                    if m % 2 == 0:
                        u.skip(2)
                    dve.wait_ge(free[m % 2], u.free[m % 2].at)
                    step(dve.tensor_tensor(TMP[:, m % 2, :], TMP[:, m % 2, :], XD[:, m, :], ALU.mult))
                    dve.tensor_tensor(XA[:, m, :], XA[:, m, :], TMP[:, m % 2, :], ALU.add).then_inc(x_made, 1)
                if layer == 0:
                    normalise(1, 0)


def _layouts(i):
    import numpy as np
    f = lambda name: np.asarray(i[name])

    def ktiles(w):
        return w.reshape(-1, P, w.shape[1]).transpose(1, 0, 2)

    def feature_major(sample, prompt):
        t = np.zeros((sample.shape[-1], T), sample.dtype)
        t[:, :SAMPLE] = sample.reshape(SAMPLE, -1).T
        t[:, SAMPLE:PADS] = prompt.reshape(SEQ, -1).T
        return ktiles(t)

    out = {"xT": feature_major(f("x_sample"), f("x_prompt"))}
    wall = np.zeros((N_SLOTS, P, SLOT), f("w_ff1").dtype)

    def put(slot, w):
        w = ktiles(w).reshape(P, -1)
        wall[slot, :, :w.shape[1]] = w
        return slot + 1

    def columns(slot, w):
        for c in range(0, w.shape[1], 256):
            slot = put(slot, w[:, c:c + 256])
        return slot

    w_in = f("w_in_ab")[0]
    columns(W_U, w_in[:, 9 * 512:])
    columns(W_QKV, w_in[:, :9 * 512])
    put(W_GLU, f("w_glu")[0])
    columns(W_OUT[0], f("w_out_ab")[0])
    columns(W_QC, f("w_in_c")[0])
    columns(W_OUT[1], f("w_out_c")[0])
    for layer in range(2):
        w1, w2, s = f("w_ff1")[layer], f("w_ff2")[layer], W_FF[layer]
        up = [w1[:, 256 * k:256 * k + 256] for k in range(FF_BLOCKS)]
        down = [w2[256 * k:256 * k + 256] for k in range(FF_BLOCKS)]
        s = put(s, up[0])
        for k in range(1, FF_BLOCKS):
            s = put(s, up[k])
            s = put(s, down[k - 1])
        put(s, down[-1])
        wall[W_PLE[layer]] = feature_major(f("p_sample")[layer], f("p_prompt")[layer]).reshape(P, -1)
        put(W_PLE[layer] + 1, f("w_ple")[layer])
        columns(W_GATE[layer], f("w_ple_gate")[layer])
    out["wall"] = wall

    tri = np.arange(P)[:, None] - np.arange(P)[None, :]
    consts = np.zeros((P, 5 * P), np.float32)
    consts[:, 0:P] = np.eye(P)
    consts[:, P:2 * P] = 1
    consts[:, 2 * P:3 * P] = np.where(tri <= 0, 0, -1e30)
    consts[:, 3 * P:4 * P] = np.where(tri >= 0, 0, -1e30)
    half = np.arange(P) % 2
    consts[:, 4 * P:5 * P] = np.where((tri >= 0) & (half[:, None] == half[None, :]), 0, -1e30)
    out["consts"] = consts
    params = np.zeros((P, N_PARAM), np.float32)
    gains = np.stack([f("g_" + g) for g in GAINS], 1)
    params[:, 0:80] = gains.reshape(2, 5, KC, P).transpose(3, 0, 1, 2).reshape(P, 80)
    params[:, C_GLU:C_GLU + 4] = f("b_glu")[0].reshape(4, P).T
    params[:, C_D:C_D + 4] = f("ssm_d")[0].reshape(4, P).T
    params[:, C_SINK:C_SINK + 16] = f("sinks_c")[0][None, :]
    params[:, C_SINKROW] = np.repeat(f("sinks_c")[0], NS)
    params[:, C_EPS] = EPS
    out["params"] = params

    s = np.tile(np.arange(NS), 2 * H_A)[:, None]
    b = np.repeat(np.arange(2), 64)[:, None]
    t = np.arange(SAMPLE)[None, :]
    smask = np.zeros((4, P, SK), bool)
    for z in range(4):
        new = [(t // NS == 2 * z + b) & (t % NS <= s) & ((s - t % NS) % d == 0) for d in DILATION]
        r1, r4 = np.arange(128)[None, :], np.arange(512)[None, :]
        smask[z] = np.concatenate([r1 >= s, *new, (r4 >= s) & ((r4 - s) % 4 == 0), (np.arange(512)[None, :] % 8 == s)], 1)
    out["smask"] = np.where(smask, 0, -1e30).astype(np.float32)
    sc_ = np.tile(np.arange(NS), H_C)[:, None]
    cm = [np.concatenate([np.arange(P)[None, :] >= sc_, (t // NS == n) & (t % NS <= sc_)], 1) for n in range(NB)]
    out["cmask"] = np.where(np.concatenate(cm, 1), 0, -1e30).astype(np.float32)

    def states(x):
        return x.reshape(ST, P, *x.shape[2:]).swapaxes(0, 1)

    dt = np.repeat(f("ssm_log_dt")[0][:, None], 64, 1)
    out["ssm"] = np.stack([states(f("ssm_a_re")[0]), states(f("ssm_a_im")[0]), states(dt)], 1).reshape(P, 3 * ST)
    h0 = [states(f(k)[0].transpose(1, 2, 0)) for k in ("state_b_re", "state_b_im")]
    out["h0"] = np.stack(h0, 1).reshape(P, -1)
    bm, cm_ = np.zeros((4, P, 4, 2, P), np.float32), np.zeros((4, P, 4, 2, P), np.float32)
    for g in range(32):
        blk, gl = divmod(g, 8)
        tile, part = divmod(gl, 2)
        for c, (kb, kc) in enumerate((("ssm_b_re", "ssm_c_re"), ("ssm_b_im", "ssm_c_im"))):
            bm[blk, 16 * gl:16 * gl + 16, tile, c, 64 * part:64 * part + 64] = f(kb)[0, g].T
            cm_[blk, 64 * part:64 * part + 64, tile, c, 16 * gl:16 * gl + 16] = f(kc)[0, g].T
    out["bmat"], out["cmat"] = bm.reshape(4, P, 1024), cm_.reshape(4, P, 1024)

    def keys(c):
        n, r = c.shape[:2]
        return c.reshape(n, r, -1, P).transpose(0, 3, 2, 1).reshape(n, P, -1)

    for g, name in enumerate(("cache_a1_kv", "cache_a2_kv", "cache_a3_kv")):
        c = f(name)[0]
        out[f"kt{g}"], out[f"v{g}"] = keys(c[:, 0]), c[:, 1].reshape(NB, ROWS[g], 512)
    c = f("cache_c_kv")[0]
    out["ktc"], out["vc"] = keys(c[:, 0]), c[:, 1].reshape(NB, ROWS_C, 256)
    return out


_OUTS = {"yT": (P, KC, T), "st_s": (P, 2 * ST * NB), "st_p": (P, 2 * ST),
         **{f"okp{g}": (P, 4, r) for g, r in enumerate(ROWS)}, **{f"ovp{g}": (r, 512) for g, r in enumerate(ROWS)},
         **{f"oks{g}": (NB, P, 4, r - NS) for g, r in enumerate(ROWS)},
         **{f"ovs{g}": (NB, r - NS, 512) for g, r in enumerate(ROWS)},
         **{f"oks_new{g}": (P, 4, SAMPLE) for g in range(3)}, **{f"ovs_new{g}": (SAMPLE, 512) for g in range(3)},
         "okc_p": (P, 2, ROWS_C), "ovc_p": (ROWS_C, 256), "okc_s": (NB, P, 2, ROWS_C - NS),
         "ovc_s": (NB, ROWS_C - NS, 256), "okc_new": (P, 2, SAMPLE), "ovc_new": (SAMPLE, 256)}


def kernel(**inputs):
    import numpy as np
    import concourse.bacc as bacc
    from concourse.bass_utils import run_bass_kernel_spmd as run

    nc = bacc.Bacc("TRN2", target_bir_lowering=False, num_devices=1)
    arrays, a = {}, {}
    for name, x in _layouts(inputs).items():
        x = np.ascontiguousarray(x)
        arrays[f"in_{name}"] = x
        a[name] = nc.dram_tensor(f"in_{name}", x.shape, mybir.dt.from_np(x.dtype), kind="ExternalInput").ap()
    for name, shape in _OUTS.items():
        a[name] = nc.dram_tensor(f"out_{name}", shape, F32, kind="ExternalOutput").ap()
    for name in ("kt", "v", "okp", "ovp", "oks", "ovs", "oks_new", "ovs_new"):
        a[name] = [a[f"{name}{g}"] for g in range(3)]
    build(nc, a)
    r = run(nc, [arrays], core_ids=[0]).results[0]
    o = {name: r[f"out_{name}"] for name in _OUTS}

    y = o["yT"].transpose(2, 1, 0).reshape(T, D_MODEL)
    outs = [y[SAMPLE:PADS].reshape(1, SEQ, D_MODEL), y[:SAMPLE].reshape(NB, NS, D_MODEL)]

    def prompt(k, v, heads):
        k = k.transpose(2, 1, 0).reshape(v.shape)
        return np.stack([k, v]).reshape(1, 1, 2, -1, heads, HEAD_DIM)

    def sample(k, k_new, v, v_new, heads):
        k = k.transpose(0, 3, 2, 1).reshape(v.shape)
        k_new = k_new.transpose(2, 1, 0).reshape(NB, NS, -1)
        k = np.concatenate([k, k_new], 1)
        v = np.concatenate([v, v_new.reshape(NB, NS, -1)], 1)
        return np.stack([k, v], 1).reshape(1, NB, 2, -1, heads, HEAD_DIM)

    for g in range(3):
        outs.append(prompt(o[f"okp{g}"], o[f"ovp{g}"], H_A))
        outs.append(sample(o[f"oks{g}"], o[f"oks_new{g}"], o[f"ovs{g}"], o[f"ovs_new{g}"], H_A))
    st_p = o["st_p"].reshape(P, 2, ST).transpose(1, 2, 0).reshape(2, 1, 1, 32, N_STATE)
    st_s = o["st_s"].reshape(P, 2, ST, NB).transpose(1, 3, 2, 0).reshape(2, 1, NB, 32, N_STATE)
    outs += [st_p[0], st_s[0], st_p[1], st_s[1]]
    outs.append(prompt(o["okc_p"], o["ovc_p"], 4))
    outs.append(sample(o["okc_s"], o["okc_new"], o["ovc_s"], o["ovc_new"], 4))
    return tuple(outs)
```

```python
from contextlib import ExitStack, contextmanager

import concourse.bass as bass
from concourse import mybir
from concourse.alu_op_type import AluOpType as ALU

F32 = mybir.dt.float32
F32R = mybir.dt.float32r
ACT = mybir.ActivationFunctionType
AX = mybir.AxisListType.X

P = 128
D_MODEL = 1024
KC = D_MODEL // P
HEAD_DIM = 64
N_STATE = 64
H_A = 8
H_C = 16
NB, NS = 8, 8
SAMPLE = NB * NS
SEQ = 1024
T = SAMPLE + SEQ + 4
CH = T // 3
PADS = SAMPLE + SEQ
DILATION = (1, 4, 16)
ROWS = (128, 512, 1024)
ROWS_C = 128
ST = 16
SLOT = 2 * T
FF_BLOCKS = 16
EPS = 1e-6
ROW = 528
GAINS = ("pre_mix", "post_mix", "pre_ffn", "post_ffn", "ple")
SK = 128 + 3 * SAMPLE + 512 + 512
SKC = ROWS_C + SAMPLE

S5_STEPS = 45
W_U, W_QKV, W_GLU, W_OUT = 0, 2, 20, (21, 69)
W_FF, W_PLE, W_GATE = (25, 73), (57, 105), (59, 107)
W_QC, W_KC, W_VC, N_SLOTS = 63, 67, 68, 111

C_GLU, C_D, C_SINK, C_SINKROW, C_EPS, N_PARAM = 80, 84, 88, 104, 105, 106

V_ARE, V_AIM, V_DT, V_X, V_R, V_TH, V_K, V_COS, V_SIN, V_ABR, V_ABI, V_CR, V_CI, V_T1, V_T2, V_T3 = range(16)
V_POW = 16
N_VEC = V_POW + 20


UNITS = ([2] * 2 + ([2] * 4 + [4] * 2) * 3 + [4] + [2] * 4 + [2] + [2, 8] * 15 + [8] + [0, 8] + [2] * 4
         + [2] * 5 + [4] + [2] * 4 + [2] + [2, 8] * 15 + [8] + [0, 8] + [2] * 4)
assert len(UNITS) == N_SLOTS
UNITS_AT = [sum(UNITS[:s]) for s in range(N_SLOTS + 1)]
LO_GLU = 8 + 4 + 4
LO_MIXED_A = LO_GLU + 9
LO_MIXED_C = LO_MIXED_A + 8 + 2 * FF_BLOCKS + 8 + 8 + 9


class Count:

    def __init__(self, sem):
        self.sem, self.base, self.extra = sem, 0, 0

    @property
    def at(self):
        return self.base + self.extra

    def add(self, n=1):
        self.extra += n
        return self.at


@contextmanager
def turns(eng, n, per):
    start = {c: c.at for c in per}
    with eng.Fori(0, n) as i:
        for c, k in per.items():
            c.base, c.extra = start[c] + i * k, 0
        yield i
    for c, k in per.items():
        assert c.extra == k, (c.sem, c.extra, k)
        c.base, c.extra = start[c] + n * k, 0


def build(nc, a):
    x_keep = nc.dram_tensor("x_keep", (P, KC, T), F32).ap()
    og = nc.dram_tensor("og", (3, SEQ, ROW), F32).ap()
    qk_keep = nc.dram_tensor("qk_keep", (P, 3, 8, SAMPLE), F32).ap()
    v_keep = nc.dram_tensor("v_keep", (SAMPLE, 3, 512), F32).ap()

    with ExitStack() as ctx:
        def region(name, cols, *stages):
            made = []
            for stage in stages:
                with ExitStack() as s:
                    for n, c, dt in stage:
                        made.append(s.enter_context(nc.sbuf_tensor(n, [P, c], dt)))
                    assert sum(c for _, c, _ in stage) <= cols, (name, stage)
            whole = ctx.enter_context(nc.sbuf_tensor(name, [P, cols], F32))
            return whole, *made

        def sb(name, cols, dt=F32):
            return ctx.enter_context(nc.sbuf_tensor(name, [P, cols], dt))

        def sem(name):
            return ctx.enter_context(nc.semaphore(name))

        w_raw = sb("w_raw", SLOT)
        w_hi = [sb(f"w_hi{i}", SLOT, F32R) for i in range(2)]
        w_lo = [sb(f"w_lo{i}", SLOT, F32R) for i in range(2)]
        ident, ones, mask, param = sb("ident", P), sb("ones", P), sb("mask", 3 * P), sb("param", N_PARAM)
        oas = sb("oas", 4 * SAMPLE)
        nsink = sb("nsink", 17)
        (_, tmp, rs, q_st, sm, pr, pt, o_st, stat, vs_new, ks_new, sstat, sc, r_blk, hs_re, hs_im, h0, bt, last,
         og_in, c_acc, c_w, ktc_sb, vc_in, cm_sb) = region(
            "region_e", 5680,
            [("tmp", 2 * T, F32), ("rs", T, F32)],
            [("q_st", 1024, F32), ("sm", 1024, F32), ("pr", 1024, F32), ("pt", 1024, F32),
             ("o_st", 2 * ROW, F32), ("stat", 128, F32)],
            [("vs_new", 3 * 512, F32), ("ks_new", 12 * SAMPLE, F32), ("sstat", 16, F32)],
            [("sc", N_VEC * ST, F32), ("r_blk", 8, F32), ("hs_re", 1024, F32), ("hs_im", 1024, F32),
             ("h0", 2 * ST * NB, F32), ("bt", 2048, F32), ("last", 16, F32)],
            [("og_in", 2 * 3 * ROW, F32), ("c_acc", 1024, F32), ("c_w", 128, F32)],
            [("ktc_sb", 2048, F32), ("vc_in", 2048, F32), ("cm_sb", NB * SKC, F32)])
        (_, hid_hi0, hid_hi1, hid_lo0, hid_lo1, xd, v_sb, u_sb, zb_, kc_sb, vc_sb, qc_st, on_c) = region(
            "region_d", 9 * 512 + 4 * T,
            [("hid_hi0", 2 * T, F32R), ("hid_hi1", 2 * T, F32R), ("hid_lo0", 2 * T, F32R), ("hid_lo1", 2 * T, F32R)],
            [("xd", KC * T, F32)],
            [("v_sb", 9 * 512, F32), ("u_sb", 4 * T, F32)],
            [("zb", 4 * T, F32)],
            [("kc_sb", 2 * T, F32), ("vc_sb", 9 * 256, F32), ("qc_st", 2048, F32), ("on_c", 1024, F32)])
        hid_hi, hid_lo = (hid_hi0, hid_hi1), (hid_lo0, hid_lo1)
        (xa, z_hi, z_lo, va, sp_t, qb, qs, tr2, ti2, tr3, ti3, sr1, si1, b_blk1, c_blk1,
         cs_s, cs_t, ocs, cstat) = region(
            "xa", KC * T,
            [("z_hi", 4 * T, F32R), ("z_lo", 4 * T, F32R)],
            [("va", 9 * 512, F32), ("sp_t", 12 * P, F32), ("qb", 960, F32), ("qs", 12 * SAMPLE, F32)],
            [(n, SEQ, F32) for n in ("tr2", "ti2", "tr3", "ti3", "sr1", "si1", "b_blk1", "c_blk1")],
            [("cs_s", NB * SKC, F32), ("cs_t", 2048, F32), ("ocs", 512, F32), ("cstat", 64, F32)])
        (_, h_hi, h_lo, kt_sb0, kt_sb1, s_sb, sm_sb, b_blk0, c_blk0, tr0, ti0, tr1, ti1, gr, gi, xt1, xt2,
         xs1, xs2, sr0, si0, sj, tp) = region(
            "region_bc", 2 * KC * T,
            [("h_hi", KC * T, F32R), ("h_lo", KC * T, F32R)],
            [("kt_sb0", 4 * sum(ROWS), F32), ("kt_sb1", 4 * sum(ROWS), F32), ("s_sb", SK, F32), ("sm_sb", SK, F32)],
            [("b_blk0", 1024, F32), ("c_blk0", 1024, F32)]
            + [(n, SEQ, F32) for n in ("tr0", "ti0", "tr1", "ti1", "gr", "gi", "xt1", "xt2", "xs1", "xs2", "sr0", "si0", "sj")]
            + [("tp", 2048, F32)])
        kt_sb = (kt_sb0, kt_sb1)
        tr, ti = (tr0, tr1, tr2, tr3), (ti0, ti1, ti2, ti3)
        sr, si = (sr0, sr1), (si0, si1)
        b_blk, c_blk = (b_blk0, b_blk1), (c_blk0, c_blk1)
        psum = ctx.enter_context(nc.psum_tensor("psum", [P, 8, 512], F32))

        raw_in, hi_made, split, slot_done = sem("raw_in"), sem("hi_made"), sem("split"), sem("slot_done")
        full, free = sem("full"), (sem("free0"), sem("free1"))
        const_in, const_made = sem("const_in"), sem("const_made")
        x_in, x_out, x_made = sem("x_in"), sem("x_out"), sem("x_made")
        sq_made, sq_used, sums_read, inv_made = sem("sq_made"), sem("sq_used"), sem("sums_read"), sem("inv_made")
        scaled, hi_act, lo_made = sem("scaled"), sem("hi_act"), sem("lo_made")
        dve_own, act_own = sem("dve_own"), sem("act_own")
        q_ready, s_mm, s_masked, max_made, exp_made = (sem(n) for n in ("q_ready", "s_mm", "s_masked", "max_made", "exp_made"))
        pt_mm, pt_taken, pv_mm, o_made, o_out = (sem(n) for n in ("pt_mm", "pt_taken", "pv_mm", "o_made", "o_out"))
        turned, zeroed = sem("turned"), sem("zeroed")
        ss_max, vec_arg = sem("ss_max"), sem("vec_arg")
        out_done, kept = sem("out_done"), sem("kept")
        sx_in, kv_in, kv_used, mask_in = sem("sx_in"), (sem("kv_in0"), sem("kv_in1")), sem("kv_used"), sem("mask_in")
        qb_made, ss_mm, ss_masked, ss_exp, ss_norm = (sem(n) for n in ("qb_made", "ss_mm", "ss_masked", "ss_exp", "ss_norm"))
        st_mm, st_taken, spv_mm, spv_taken = (sem(n) for n in ("st_mm", "st_taken", "spv_mm", "spv_taken"))
        ssm_in, b_in, b_used, blk_in, vec_act, vec_dve, bu_mm, bu_used = (
            sem(n) for n in ("ssm_in", "b_in", "b_used", "blk_in", "vec_act", "vec_dve", "bu_mm", "bu_used"))
        powers_made, level_prod, level_made, xs_made, sr_made, si_made, pool_own = (
            sem(n) for n in ("powers_made", "level_prod", "level_made", "xs_made", "sr_made",
                             "si_made", "pool_own"))
        hs_made, ys_mm, h_used, y_made, state_out = (
            sem(n) for n in ("hs_made", "ys_mm", "h_used", "y_made", "state_out"))
        w_dif, w_exp, comb_made = sem("w_dif"), sem("w_exp"), sem("comb_made")
        og_loaded, og_used = (sem("og_loaded0"), sem("og_loaded1")), sem("og_used")

        def tiles(t, n):
            return t[:, :].rearrange("p (n c) -> p n c", n=n)

        XA, XD, TMP = tiles(xa, KC), tiles(xd, KC), tiles(tmp, 2)
        HH, HL = tiles(h_hi, KC), tiles(h_lo, KC)
        HIDH, HIDL = [tiles(t, 2) for t in hid_hi], [tiles(t, 2) for t in hid_lo]
        U, ZB, ZH, ZL = tiles(u_sb, 4), tiles(zb_, 4), tiles(z_hi, 4), tiles(z_lo, 4)
        V, VC, KCT = tiles(v_sb, 9), tiles(vc_sb, 9), tiles(kc_sb, 2)
        G = param[:, 0:80].rearrange("p (l k c) -> p l k c", l=2, k=5)
        QST, QCST = tiles(q_st, 8), tiles(qc_st, 16)
        OST = tiles(o_st, 2)
        UNIT = [psum[:, 3 * s:3 * s + 3, 0:CH] for s in range(2)]

        def chunked(ap):
            return ap.rearrange("p (c n) -> p c n", c=3)


        def prompt_cols(g, i):
            if g == 0:
                return lambda x: x[:, :, bass.ds(SAMPLE + i * P, P)]
            if g == 1:
                return lambda x: x[:, :, bass.ds(SAMPLE + i[1] * 512 + i[0], P, 4)]
            return lambda x: x[:, :, bass.ds(SAMPLE + i, P, 8)]

        def key_cols(g, i, nk):
            if nk == 1:
                return prompt_cols(g, i)
            if g == 0:
                return lambda x: x[:, :, bass.ds(SAMPLE - P + i * P, 2 * P)]
            return lambda x: x[:, :, bass.ds(SAMPLE + i[0], 2 * P, 4)]

        def value_tile(g, i):
            return 2 * i[0] + i[1] if g == 1 else i

        def over_tiles(eng, g, per_tile, tile):
            if g == 0:
                tile(0, 1)
                with turns(eng, 7, per_tile) as i:
                    tile(i + 1, 2)
            elif g == 1:
                with turns(eng, 4, {c: 2 * k for c, k in per_tile.items()}) as i:
                    tile((i, 0), 1)
                    tile((i, 1), 2)
            else:
                with turns(eng, 8, per_tile) as i:
                    tile(i, 1)

        class Units:

            def __init__(self):
                self.full, self.done, self.free = Count(full), Count(slot_done), (Count(free[0]), Count(free[1]))

            def wait(self, eng, last):
                c = self.done if last else self.full
                eng.wait_ge(c.sem, c.add())

            def skip(self, *slots):
                for n in slots:
                    self.full.add(n - 1)
                    self.done.add()
                    self.free[0].add(n // 2)
                    self.free[1].add(n // 2)

            def skip_half(self, m):
                (self.done if m else self.full).add()
                self.free[m].add()

            def per(self, *slots):
                n = sum(slots)
                return {self.full: n - len(slots), self.done: len(slots), self.free[0]: n // 2, self.free[1]: n // 2}

            def all_free(self, eng):
                eng.wait_ge(free[0], self.free[0].at)
                eng.wait_ge(free[1], self.free[1].at)

        block = ctx.enter_context(nc.Block())
        N_A_STEPS, N_C_STEPS = 3 * 8 * 4, 8 * 8

        @block.sync
        def _(sp):
            spl, stored, units = Count(split), Count(out_done), Units()
            made, oout, keeps = Count(o_made), Count(o_out), Count(kept)
            xin, xout, xm = Count(x_in), Count(x_out), Count(x_made)
            fed = [0]

            def feed(slot, first=False):
                if not first:
                    sp.wait_ge(split, spl.add())
                src = a["wall"][bass.ds(slot, 1), :, :].rearrange("a p n -> p (a n)")
                sp.dma_start(w_raw[:, :], src).then_inc(raw_in, 16)

            def feed_to(end):
                n = end - fed[0]
                if not fed[0]:
                    feed(0, first=True)
                    n, fed[0] = n - 1, 1
                if n > 0:
                    with turns(sp, n, {spl: 1}) as i:
                        feed(i + fed[0])
                fed[0] = end

            def store(dst, src):
                sp.dma_start(dst, src).then_inc(out_done, 16)
                stored.add(16)

            c = a["consts"]
            sp.dma_start(ident[:, :], c[:, 0:P]).then_inc(const_in, 16)
            sp.dma_start(ones[:, :], c[:, P:2 * P]).then_inc(const_in, 16)
            sp.dma_start(mask[:, :], c[:, 2 * P:5 * P]).then_inc(const_in, 16)
            sp.dma_start(param[:, :], a["params"]).then_inc(const_in, 16)
            sp.dma_start(XA, a["xT"]).then_inc(x_in, 16)
            xin.add(16)
            feed_to(11)

            units.skip(2, 2)
            for g in range(3):
                units.skip(2, 2, 2, 2, 4, 4)
                units.all_free(sp)
                w = min(ROWS[g], SEQ)
                store(a["okp"][g], XA[:, 4:8, PADS - w:PADS])
                if g == 0:
                    store(a["ovp"][g], V[:, 7, :])
                elif g == 1:
                    for phase in range(4):
                        store(a["ovp"][g].rearrange("(n r) c -> r n c", r=4)[phase], V[:, 2 * phase + 1, :])
                else:
                    for t in range(8):
                        store(a["ovp"][g].rearrange("(n r) c -> r n c", r=8)[t], V[:, t, :])
                store(a["oks_new"][g], XA[:, 4:8, 0:SAMPLE])
                store(a["ovs_new"][g], V[0:SAMPLE, 8, :])
                sp.dma_start(qk_keep[:, g, :, :], XA[:, :, 0:SAMPLE]).then_inc(kept, 16)
                sp.dma_start(v_keep[:, g, :], V[0:SAMPLE, 8, :]).then_inc(kept, 16)
                keeps.add(32)

                def tile(i, nk, g=g):
                    sp.wait_ge(o_made, made.add())
                    row = og[g]
                    if g == 0:
                        sp.dma_start(row[bass.ds(i * P, P), :], o_st[:, 0:ROW]).then_inc(o_out, 16)
                        oout.add(16)
                    elif g == 1:
                        dst = row.rearrange("(h n r) c -> h r n c", h=2, r=4)[i[1], bass.ds(i[0], 1), :, :]
                        sp.dma_start(dst.rearrange("r n c -> (r n) c"), o_st[:, 0:ROW]).then_inc(o_out, 16)
                        oout.add(16)
                    else:
                        dst = row.rearrange("(n r) c -> r n c", r=8)[bass.ds(i, 1), :, :]
                        sp.dma_start(dst.rearrange("r n c -> (r n) c"), o_st[:, 0:ROW]).then_inc(o_out, 16)
                        oout.add(16)

                over_tiles(sp, g, {made: 1, oout: 16}, tile)
                sp.wait_ge(out_done, stored.at)
                feed_to((17, 23, 23)[g])

            sp.wait_ge(kept, keeps.at)
            sp.wait_ge(o_out, oout.at)
            sp.wait_ge(pv_mm, N_A_STEPS)
            sp.dma_start(tiles(qs, 3).rearrange("p g (j t) -> p g j t", j=4), qk_keep[:, :, 0:4, :]).then_inc(sx_in, 16)
            sp.dma_start(tiles(ks_new, 3).rearrange("p g (j t) -> p g j t", j=4),
                         qk_keep[:, :, 4:8, :]).then_inc(sx_in, 16)
            sp.dma_start(vs_new[0:SAMPLE, :], v_keep.rearrange("t g c -> t (g c)")).then_inc(sx_in, 16)
            used = Count(kv_used)

            def load_batch(n, b):
                o = 0
                for g in range(3):
                    c = 4 * ROWS[g]
                    sp.dma_start(kt_sb[b][:, o:o + c], a["kt"][g][bass.ds(n, 1), :, :].rearrange("n p c -> p (n c)"))\
                        .then_inc(kv_in[b], 16)
                    o += c
                vb = (va, v_sb)[b]
                sp.dma_start(vb[:, 0:512], a["v"][0][bass.ds(n, 1), :, :].rearrange("n p c -> p (n c)")).then_inc(kv_in[b], 16)
                for c in range(4):
                    sp.dma_start(vb[:, 512 * (1 + c):512 * (2 + c)],
                                 a["v"][1][bass.ds(n, 1), P * c:P * c + P, :].rearrange("n p c -> p (n c)"))\
                        .then_inc(kv_in[b], 16)
                    src = a["v"][2][bass.ds(n, 1), 256 * c:256 * c + 256, :].rearrange("n (i s) c -> (n i) s c", s=16)
                    sp.dma_start(vb[:, 512 * (5 + c):512 * (6 + c)], src[:, 0:8, :]).then_inc(kv_in[b], 16)

            def load_mask(z):
                sp.dma_start(sm_sb[:, :], a["smask"][bass.ds(z, 1), :, :].rearrange("z p c -> p (z c)")).then_inc(mask_in, 16)

            masked = Count(ss_masked)
            load_batch(0, 0)
            load_mask(0)
            load_batch(1, 1)
            with turns(sp, 3, {used: 2, masked: 1}) as z:
                sp.wait_ge(kv_used, used.add())
                load_batch(z * 2 + 2, 0)
                sp.wait_ge(ss_masked, masked.add())
                load_mask(z + 1)
                sp.wait_ge(kv_used, used.add())
                load_batch(z * 2 + 3, 1)

            sp.wait_ge(kv_used, 8)
            sp.wait_ge(ss_norm, 4)
            sp.wait_ge(spv_taken, 4)
            sp.dma_start(sc[:, 0:3 * ST], a["ssm"]).then_inc(ssm_in, 16)
            sp.dma_start(h0[:, :], a["h0"]).then_inc(ssm_in, 16)
            for b in range(4):
                sp.dma_start((b_blk + c_blk)[b][:, :], a["bmat"][b]).then_inc(b_in, 16)
            for z in range(2):
                if z == 0:
                    sp.wait_ge(b_used, 1)
                else:
                    sp.wait_ge(h_used, 8)
                for k in range(2):
                    for t, m in ((b_blk[k], "bmat"), (c_blk[k], "cmat")):
                        sp.dma_start(t[:, :], a[m][z * 2 + k]).then_inc(blk_in, 16)
            sp.wait_ge(state_out, 1)
            store(a["st_s"], h0[:, :])
            store(a["st_p"], sc[:, V_T1 * ST:(V_T2 + 1) * ST])

            sp.wait_ge(out_done, stored.at)
            sp.wait_ge(lo_made, LO_GLU)
            ogu = Count(og_used)
            for t in range(2):
                sp.dma_start(tiles(og_in, 2)[:, t, :].rearrange("p (g c) -> p g c", g=3),
                             og[:, P * t:P * t + P, :].rearrange("g p c -> p g c")).then_inc(og_loaded[t], 16)
            with turns(sp, 3, {ogu: 2}) as t:
                for b in range(2):
                    sp.wait_ge(og_used, ogu.add())
                    sp.dma_start(tiles(og_in, 2)[:, b, :].rearrange("p (g c) -> p g c", g=3),
                                 og[:, bass.ds(t * 256 + 256 + P * b, P), :].rearrange("g p c -> p g c"))\
                        .then_inc(og_loaded[b], 16)

            for layer in range(2):
                if layer == 0:
                    sp.wait_ge(lo_made, LO_MIXED_A)
                    sp.dma_start(XD, a["xT"]).then_inc(x_in, 16)
                else:
                    sp.wait_ge(lo_made, LO_MIXED_C)
                    sp.wait_ge(x_out, xout.at)
                    sp.dma_start(XD, x_keep).then_inc(x_in, 16)
                xin.add(16)
                feed_to(W_OUT[layer] + 7)
                sp.wait_ge(x_made, xm.add(8))
                sp.dma_start(x_keep, XA).then_inc(x_out, 16)
                xout.add(16)

                def copy_batch(n, layer=layer):
                    s = bass.ds(n, 1)
                    for g in ((2,) if layer == 0 else (0, 1)):
                        r = ROWS[g]
                        store(a["oks"][g][s, :, :, 0:r - NS], a["kt"][g].rearrange("n p (j r) -> n p j r", j=4)[s, :, :, NS:r])
                        store(a["ovs"][g][s, 0:r - NS, :], a["v"][g][s, NS:r, :])
                    if layer == 1:
                        store(a["okc_s"][s, :, :, 0:ROWS_C - NS],
                              a["ktc"].rearrange("n p (j r) -> n p j r", j=2)[s, :, :, NS:ROWS_C])
                        store(a["ovc_s"][s, 0:ROWS_C - NS, :], a["vc"][s, NS:ROWS_C, :])

                n_copies = 16 * (2 if layer == 0 else 6)
                base = fed[0]
                with turns(sp, 7, {spl: 4, stored: n_copies}) as i:
                    for k in range(4):
                        feed(i * 4 + base + k)
                    copy_batch(i)
                fed[0] += 28
                copy_batch(7)
                feed_to(W_PLE[layer] + 3)
                sp.wait_ge(slot_done, W_PLE[layer])
                sp.wait_ge(x_out, xout.at)
                sp.dma_start(XD, x_keep).then_inc(x_in, 16)
                xin.add(16)
                xm.add(8)
                if layer == 0:
                    feed_to(W_GATE[0] + 7)
                    sp.wait_ge(x_made, xm.add(8))
                    sp.dma_start(x_keep, XA).then_inc(x_out, 16)
                    xout.add(16)
                    feed_to(W_VC + 4)
                    sp.wait_ge(slot_done, W_VC + 1)
                    sp.wait_ge(free[0], UNITS_AT[W_VC + 1] // 2)
                    sp.wait_ge(free[1], UNITS_AT[W_VC + 1] // 2)
                    store(a["okc_p"], KCT[:, :, PADS - ROWS_C:PADS])
                    store(a["ovc_p"], VC[:, 7, :])
                    store(a["okc_new"], KCT[:, :, 0:SAMPLE])
                    store(a["ovc_new"], VC[0:SAMPLE, 8, :])
                    sp.wait_ge(o_made, made.add(8))
                    sp.dma_start(ktc_sb[:, :].rearrange("p (n c) -> p n c", n=NB), a["ktc"].rearrange("n p c -> p n c")).then_inc(sx_in, 16)
                    sp.dma_start(vc_in[:, :].rearrange("p (n c) -> p n c", n=NB), a["vc"].rearrange("n p c -> p n c")).then_inc(sx_in, 16)
                    sp.dma_start(cm_sb[:, :], a["cmask"]).then_inc(sx_in, 16)
                    sp.wait_ge(out_done, stored.at)
                else:
                    feed_to(N_SLOTS)
                    sp.wait_ge(x_made, xm.add(8))
                    store(a["yT"], XA)
            sp.wait_ge(out_done, stored.at)
            sp.wait_ge(x_out, xout.at)
            sp.wait_ge(o_out, oout.at)
            sp.wait_ge(kept, keeps.at)

        @block.gpsimd
        def _(pool):
            raw, hi, done = Count(raw_in), Count(hi_made), Count(slot_done)

            def split_slot(b, wait_free=True):
                pool.wait_ge(raw_in, raw.add(16))
                if wait_free:
                    pool.wait_ge(slot_done, done.add())
                pool.tensor_tensor(w_hi[b][:, :], w_raw[:, :], ones[:, 0:1].broadcast_to([P, SLOT]), ALU.mult).then_inc(hi_made, 1)
                pool.wait_ge(hi_made, hi.add())
                pool.tensor_tensor(w_lo[b][:, :], w_raw[:, :], w_hi[b][:, :].bitcast(F32), ALU.subtract).then_inc(split, 1)

            pool.wait_ge(const_in, 64)
            split_slot(0, wait_free=False)
            split_slot(1, wait_free=False)
            with turns(pool, W_GLU // 2, {raw: 32, hi: 2, done: 2}):
                split_slot(0)
                split_slot(1)

            prod, xsm, hus, pown, sim = (Count(s) for s in (level_prod, xs_made, h_used, pool_own, si_made))

            def level(t, k):
                n = 1 << k
                pool.wait_ge(level_prod, prod.add())
                pool.tensor_tensor(tr[t][:, n:2 * n], tp[:, 0:n], tp[:, 512:512 + n], ALU.subtract)
                pool.tensor_tensor(ti[t][:, n:2 * n], tp[:, 1024:1024 + n], tp[:, 1536:1536 + n], ALU.add).then_inc(level_made, 1)

            def block_of(tables):
                for t in range(4):
                    S = si[t % 2]
                    pool.wait_ge(xs_made, xsm.add())
                    pool.wait_ge(h_used, hus.at if t < 2 else hus.add())
                    pool.tensor_tensor(S[:, :], xs1[:, :], ti[t][:, :], ALU.mult)
                    if t < tables:
                        level((t + 2) % 4, 6)
                    pool.wait_ge(si_made, sim.at)
                    sim.add()
                    pool.tensor_tensor(sj[:, :], xs2[:, :], tr[t][:, :], ALU.mult).then_inc(pool_own, 1)
                    if t < tables:
                        level((t + 2) % 4, 7)
                    pool.wait_ge(pool_own, pown.add())
                    pool.tensor_tensor(S[:, :], S[:, :], sj[:, :], ALU.add).then_inc(si_made, 1)
                    if t < tables:
                        level((t + 2) % 4, 8)
                    if t < tables:
                        level((t + 2) % 4, 9)
                hus.add(2)

            for t in range(2):
                for k in range(6, 10):
                    level(t, k)
            with turns(pool, 3, {prod: 16, xsm: 4, hus: 4, pown: 4, sim: 4}):
                block_of(4)
            block_of(2)

            with turns(pool, (N_SLOTS - W_GLU - 3) // 2, {raw: 32, hi: 2, done: 2}):
                split_slot(0)
                split_slot(1)
            split_slot(0)

        @block.tensor
        def _(pe):
            u, spl = Units(), Count(split)
            sqm, rms, lo = Count(sq_made), Count(sums_read), Count(lo_made)
            n_q, n_s, n_mask, n_exp, n_ptt, n_pt, n_pv, n_o = (
                Count(s) for s in (q_ready, s_mm, s_masked, exp_made, pt_taken, pt_mm, pv_mm, o_made))

            def sums():
                pe.wait_ge(free[0], u.free[0].at)
                for kc in range(KC):
                    pe.wait_ge(sq_made, sqm.add())
                    for c in range(3):
                        mm = pe.matmul(UNIT[0][:, c, :], ones[:, :], TMP[:, kc % 2, c * CH:(c + 1) * CH],
                                       start=kc == 0, stop=kc == KC - 1)
                    mm.then_inc(sq_used, 1)
                pe.wait_ge(sums_read, rms.add())

            def halves(slot, kcs):
                return [t[slot % 2][:, 0:2048].rearrange("p (k c) -> p k c", k=kcs) for t in (w_hi, w_lo)]

            def slot_ready():
                pe.wait_ge(split, spl.add())

            def features(slot, XH, XL, kcs=KC, n_units=2, done=1, arriving=False):
                WH, WL = halves(slot, kcs)
                for m in range(n_units):
                    cols = slice(m * P, m * P + P)
                    s = m % 2
                    if not (isinstance(u.free[s].at, int) and u.free[s].at == 0):
                        pe.wait_ge(free[s], u.free[s].at)
                    u.free[s].add()
                    for kc in range(kcs):
                        if arriving and m == 0:
                            pe.wait_ge(lo_made, lo.add())
                        for w, x in ((WH, XH), (WL, XH), (WH, XL)):
                            first, last = kc == 0 and w is WH and x is XH, kc == kcs - 1 and x is XL
                            for c in range(3):
                                mm = pe.matmul(UNIT[s][:, c, :], w[:, kc, cols], x[:, kc, c * CH:(c + 1) * CH],
                                               start=first, stop=last)
                    if m == n_units - 1:
                        mm.then_inc(slot_done, done)
                        u.done.add(done)
                    else:
                        mm.then_inc(full, 1)
                        u.full.add()

            def values(slot, g):
                WH, WL = halves(slot, KC)
                for n, tt in enumerate(((0, 1, 2), (3, 4, 5), (6, 7), (8,))):
                    s = n % 2
                    pe.wait_ge(free[s], u.free[s].at)
                    u.free[s].add()
                    for c, t in enumerate(tt):
                        pick = (lambda x: x[:, :, 0:P]) if t == 8 else prompt_cols(g, divmod(t, 2) if g == 1 else t)
                        XH, XL = pick(HH), pick(HL)
                        for kc in range(KC):
                            for x, w in ((XH, WH), (XH, WL), (XL, WH)):
                                mm = pe.matmul(psum[:, 3 * s + c, 0:256], x[:, kc], w[:, kc, :],
                                               start=kc == 0 and x is XH and w is WH, stop=kc == KC - 1 and x is XL)
                    if n == 3:
                        mm.then_inc(slot_done, 1)
                        u.done.add()
                    else:
                        mm.then_inc(full, 1)
                        u.full.add()

            def slot_pairs(n, first, XH, XL, arriving=False):
                if arriving:
                    for k in range(2):
                        slot_ready()
                        features(first + k, XH, XL, arriving=k == 0)
                    n -= 1
                with turns(pe, n, {spl: 2, **u.per(2, 2)}):
                    for k in range(2):
                        slot_ready()
                        features(first + k, XH, XL)

            def attend(g, heads, keys, vals):
                steps, per_kv = heads // 2, 1 if heads == H_A else 4
                staged = QST if heads == H_A else QCST

                def tile(i, nk):
                    K = key_cols(g, i, nk)(keys)
                    pe.wait_ge(q_ready, n_q.add())
                    base = n_mask.at

                    def scores(k):
                        m = n_mask.add()
                        if not (isinstance(m, int) and m <= 2):
                            pe.wait_ge(s_masked, m - 2)
                        for hh in range(2):
                            h = 2 * k + hh
                            kt = h // 2 if per_kv == 1 else h // 8
                            mm = pe.matmul(psum[:, k % 2, hh * 256:hh * 256 + nk * P], staged[:, h, :], K[:, kt],
                                           start=True, stop=True)
                        mm.then_inc(s_mm, 1)

                    def turn(k):
                        pe.wait_ge(exp_made, n_exp.add())
                        m = n_ptt.add()
                        if not (isinstance(m, int) and m <= 2):
                            pe.wait_ge(pt_taken, m - 2)
                        for hh in range(2):
                            for kb in range(nk):
                                o = (k % 2) * 512 + hh * 256 + kb * P
                                mm = pe.transpose(psum[:, 2 + k % 2, hh * 256 + kb * P:hh * 256 + kb * P + P],
                                                  pr[:, o:o + P], ident[:, :])
                        mm.then_inc(pt_mm, 1)

                    def weigh(k):
                        if k == 0:
                            m = n_o.add()
                            if not (isinstance(m, int) and m <= 1):
                                pe.wait_ge(o_made, m - 1)
                        pe.wait_ge(pt_taken, n_pv.add())
                        for hh in range(2):
                            h = 2 * k + hh
                            c = (h // per_kv) * HEAD_DIM
                            for kb in range(nk):
                                t = value_tile(g, i) - (nk - 1 - kb)
                                o = (k % 2) * 512 + hh * 256 + kb * P
                                mm = pe.matmul(psum[:, 4 + h // 8, (h % 8) * HEAD_DIM:(h % 8 + 1) * HEAD_DIM],
                                               pt[:, o:o + P], vals[:, bass.ds(t, 1), c:c + HEAD_DIM],
                                               start=kb == 0, stop=kb == nk - 1)
                        mm.then_inc(pv_mm, 1)

                    for k in range(steps + 2):
                        if k < steps:
                            scores(k)
                        if 1 <= k <= steps:
                            turn(k - 1)
                        if k >= 2:
                            weigh(k - 2)
                    if heads == H_C:
                        pe.wait_ge(o_made, n_o.at)
                        m = lo.at
                        pe.wait_ge(lo_made, m)
                        for k in range(KC):
                            mm = pe.transpose(psum[:, 6 + k // 4, (k % 4) * P:(k % 4 + 1) * P],
                                              on_c[:, k * P:(k + 1) * P], ident[:, :])
                        mm.then_inc(turned, 1)
                        lo.add()

                per = {n_q: 1, n_mask: steps, n_exp: steps, n_ptt: steps, n_pv: steps, n_o: 1}
                if heads == H_C:
                    per[lo] = 1
                over_tiles(pe, g, per, tile)
                pe.wait_ge(o_made, n_o.at)

            pe.wait_ge(const_in, 64)
            sums()
            for k in range(2):
                slot_ready()
                features(W_U + k, HH, HL, arriving=k == 0)
            for g in range(3):
                slot_pairs(2, W_QKV + 6 * g, HH, HL)
                for k in range(2):
                    slot_ready()
                    values(W_QKV + 6 * g + 4 + k, g)
                u.all_free(pe)
                attend(g, H_A, XA[:, 4:8, :], V)

            pe.wait_ge(sx_in, 48)
            pe.wait_ge(o_made, n_o.at)
            KSN, VSN = tiles(ks_new, 12), tiles(vs_new, 3)
            QB, PT = qb[:, :].rearrange("p (g c) -> p g c", g=3), tiles(sp_t, 12)
            qbm, kvi, ssm_, sse, stt_, spt_ = Count(qb_made), [Count(s) for s in kv_in], Count(ss_masked), Count(ss_norm), Count(st_taken), Count(spv_taken)
            with turns(pe, 4, {qbm: 2, kvi[0]: 16 * 12, kvi[1]: 16 * 12, ssm_: 1, sse: 1, stt_: 1, spt_: 1}):
                for b in range(2):
                    KT_ = kt_sb[b]
                    pe.wait_ge(qb_made, qbm.add())
                    pe.wait_ge(kv_in[b], kvi[b].add(16 * 12))
                    if b == 0:
                        pe.wait_ge(ss_masked, ssm_.add() - 1)
                    rows = slice(64 * b, 64 * b + 64)

                    def score(out, g, keys):
                        for j in range(4):
                            mm = pe.matmul(out, QB[:, g, j * 64:j * 64 + 64], keys[j], start=j == 0, stop=j == 3)
                        return mm

                    off = 0
                    for g in range(3):
                        kk = KT_[:, off:off + 4 * ROWS[g]].rearrange("p (j r) -> p j r", j=4)
                        off += 4 * ROWS[g]
                        if g == 2:
                            cached = [kk[:, j].rearrange("p (i s) -> p i s", s=16)[:, :, 0:8] for j in range(4)]
                        else:
                            cached = [kk[:, j, :] for j in range(4)]
                        score(psum[rows, g, 0:(P, 512, 512)[g]], g, cached)
                        mm = score(psum[rows, 0, P + 64 * g:P + 64 * g + 64], g, [KSN[:, 4 * g + j, :] for j in range(4)])
                    mm.then_inc(ss_mm, 1)
                pe.wait_ge(ss_norm, sse.add())
                pe.wait_ge(st_taken, stt_.add() - 1)
                for n in range(9):
                    o = 0 if n == 0 else 320 + (n - 1) * P
                    out = psum[:, 4 + n // 4, (n % 4) * P:(n % 4 + 1) * P] if n < 8 else psum[:, 3, 384:512]
                    pe.transpose(out, s_sb[:, o:o + P], ident[:, :])
                for g in range(3):
                    mm = pe.transpose(psum[0:64, 3, g * P:g * P + P], s_sb[:, P + 64 * g:P + 64 * g + 64], ident[:, :])
                mm.then_inc(st_mm, 1)
                pe.wait_ge(st_taken, stt_.at)
                pe.wait_ge(spv_taken, spt_.add() - 1)
                for b in range(2):
                    vb = tiles((va, v_sb)[b], 9)
                    for j in range(4):
                        out = psum[:, 6, b * 64 + j * 16:b * 64 + j * 16 + 16]
                        cols = slice(b * 64 + j * 16, b * 64 + j * 16 + 16)
                        for g in range(3):
                            pe.matmul(out, VSN[0:64, g, j * P:(j + 1) * P], PT[0:64, g, cols], start=g == 0, stop=False)
                        for n in range(9):
                            mm = pe.matmul(out, vb[:, n, j * P:(j + 1) * P], PT[:, 3 + n, cols], start=False, stop=n == 8)
                    mm.then_inc(kv_used, 1)

            pe.wait_ge(spv_taken, 4)
            bi, vd, ym, srm, sim, bus, hus = (Count(s) for s in (blk_in, vec_dve, y_made, sr_made, si_made, bu_used, h_used))
            def by_tile(t):
                return t[:, :].rearrange("p (t c s) -> p t c s", t=4, c=2)

            pe.wait_ge(b_in, 64)
            for b in range(4):
                B = by_tile((b_blk + c_blk)[b])
                for c in range(2):
                    for t in range(4):
                        mm = pe.matmul(psum[:, b, c * 256 + t * 64:c * 256 + t * 64 + 64], B[:, t, c, :],
                                       U[:, b:b + 1, 0:SAMPLE], start=True, stop=True)
            mm.then_inc(b_used, 1)
            HSR, HSI = tiles(hs_re, 16), tiles(hs_im, 16)
            with turns(pe, 2, {bi: 64, vd: 1, ym: 2, srm: 8, sim: 8, bus: 8}) as z:
                pe.wait_ge(blk_in, bi.add(64))

                def inputs(k):
                    b, t = divmod(k, 4)
                    pe.wait_ge(bu_used, bus.add())
                    for c in range(2):
                        for n in range(2):
                            mm = pe.matmul(psum[:, 2 * c + n, :], by_tile(b_blk[b])[:, t, c, :],
                                           U[:, bass.ds(z * 2 + b, 1), SAMPLE + n * 512:SAMPLE + n * 512 + 512],
                                           start=True, stop=True)
                    mm.then_inc(bu_mm, 1)

                def outputs(k):
                    b, t = divmod(k, 4)
                    if t == 0:
                        pe.wait_ge(y_made, ym.at)
                        ym.add()
                    pe.wait_ge(sr_made, srm.add())
                    pe.wait_ge(si_made, sim.add())
                    for n in range(2):
                        for c, H in ((0, sr[t % 2]), (1, si[t % 2])):
                            mm = pe.matmul(psum[:, 4 + n, :], by_tile(c_blk[b])[:, t, c, :], H[:, n * 512:n * 512 + 512],
                                           start=t == 0 and c == 0, stop=t == 3 and c == 1, skip_group_check=True)
                    mm.then_inc(h_used, 1)

                inputs(0)
                pe.wait_ge(hs_made, 1)
                pe.wait_ge(y_made, ym.at)
                for b in range(2):
                    for t in range(4):
                        for c, H in ((0, HSR), (1, HSI)):
                            mm = pe.matmul(psum[:, 6, b * SAMPLE:(b + 1) * SAMPLE], by_tile(c_blk[b])[:, t, c, :],
                                           H[:, bass.ds(z * 8 + b * 4 + t, 1), :],
                                           start=t == 0 and c == 0, stop=t == 3 and c == 1)
                mm.then_inc(ys_mm, 1)
                inputs(1)
                pe.wait_ge(vec_dve, vd.add())
                for k in range(8):
                    if k < 6:
                        inputs(k + 2)
                    outputs(k)

            pe.wait_ge(lo_made, lo.add(4))
            slot_ready()
            features(W_GLU, ZH, ZL, kcs=4, n_units=4)
            lo.add(4)

            cmb = Count(comb_made)
            lo.add()
            with turns(pe, 4, {cmb: 2, lo: 2}):
                for b in range(2):
                    pe.wait_ge(comb_made, cmb.add())
                    m = lo.add()
                    pe.wait_ge(lo_made, m - 2)
                    for k in range(4):
                        mm = pe.transpose(psum[:, 6 + b, k * P:k * P + P], c_acc[:, b * 512 + k * P:b * 512 + k * P + P],
                                          ident[:, :])
                    mm.then_inc(turned, 1)

            for layer in range(2):
                if layer == 1:
                    slot_pairs(2, W_QC, HH, HL, arriving=True)
                    slot_ready()
                    features(W_KC, HH, HL)
                    slot_ready()
                    values(W_VC, 0)
                    u.all_free(pe)
                    attend(0, H_C, KCT, VC)
                    pe.wait_ge(sx_in, 48 + 48)
                    pe.wait_ge(qb_made, 9)
                    QS = qc_st[:, :].rearrange("p (n j c) -> p n j c", n=NB, j=2)
                    KS, VS = ktc_sb[:, :].rearrange("p (n j r) -> p n j r", n=NB, j=2), tiles(vc_in, NB)
                    for n in range(NB):
                        o = (n % 2) * SKC
                        for out, keys in ((psum[:, n // 2, o:o + P], [KS[:, n, j] for j in range(2)]),
                                          (psum[:, n // 2, o + P:o + SKC], [KCT[:, j, 0:SAMPLE] for j in range(2)])):
                            for j in range(2):
                                mm = pe.matmul(out, QS[:, n, j, :], keys[j], start=j == 0, stop=j == 1)
                    mm.then_inc(ss_mm, 1)
                    pe.wait_ge(ss_norm, 5)
                    pe.wait_ge(lo_made, lo.at)
                    S, PTC = tiles(cs_s, NB), tiles(cs_t, 16)
                    for n in range(NB):
                        pe.transpose(psum[:, 4 + n // 4, (n % 4) * P:(n % 4 + 1) * P], S[:, n, 0:P], ident[:, :])
                        mm = pe.transpose(psum[0:64, 6 + n // 4, (n % 4) * P:(n % 4 + 1) * P], S[:, n, P:SKC], ident[:, :])
                    mm.then_inc(st_mm, 1)
                    pe.wait_ge(st_taken, 5)
                    for n in range(NB):
                        for j in range(2):
                            out = psum[:, n // 4, (n % 4) * P + j * 64:(n % 4) * P + j * 64 + 64]
                            pe.matmul(out, VS[:, n, j * P:j * P + P], PTC[:, n, j * 64:j * 64 + 64], start=True, stop=False)
                            mm = pe.matmul(out, VC[0:SAMPLE, 8, j * P:j * P + P], PTC[0:64, 8 + n, j * 64:j * 64 + 64],
                                           start=False, stop=True)
                    mm.then_inc(spv_mm, 1)
                    lo.add()
                pe.wait_ge(lo_made, lo.at)
                slot_pairs(2, W_OUT[layer], HH, HL)
                sums()
                sums()
                up = W_FF[layer]

                def ff_up(slot, arriving=False):
                    slot_ready()
                    features(slot, HH, HL, arriving=arriving)
                    lo.add(2)

                def ff_down(slot, h):
                    slot_ready()
                    pe.wait_ge(lo_made, lo.at - (0 if slot == up + 31 else 2))
                    features(slot, HIDH[h], HIDL[h], kcs=2, n_units=8)

                ff_up(up, arriving=True)
                with turns(pe, 7, {spl: 4, lo: 4, **u.per(2, 8, 2, 8)}):
                    ff_up(up + 1)
                    ff_down(up + 2, 0)
                    ff_up(up + 3)
                    ff_down(up + 4, 1)
                ff_up(up + 29)
                ff_down(up + 30, 0)
                ff_down(up + 31, 1)
                sums()
                slot_ready()
                slot_ready()
                s = W_PLE[layer] % 2
                PH, PL = (t[s][:, :].rearrange("p (k c) -> p k c", k=2) for t in (w_hi, w_lo))
                features(W_PLE[layer] + 1, PH, PL, kcs=2, n_units=8, done=2)
                sums()
                slot_pairs(2, W_GATE[layer], HH, HL, arriving=True)
                if layer == 0:
                    sums()

        OUT_G = (64, 64 + 112, 64 + 112 + 176)
        OUT_S5 = OUT_G[2] + 32


        @block.scalar
        def _(act):
            u, squ, lo, scl, rd = Units(), Count(sq_used), Count(lo_made), Count(scaled), Count(sums_read)
            xm, own = Count(x_made), Count(act_own)
            n_s, n_max, n_ptx, n_pt, n_pv, n_o, n_sc = (Count(s) for s in (s_mm, max_made, pt_mm, pt_mm, pv_mm, o_made, w_dif))
            n_turn, n_out = Count(turned), Count(o_out)

            def late(sem_, value):
                if not (isinstance(value, int) and value <= 0):
                    act.wait_ge(sem_, value)

            def squares(ready):
                for kc in range(KC):
                    ready(kc)
                    late(sq_used, squ.add() - 2)
                    act.activation(TMP[:, kc % 2, :], XA[:, kc, :], ACT.Square).then_inc(sq_made, 1)
                act.wait_ge(sq_used, squ.at)
                act.activation(chunked(rs[:, :]), UNIT[0], ACT.Ln, bias=param[:, C_EPS:C_EPS + 1],
                               scale=1.0 / D_MODEL).then_inc(sums_read, 1)
                act.wait_ge(sums_read, rd.add())
                act.activation(rs[:, :], rs[:, :], ACT.Exp, scale=-0.5).then_inc(inv_made, 1)

            def high(dst, src, ready, n):
                act.wait_ge(ready, n)
                act.activation(dst, src, ACT.Copy).then_inc(hi_act, 1)

            def norm_highs():
                for kc in range(KC):
                    high(HH[:, kc, :], TMP[:, kc % 2, :], scaled, scl.add())
                lo.add(8)

            def take(dst, m, last, func=ACT.Copy, **kw):
                u.wait(act, last)
                act.activation(chunked(dst), UNIT[m % 2], func, **kw).then_inc(free[m % 2], 1)
                u.free[m % 2].add()

            def take_pairs(n, buf, first=0):
                with turns(act, n, u.per(2, 2)) as i:
                    for k in range(4):
                        take(buf[:, bass.ds(i * 4 + k + first, 1), :].rearrange("p a t -> p (a t)"), k, k % 2 == 1)

            def take_values(buf, cols):
                for n, (t, k) in enumerate(((0, 3), (3, 3), (6, 2), (8, 1))):
                    rows = slice(0, SAMPLE) if n == 3 else slice(0, P)
                    u.wait(act, n == 3)
                    s = n % 2
                    act.activation(buf[rows, t:t + k, cols], psum[rows, 3 * s:3 * s + k, 0:256], ACT.Copy).then_inc(free[s], 1)
                    u.free[s].add()

            def attend(g, heads):
                steps = heads // 2
                src = XA if heads == H_C else XA[:, 0:4, :]

                def tile(i, nk):
                    late(s_mm, n_s.at)
                    n_s.add(steps)
                    for par in range(2):
                        rows = slice(64 * par, 64 * par + 64)
                        if heads == H_A:
                            q = prompt_cols(g, i)(src)[rows]
                            out = QST.rearrange("p (j h) c -> p h j c", h=2)[rows, par]
                            mm = act.activation(out, q, ACT.Copy, scale=HEAD_DIM ** -0.5)
                        else:
                            for o in range(2):
                                q = prompt_cols(g, i)(src)[rows].rearrange("p (k o y) c -> p k o y c", k=2, o=2)[:, :, o]
                                out = QCST.rearrange("p (k o y h) c -> p k o y h c", k=2, o=2, y=2)[64 * o:64 * o + 64, :, o, :, par]
                                mm = act.activation(out, q, ACT.Copy, scale=HEAD_DIM ** -0.5)
                    mm.then_inc(q_ready, 1)
                    late(o_made, n_o.at)
                    n_o.add()

                    def exps(k):
                        act.wait_ge(max_made, n_max.add())
                        late(pt_mm, n_ptx.add() - 2)
                        for hh in range(2):
                            h = 2 * k + hh
                            o = (k % 2) * 512 + hh * 256
                            mm = act.activation(pr[:, o:o + nk * P], sm[:, o:o + nk * P], ACT.Exp, bias=stat[:, h:h + 1],
                                                accum_out=stat[:, 16 + h:17 + h])
                        mm.then_inc(exp_made, 1)

                    def turned_out(k):
                        act.wait_ge(pt_mm, n_pt.add())
                        late(pv_mm, n_pv.add() - 2)
                        o = (k % 2) * 512
                        act.activation(pt[:, o:o + 512].rearrange("p (h c) -> p h c", h=2)[:, :, 0:nk * P],
                                       psum[:, 2 + k % 2, :].rearrange("p (h c) -> p h c", h=2)[:, :, 0:nk * P],
                                       ACT.Copy).then_inc(pt_taken, 1)

                    exps(0)
                    for k in range(steps):
                        if k + 1 < steps:
                            exps(k + 1)
                        turned_out(k)
                    if heads == H_C:
                        act.wait_ge(w_dif, n_sc.add())
                        act.activation(stat[:, 48:64], stat[:, 32:48], ACT.Exp).then_inc(w_exp, 1)
                        high(HH[:, :, bass.ds(i * P + SAMPLE, P)],
                             psum[:, 6:8, :].rearrange("p b (k c) -> p (b k) c", c=P), turned, n_turn.add())

                per = {n_s: steps, n_o: 1, n_max: steps, n_ptx: steps, n_pt: steps, n_pv: steps}
                if heads == H_C:
                    per |= {n_sc: 1, n_turn: 1}
                over_tiles(act, g, per, tile)

            act.wait_ge(const_in, 64)
            squares(lambda kc: act.wait_ge(x_in, 16))
            norm_highs()
            for m in range(4):
                take(U[:, m, :], m, m % 2 == 1)
            act.wait_ge(lo_made, lo.at)
            act.wait_ge(zeroed, 1)
            for g in range(3):
                if g:
                    act.wait_ge(out_done, OUT_G[g - 1])
                    act.wait_ge(kept, 32 * g)
                take_pairs(2, XA)
                for k in range(2):
                    take_values(V, slice(256 * k, 256 * k + 256))
                u.all_free(act)
                attend(g, H_A)

            smx, stm, kvu = Count(ss_max), Count(st_mm), Count(kv_used)
            PT = tiles(sp_t, 12)
            with turns(act, 4, {smx: 1, stm: 1, kvu: 2}):
                act.wait_ge(ss_max, smx.add())
                act.activation(s_sb[:, :], s_sb[:, :], ACT.Exp, bias=sstat[:, 0:1], accum_out=sstat[:, 1:2]).then_inc(ss_exp, 1)
                act.wait_ge(st_mm, stm.add())
                act.wait_ge(kv_used, kvu.at)
                kvu.add(2)
                act.activation(PT[0:64, 0:3, :], psum[0:64, 3, 0:384].rearrange("p (g c) -> p g c", g=3), ACT.Copy)
                act.activation(PT[:, 3:11, :], psum[:, 4:6, :].rearrange("p b (n c) -> p (b n) c", c=P), ACT.Copy)
                act.activation(PT[:, 11, :], psum[:, 3, 384:512], ACT.Copy).then_inc(st_taken, 1)

            def vec(v):
                return sc[:, v * ST:(v + 1) * ST]

            act.wait_ge(ssm_in, 32)
            act.activation(vec(V_DT), vec(V_DT), ACT.Exp).then_inc(vec_act, 1)
            act.wait_ge(vec_arg, 1)
            act.activation(vec(V_R), vec(V_X), ACT.Exp)
            act.activation(vec(V_SIN), vec(V_K), ACT.Sin)
            act.activation(vec(V_COS), vec(V_COS), ACT.Sin).then_inc(vec_act, 1)

            BT, TP = bt[:, :].rearrange("p (c t l) -> p c t l", c=2, t=ST), tiles(tp, 4)
            SC = tiles(sc, N_VEC)
            srm, sim, lev = (Count(s) for s in (sr_made, si_made, level_made))

            def table(n, t):
                R_, I_ = tr[t], ti[t]
                act.activation(R_[:, 0:64], BT[:, 0, bass.ds(n, 1), :].rearrange("p a l -> p (a l)"), ACT.Copy)
                act.activation(I_[:, 0:64], BT[:, 1, bass.ds(n, 1), :].rearrange("p a l -> p (a l)"), ACT.Copy)\
                    .then_inc(act_own, 1)
                act.wait_ge(act_own, own.add())
                for k in range(6, 10):
                    m = 1 << k
                    act.wait_ge(level_made, lev.at)
                    lev.add()
                    wr, wi = SC[:, V_POW + 2 * k, bass.ds(n, 1)], SC[:, V_POW + 2 * k + 1, bass.ds(n, 1)]
                    for q, (src, w) in enumerate(((R_, wr), (I_, wi), (I_, wr), (R_, wi))):
                        mm = act.activation(TP[:, q, 0:m], src[:, 0:m], ACT.Copy, scale=w)
                    mm.then_inc(level_prod, 1)

            act.wait_ge(powers_made, 1)
            table(0, 0)
            table(1, 1)
            table(2, 2)
            table(3, 3)
            with turns(act, 3, {srm: 4, sim: 4, lev: 16, own: 4}) as b:
                for t in range(4):
                    act.wait_ge(sr_made, srm.add())
                    act.wait_ge(si_made, sim.add())
                    table(b * 4 + 4 + t, t)
            act.wait_ge(y_made, 4)
            act.wait_ge(zeroed, 2)
            for m in range(4):
                act.activation(ZB[:, m, :], ZB[:, m, :], ACT.Gelu_apprx_tanh).then_inc(act_own, 1)
                high(ZH[:, m, :], ZB[:, m, :], act_own, own.add())
            lo.add(4)
            act.wait_ge(out_done, OUT_S5)
            for m in range(4):
                act.wait_ge(lo_made, lo.at - (1 if m < 2 else 0) + (m - 2 if m >= 2 else 0))
                if m >= 2:
                    act.wait_ge(lo_made, lo.at + m - 1)
                take(TMP[:, m % 2, :], m, m == 3, ACT.Sigmoid, bias=param[:, C_GLU + m:C_GLU + m + 1])
                if m:
                    high(HH[:, 3 + m, :], TMP[:, (m - 1) % 2, :], scaled, scl.add())
            high(HH[:, 7, :], TMP[:, 1, :], scaled, scl.add())
            lo.add(4)

            high(HH[:, 0:4, 0:SAMPLE], tiles(oas, 4), spv_taken, 4)
            lo.add()
            with turns(act, 4, {n_sc: 2, n_turn: 2}) as t:
                for b in range(2):
                    act.wait_ge(w_dif, n_sc.add())
                    act.activation(c_w[:, b * 64 + 32:b * 64 + 56], c_w[:, b * 64 + 8:b * 64 + 32], ACT.Exp).then_inc(w_exp, 1)
                    high(HH[:, 0:4, bass.ds(t * 256 + SAMPLE + P * b, P)],
                         psum[:, 6 + b, :].rearrange("p (k c) -> p k c", c=P), turned, n_turn.add())
            lo.add(8)

            for layer in range(2):
                if layer == 1:
                    act.wait_ge(x_out, 32)
                    take_pairs(2, XA)
                    for m in range(2):
                        take(KCT[:, m, :], m, m == 1)
                    take_values(VC, slice(0, 256))
                    u.all_free(act)
                    act.wait_ge(zeroed, 3)
                    attend(0, H_C)
                    lo.add(8)
                    for n in range(NB):
                        act.wait_ge(ss_max, 5)
                        mm = act.activation(tiles(cs_s, NB)[:, n, :], tiles(cs_s, NB)[:, n, :], ACT.Exp,
                                            bias=cstat[:, n:n + 1], accum_out=cstat[:, 8 + n:9 + n])
                    act.activation(cstat[:, 16:24], cstat[:, 0:8], ACT.Exp,
                                   bias=param[:, C_SINKROW:C_SINKROW + 1]).then_inc(ss_exp, 1)
                    act.wait_ge(st_mm, 5)
                    PTC = tiles(cs_t, 16)
                    act.activation(PTC[:, 0:8, :], psum[:, 4:6, :].rearrange("p b (n c) -> p (b n) c", c=P), ACT.Copy)
                    act.activation(PTC[0:64, 8:16, :], psum[0:64, 6:8, :].rearrange("p b (n c) -> p (b n) c", c=P),
                                   ACT.Copy).then_inc(st_taken, 1)
                    high(HH[:, :, 0:SAMPLE], tiles(ocs, 8), spv_taken, 5)
                    lo.add()
                act.wait_ge(lo_made, lo.at)
                take_pairs(2, XA)

                def ready_r(kc):
                    act.wait_ge(free[kc % 2], u.free[kc % 2].at - 3 + kc // 2)

                def ready_x(kc):
                    act.wait_ge(x_made, xm.add())

                squares(ready_r)
                squares(ready_x)
                norm_highs()

                def ff_up(h):
                    for m in range(2):
                        act.wait_ge(lo_made, lo.at - 1 + m)
                        take(TMP[:, m, :], m, m == 1, ACT.Relu)
                    for m in range(2):
                        high(HIDH[h][:, m, :], TMP[:, m, :], scaled, scl.add())
                    lo.add(2)

                ff_up(0)
                with turns(act, 7, {lo: 4, scl: 4, **u.per(2, 8, 2, 8)}):
                    ff_up(1)
                    u.skip(8)
                    ff_up(0)
                    u.skip(8)
                ff_up(1)
                u.skip(8, 8)
                act.wait_ge(lo_made, lo.at)
                squares(ready_r)
                for m in range(8):
                    act.wait_ge(x_made, xm.at + m + 1)
                    if m < 7:
                        take(XD[:, m, :], m, m == 6 and False)
                    else:
                        u.done.add(1)
                        take(XD[:, m, :], m, True)
                squares(ready_x)
                norm_highs()
                act.wait_ge(lo_made, lo.at)
                for m in range(8):
                    if m >= 2:
                        act.wait_ge(x_made, xm.at + m - 1)
                    take(TMP[:, m % 2, :], m, m % 2 == 1, ACT.Sigmoid)
                if layer == 0:
                    act.wait_ge(x_made, xm.at + 8)
                    squares(ready_x)
                    norm_highs()

        @block.vector
        def _(dve):
            u, lo, hi, inv_, own = Units(), Count(lo_made), Count(hi_act), Count(inv_made), Count(dve_own)
            xin = Count(x_in)
            xin.add(16)
            n_s, n_exp, n_pv, n_out, n_we, n_turn = (Count(s) for s in (s_mm, exp_made, pv_mm, o_out, w_exp, turned))

            def step(ins):
                ins.then_inc(dve_own, 1)
                dve.wait_ge(dve_own, own.add())

            def late(sem_, value):
                if not (isinstance(value, int) and value <= 0):
                    dve.wait_ge(sem_, value)

            def copy(dst, src):
                return dve.tensor_scalar(dst, src, 1.0, None, ALU.mult)

            def low(dst, src, high_):
                dve.wait_ge(hi_act, hi.add())
                dve.tensor_tensor(dst, src, high_.bitcast(F32), ALU.subtract).then_inc(lo_made, 1)
                lo.add()

            def inverse():
                dve.wait_ge(inv_made, inv_.add())

            def normalise(layer, kind):
                inverse()
                first = lo.at
                for kc in range(KC + 1):
                    if kc < KC:
                        if kc >= 2:
                            dve.wait_ge(lo_made, first + kc - 1)
                        dve.scalar_tensor_tensor(TMP[:, kc % 2, :], XA[:, kc, :], G[:, layer, kind, kc:kc + 1], rs[:, :],
                                                 ALU.mult, ALU.mult).then_inc(scaled, 1)
                    if kc:
                        low(HL[:, kc - 1, :], TMP[:, (kc - 1) % 2, :], HH[:, kc - 1, :])

            def residual(layer, kind):
                inverse()
                dve.wait_ge(x_in, xin.add(16))
                for kc in range(KC + 1):
                    if kc < KC:
                        dve.scalar_tensor_tensor(XA[:, kc, :], XA[:, kc, :], G[:, layer, kind, kc:kc + 1], rs[:, :],
                                                 ALU.mult, ALU.mult).then_inc(dve_own, 1)
                        own.add()
                    if kc:
                        dve.wait_ge(dve_own, own.at - (1 if kc < KC else 0))
                        dve.tensor_tensor(XA[:, kc - 1, :], XA[:, kc - 1, :], XD[:, kc - 1, :], ALU.add).then_inc(x_made, 1)

            def attend(g, heads):
                steps = heads // 2

                def tile(i, nk):
                    for k in range(steps):
                        dve.wait_ge(s_mm, n_s.add())
                        late(exp_made, n_exp.add() - 2)
                        out = sm[:, (k % 2) * 512:(k % 2) * 512 + 512].rearrange("p (h c) -> p h c", h=2)[:, :, 0:nk * P]
                        m = mask[:, 2 * P:3 * P] if g == 2 else mask[:, 2 * P - nk * P:2 * P]
                        if k == 0:
                            late(o_out if heads == H_A else o_made, n_out.at if heads == H_A else n_om.at)
                        dve.tensor_tensor(out, psum[:, k % 2, :].rearrange("p (h c) -> p h c", h=2)[:, :, 0:nk * P],
                                          m.unsqueeze(1).broadcast_to([P, 2, nk * P]), ALU.add).then_inc(s_masked, 1)
                        dve.wait_ge(s_masked, n_mk.add())
                        red = dve.tensor_reduce(stat[:, 2 * k:2 * k + 2], out, AX, ALU.max, negate=True)
                        if heads == H_C:
                            step(red)
                            red = dve.tensor_tensor(stat[:, 2 * k:2 * k + 2], stat[:, 2 * k:2 * k + 2],
                                                    nsink[:, 2 * k:2 * k + 2], ALU.min)
                        red.then_inc(max_made, 1)
                    dve.wait_ge(exp_made, n_exp.at)
                    sums_ = stat[:, 16:16 + heads]
                    if heads == H_C:
                        dve.wait_ge(max_made, n_s.at - 0 * steps)
                        dve.tensor_tensor(stat[:, 32:48], param[:, C_SINK:C_SINK + 16], stat[:, 0:16], ALU.add).then_inc(w_dif, 1)
                        dve.wait_ge(w_exp, n_we.add())
                        step(dve.tensor_tensor(sums_, sums_, stat[:, 48:64], ALU.add))
                    step(dve.reciprocal(stat[:, 64:64 + heads], sums_))
                    dve.wait_ge(pv_mm, n_pv.add(steps))
                    inv = stat[:, 64:64 + heads].unsqueeze(2).broadcast_to([P, heads, HEAD_DIM])
                    if heads == H_A:
                        dve.tensor_copy(o_st[:, 512:520], sums_)
                        dve.tensor_copy(o_st[:, 520:528], stat[:, 0:8])
                        dve.tensor_tensor(o_st[:, 0:512].rearrange("p (h d) -> p h d", h=8),
                                          psum[:, 4, :].rearrange("p (h d) -> p h d", h=8), inv, ALU.mult).then_inc(o_made, 1)
                        n_out.add(16)
                        n_om.add()
                    else:
                        late(turned, n_turn.at)
                        dve.tensor_tensor(on_c[:, :].rearrange("p (h d) -> p h d", h=16),
                                          psum[:, 4:6, :].rearrange("p b (h d) -> p (b h) d", h=8), inv, ALU.mult)\
                            .then_inc(o_made, 1)
                        n_turn.add()
                        n_om.add()
                        low(HL[:, :, bass.ds(i * P + SAMPLE, P)], psum[:, 6:8, :].rearrange("p b (k c) -> p (b k) c", c=P),
                            HH[:, :, bass.ds(i * P + SAMPLE, P)])

                per = {n_s: steps, n_exp: steps, n_mk: steps, n_pv: steps, n_om: 1}
                if heads == H_A:
                    per[n_out] = 16
                else:
                    per |= {own: steps + 2, n_we: 1, n_turn: 1, hi: 1, lo: 1}
                if heads == H_A:
                    per[own] = 1
                over_tiles(dve, g, per, tile)

            n_mk, n_om = Count(s_masked), Count(o_made)

            dve.wait_ge(const_in, 64)
            dve.tensor_scalar(nsink[:, :], param[:, C_SINK:C_SINK + 17], -1.0, None, ALU.mult)
            normalise(0, 0)
            dve.wait_ge(lo_made, lo.at)
            dve.memset(QST, 0.0).then_inc(zeroed, 1)
            u.skip(2, 2)
            for g in range(3):
                u.skip(2, 2, 2, 2, 4, 4)
                attend(g, H_A)

            kvi, mi, ssm_, sse, spv, stt_ = (Count(ss_mm), Count(mask_in), Count(ss_mm), Count(ss_exp), Count(kv_used), Count(st_mm))
            QSF, QB = qs[:, :].rearrange("p (g j t) -> p g j t", g=3, j=4), qb[:, :].rearrange("p (g c) -> p g c", g=3)
            dve.wait_ge(sx_in, 48)
            dve.wait_ge(pv_mm, N_A_STEPS)
            step(dve.memset(qb[:, :], 0.0))
            OAS = tiles(oas, 4)
            with turns(dve, 4, {ssm_: 2, mi: 16, own: 3, sse: 1, spv: 2, stt_: 1}) as z:
                for b in range(2):
                    late(ss_mm, ssm_.at)
                    if b == 0:
                        pass
                    for par in range(2):
                        rows = slice(64 * par, 64 * par + 64)
                        out = QB[rows].rearrange("p g (j c) -> p g j c", c=80)[:, :, :, 8 * par:8 * par + 8]
                        ins = dve.tensor_scalar(out, QSF[rows, :, :, bass.ds(z * 16 + b * 8, 8)], HEAD_DIM ** -0.5, None, ALU.mult)
                    ins.then_inc(qb_made, 1)
                    ssm_.add()
                dve.wait_ge(ss_mm, ssm_.at)
                dve.wait_ge(mask_in, mi.add(16))
                dve.wait_ge(st_mm, stt_.at)
                stt_.add()
                dve.tensor_tensor(s_sb[:, 0:320], psum[:, 0, 0:320], sm_sb[:, 0:320], ALU.add)
                dve.tensor_tensor(s_sb[:, 320:SK].rearrange("p (b c) -> p b c", b=2), psum[:, 1:3, :],
                                  sm_sb[:, 320:SK].rearrange("p (b c) -> p b c", b=2), ALU.add).then_inc(ss_masked, 1)
                step(dve.tensor_copy(sstat[:, 4:5], nsink[:, 0:1]))
                dve.tensor_reduce(sstat[:, 0:1], s_sb[:, :], AX, ALU.max, negate=True).then_inc(ss_max, 1)
                dve.wait_ge(ss_exp, sse.add())
                step(dve.reciprocal(sstat[:, 2:3], sstat[:, 1:2]))
                dve.tensor_scalar(s_sb[:, :], s_sb[:, :], sstat[:, 2:3], None, ALU.mult).then_inc(ss_norm, 1)
                dve.wait_ge(kv_used, spv.add(2))
                for par in range(2):
                    rows = slice(64 * par, 64 * par + 64)
                    src = psum[rows, 6, 0:128].rearrange("p (b j c) -> p b j c", b=2, j=4)[:, :, :, 8 * par:8 * par + 8]
                    out = OAS[rows, :, bass.ds(z * 16, 16)].rearrange("p j (b q) -> p b j q", b=2)
                    ins = copy(out, src)
                    if par == 0:
                        step(ins)
                ins.then_inc(spv_taken, 1)

            def vec(v, n=1):
                return sc[:, v * ST:(v + n) * ST]

            def vv(out, x, y, op):
                step(dve.tensor_tensor(vec(out), vec(x), vec(y), op))

            def vs(out, x, s1, op0, s2=None, op1=None):
                step(dve.tensor_scalar(vec(out), vec(x), s1, s2, op0, op1) if op1 else
                     dve.tensor_scalar(vec(out), vec(x), s1, None, op0))

            PI, ROUND = 3.1415925, 12582912.0
            dve.wait_ge(ssm_in, 32)
            dve.wait_ge(vec_act, 1)
            vv(V_X, V_ARE, V_DT, ALU.mult)
            vv(V_TH, V_AIM, V_DT, ALU.mult)
            vs(V_T1, V_TH, 1 / 6.283185307179586, ALU.mult)
            vs(V_T1, V_T1, ROUND, ALU.add)
            vs(V_T1, V_T1, -ROUND, ALU.add)
            step(dve.scalar_tensor_tensor(vec(V_K), vec(V_T1), -6.28125, vec(V_TH), ALU.mult, ALU.add))
            step(dve.scalar_tensor_tensor(vec(V_K), vec(V_T1), -1.9353071795864769e-3, vec(V_K), ALU.mult, ALU.add))
            vs(V_COS, V_K, 1.5707963267948966, ALU.add)
            vs(V_T1, V_COS, PI, ALU.is_gt)
            step(dve.scalar_tensor_tensor(vec(V_COS), vec(V_T1), -6.283185307179586, vec(V_COS), ALU.mult, ALU.add))
            vs(V_COS, V_COS, -PI, ALU.max, PI, ALU.min)
            step(dve.tensor_scalar(vec(V_K), vec(V_K), -PI, PI, ALU.max, ALU.min))
            dve.tensor_copy(vec(V_T3), vec(V_K)).then_inc(vec_arg, 1)
            dve.wait_ge(vec_act, 2)
            vv(V_ABR, V_R, V_COS, ALU.mult)
            vv(V_ABI, V_R, V_SIN, ALU.mult)
            vv(V_T1, V_ARE, V_ARE, ALU.mult)
            vv(V_T2, V_AIM, V_AIM, ALU.mult)
            vv(V_T1, V_T1, V_T2, ALU.add)
            step(dve.reciprocal(vec(V_T1), vec(V_T1)))
            vs(V_T2, V_ABR, -1.0, ALU.add)
            vv(V_CR, V_T2, V_ARE, ALU.mult)
            vv(V_T3, V_ABI, V_AIM, ALU.mult)
            vv(V_CR, V_CR, V_T3, ALU.add)
            vv(V_CR, V_CR, V_T1, ALU.mult)
            vv(V_CI, V_ABI, V_ARE, ALU.mult)
            vv(V_T3, V_T2, V_AIM, ALU.mult)
            vv(V_CI, V_CI, V_T3, ALU.subtract)
            vv(V_CI, V_CI, V_T1, ALU.mult)
            step(dve.tensor_copy(vec(V_POW), vec(V_COS)))
            step(dve.tensor_copy(vec(V_POW + 1), vec(V_SIN)))
            for k in range(10):
                w = V_POW + 2 * k
                if k:
                    vv(V_T1, w - 2, w - 2, ALU.mult)
                    vv(V_T2, w - 1, w - 1, ALU.mult)
                    vv(w, V_T1, V_T2, ALU.subtract)
                    vv(w + 1, w - 2, w - 1, ALU.mult)
                    vs(w + 1, w + 1, 2.0, ALU.mult)
                vv(V_T1, w, w, ALU.mult)
                vv(V_T2, w + 1, w + 1, ALU.mult)
                vv(V_T1, V_T1, V_T2, ALU.add)
                vs(V_T1, V_T1, -0.5, ALU.mult, 1.5, ALU.add)
                vv(w, w, V_T1, ALU.mult)
                vv(w + 1, w + 1, V_T1, ALU.mult)

            SC = tiles(sc, N_VEC)
            SC4 = SC.rearrange("p v (b t) -> p v b t", b=4)
            HS4 = [t[:, :].rearrange("p (b t n) -> p b t n", b=4, t=4) for t in (hs_re, hs_im)]
            HF = [t[:, :].rearrange("p (tn s) -> p tn s", s=NS) for t in (hs_re, hs_im)]
            BT = bt[:, :].rearrange("p (c t l) -> p c t l", c=2, t=ST)

            def tt(out, x, y, op):
                step(dve.tensor_tensor(out, x, y, op))

            def wide(v, n):
                return SC[:, v, :].unsqueeze(2).broadcast_to([P, ST, n])

            def wide4(v):
                return SC4[:, v].unsqueeze(3).broadcast_to([P, 4, 4, SAMPLE])

            def x16(t, n):
                return t[:, 0:ST * n].rearrange("p (t n) -> p t n", t=ST)

            dve.wait_ge(b_used, 1)
            br, bi_ = (psum[:, 0:4, 256 * c:256 * c + 256].rearrange("p b (t n) -> p b t n", t=4) for c in range(2))
            x1, x2 = (t[:, :].rearrange("p (b t n) -> p b t n", b=4, t=4) for t in (xt1, xt2))
            tt(x1, br, wide4(V_CR), ALU.mult)
            tt(x2, bi_, wide4(V_CI), ALU.mult)
            tt(HS4[0], x1, x2, ALU.subtract)
            tt(x1, br, wide4(V_CI), ALU.mult)
            dve.tensor_tensor(x2, bi_, wide4(V_CR), ALU.mult).then_inc(bu_used, 1)
            dve.wait_ge(bu_used, 1)
            tt(HS4[1], x1, x2, ALU.add)
            tt(x16(gr, NB), wide(V_ABR, NB), wide(V_ABR, NB), ALU.max)
            tt(x16(gi, NB), wide(V_ABI, NB), wide(V_ABI, NB), ALU.max)
            NH = ST * NB
            abr, abi, t1, t2, t3, t4 = gr[:, 0:NH], gi[:, 0:NH], *(xt1[:, NH * i:NH * i + NH] for i in range(4))

            def advance(pr_, pi_, cr_, ci_):
                dve.tensor_tensor(t1, pr_, abr, ALU.mult)
                dve.tensor_tensor(t2, pi_, abi, ALU.mult)
                dve.tensor_tensor(t3, pr_, abi, ALU.mult)
                tt(t4, pi_, abr, ALU.mult)
                dve.tensor_tensor(t1, t1, t2, ALU.subtract)
                tt(t3, t3, t4, ALU.add)
                dve.tensor_tensor(cr_, cr_, t1, ALU.add)
                tt(ci_, ci_, t3, ALU.add)

            advance(h0[:, 0:NH], h0[:, NH:2 * NH], HF[0][:, :, 0], HF[1][:, :, 0])
            for s in range(1, NS):
                advance(HF[0][:, :, s - 1], HF[1][:, :, s - 1], HF[0][:, :, s], HF[1][:, :, s])
            for c in range(2):
                step(dve.tensor_copy(h0[:, c * NH:(c + 1) * NH], HF[c][:, :, NS - 1]))
            dve.tensor_scalar(hs_im[:, :], hs_im[:, :], -1.0, None, ALU.mult).then_inc(hs_made, 1)
            dve.memset(BT[:, 0, :, 0:1], 1.0)
            step(dve.memset(BT[:, 1, :, 0:1], 0.0))
            for k in range(6):
                n = 1 << k
                wr, wi = wide(V_POW + 2 * k, n), wide(V_POW + 2 * k + 1, n)
                er, ei = BT[:, 0, :, 0:n], BT[:, 1, :, 0:n]
                dve.tensor_tensor(x16(xt1, n), er, wr, ALU.mult)
                dve.tensor_tensor(x16(xt2, n), ei, wi, ALU.mult)
                dve.tensor_tensor(x16(gr, n), er, wi, ALU.mult)
                tt(x16(gi, n), ei, wr, ALU.mult)
                dve.tensor_tensor(BT[:, 0, :, n:2 * n], x16(xt1, n), x16(xt2, n), ALU.subtract)
                if k < 5:
                    tt(BT[:, 1, :, n:2 * n], x16(gr, n), x16(gi, n), ALU.add)
                else:
                    dve.tensor_tensor(BT[:, 1, :, n:2 * n], x16(gr, n), x16(gi, n), ALU.add).then_inc(powers_made, 1)
                    dve.wait_ge(powers_made, 1)

            bi, bum, ysm, hus, lev, xsm, srm, pown = (
                Count(s) for s in (blk_in, bu_mm, ys_mm, h_used, level_made, xs_made, sr_made, pool_own))

            def x4(t):
                return t[:, 0:4 * P].rearrange("p (t n) -> p t n", t=4)

            with turns(dve, 2, {own: S5_STEPS, bi: 64, bum: 8, ysm: 1, hus: 8, lev: 32, xsm: 8, srm: 8, pown: 8}) as z:
                step(copy(r_blk[:, :], SC[:, V_R, bass.ds(z * 8, 8)]))
                dve.wait_ge(blk_in, bi.add(64))
                dve.wait_ge(ys_mm, ysm.add())
                for b in range(2):
                    cre, cim = (c_blk[b][:, :].rearrange("p (t c s) -> p t c s", t=4, c=2)[:, :, c, :] for c in range(2))
                    fr, fi = (SC[:, v, bass.ds(z * 8 + b * 4, 4)].unsqueeze(2).broadcast_to([P, 4, P]) for v in (V_CR, V_CI))
                    dve.tensor_tensor(x4(gr), cre, fr, ALU.mult)
                    dve.tensor_tensor(x4(gi), cim, fi, ALU.mult)
                    dve.tensor_tensor(x4(xt1), cre, fi, ALU.mult)
                    tt(x4(xt2), cim, fr, ALU.mult)
                    dve.tensor_tensor(cre, x4(gr), x4(gi), ALU.subtract)
                    ins = dve.scalar_tensor_tensor(cim, x4(xt1), -1.0, x4(xt2), ALU.mult, ALU.subtract)
                    if b == 0:
                        step(ins)
                ins.then_inc(vec_dve, 1)
                dve.wait_ge(vec_dve, z + 1)

                def skip_path(b, tokens, y):
                    return dve.scalar_tensor_tensor(ZB[:, bass.ds(z * 2 + b, 1), tokens], U[:, bass.ds(z * 2 + b, 1), tokens],
                                                    param[:, bass.ds(z * 2 + (b + C_D), 1)], y, ALU.mult, ALU.add)

                def finish(b):
                    dve.wait_ge(h_used, z * 8 + 4 * (b + 1))
                    skip_path(b, slice(SAMPLE, PADS), psum[:, 4:6, :].rearrange("p (a b) c -> p a (b c)", a=1)).then_inc(y_made, 1)

                for b in range(2):
                    skip_path(b, slice(0, SAMPLE), psum[:, 6:7, b * SAMPLE:(b + 1) * SAMPLE])
                for k in range(8):
                    t = k % 4
                    TR, TI = tr[t], ti[t]
                    dve.wait_ge(level_made, lev.add(4))
                    dve.wait_ge(bu_mm, bum.add())
                    ur, ui = psum[:, 0:2, :].rearrange("p b c -> p (b c)"), psum[:, 2:4, :].rearrange("p b c -> p (b c)")
                    dve.tensor_tensor(xt1[:, :], ur, TR[:, :], ALU.mult)
                    step(dve.tensor_tensor(xt2[:, :], ui, TI[:, :], ALU.mult))
                    tt(gr[:, :], xt1[:, :], xt2[:, :], ALU.add)
                    dve.tensor_tensor(xt1[:, :], ui, TR[:, :], ALU.mult)
                    dve.tensor_tensor(xt2[:, :], ur, TI[:, :], ALU.mult).then_inc(bu_used, 1)
                    dve.wait_ge(bu_used, z * 8 + k + 2)
                    tt(gi[:, :], xt1[:, :], xt2[:, :], ALU.subtract)
                    dve.wait_ge(pool_own, pown.at)
                    pown.add()
                    r = r_blk[:, k:k + 1].broadcast_to([P, SEQ])
                    dve.tensor_tensor_scan(xs1[:, :], r, gr[:, :], 0.0, ALU.mult, ALU.add)
                    dve.tensor_tensor_scan(xs2[:, :], r, gi[:, :], 0.0, ALU.mult, ALU.add).then_inc(xs_made, 1)
                    dve.wait_ge(xs_made, xsm.add())
                    dve.wait_ge(h_used, hus.at if k < 2 else hus.add())
                    dve.tensor_tensor(xt1[:, :], xs1[:, :], TR[:, :], ALU.mult)
                    step(dve.tensor_tensor(xt2[:, :], xs2[:, :], TI[:, :], ALU.mult))
                    dve.tensor_tensor(sr[t % 2][:, :], xt1[:, :], xt2[:, :], ALU.subtract).then_inc(sr_made, 1)
                    dve.wait_ge(sr_made, srm.add())
                    dve.tensor_copy(last[:, k:k + 1], sr[t % 2][:, SEQ - 1:SEQ])
                    if k:
                        dve.wait_ge(si_made, z * 8 + k)
                        step(dve.tensor_copy(last[:, 7 + k:8 + k], si[(k - 1) % 2][:, SEQ - 1:SEQ]))
                    if k == 5:
                        finish(0)
                hus.add(2)
                dve.wait_ge(si_made, z * 8 + 8)
                step(dve.tensor_copy(last[:, 15:16], si[1][:, SEQ - 1:SEQ]))
                copy(SC[:, V_X, bass.ds(z * 8, 8)], last[:, 0:8])
                step(copy(SC[:, V_TH, bass.ds(z * 8, 8)], last[:, 8:16]))
                finish(1)
            dve.memset(ZB[:, :, PADS:T], 0.0).then_inc(zeroed, 1)
            vv(V_T1, V_X, V_CR, ALU.mult)
            vv(V_T2, V_TH, V_CI, ALU.mult)
            vv(V_T1, V_T1, V_T2, ALU.subtract)
            vv(V_T2, V_X, V_CI, ALU.mult)
            vv(V_T3, V_TH, V_CR, ALU.mult)
            dve.tensor_tensor(vec(V_T2), vec(V_T2), vec(V_T3), ALU.add).then_inc(state_out, 1)
            for m in range(4):
                low(ZL[:, m, :], ZB[:, m, :], ZH[:, m, :])

            for m in range(4):
                dve.wait_ge(free[m % 2], UNITS_AT[W_GLU] // 2 + m // 2 + 1)
                dve.tensor_tensor(TMP[:, m % 2, :], TMP[:, m % 2, :], ZB[:, m, :], ALU.mult).then_inc(scaled, 1)
                low(HL[:, 4 + m, :], TMP[:, m % 2, :], HH[:, 4 + m, :])
            u.skip(4)

            dve.memset(HH[:, 0:4, PADS:T].bitcast(F32), 0.0)
            dve.memset(HL[:, 0:4, PADS:T].bitcast(F32), 0.0)
            low(HL[:, 0:4, 0:SAMPLE], tiles(oas, 4), HH[:, 0:4, 0:SAMPLE])
            ogl = [Count(s) for s in og_loaded]
            turn_ = Count(turned)
            with turns(dve, 4, {ogl[0]: 16, ogl[1]: 16, own: 20, n_we: 2, hi: 2, lo: 2}) as t:
                for b in range(2):
                    IN = og_in[:, b * 3 * ROW:(b + 1) * 3 * ROW].rearrange("p (g c) -> p g c", g=3)
                    W = c_w[:, b * 64:b * 64 + 64]
                    acc = c_acc[:, b * 512:b * 512 + 512].rearrange("p (h d) -> p h d", h=8)
                    og_o = [IN[:, g, 0:512].rearrange("p (h d) -> p h d", h=8) for g in range(3)]
                    dve.wait_ge(og_loaded[b], ogl[b].add(16))
                    nm, ls = IN[:, :, 520:528], IN[:, :, 512:520]
                    tt(W[:, 0:8], nm[:, 0], nm[:, 1], ALU.min)
                    tt(W[:, 0:8], W[:, 0:8], nm[:, 2], ALU.min)
                    E = W[:, 32:56].rearrange("p (g h) -> p g h", g=3)
                    D = W[:, 8:32].rearrange("p (g h) -> p g h", g=3)
                    dve.tensor_tensor(D, W[:, 0:8].unsqueeze(1).broadcast_to([P, 3, 8]), nm, ALU.subtract).then_inc(w_dif, 1)
                    dve.wait_ge(w_exp, n_we.add())
                    tt(E, E, ls, ALU.mult)
                    tt(W[:, 0:8], E[:, 0], E[:, 1], ALU.add)
                    tt(W[:, 0:8], W[:, 0:8], E[:, 2], ALU.add)
                    step(dve.reciprocal(W[:, 56:64], W[:, 0:8]))
                    tt(D, E, W[:, 56:64].unsqueeze(1).broadcast_to([P, 3, 8]), ALU.mult)
                    for g in range(3):
                        dve_in = og_o[g]
                        ins = dve.tensor_tensor(dve_in, dve_in, D[:, g].unsqueeze(2).broadcast_to([P, 8, HEAD_DIM]), ALU.mult)
                    step(ins)
                    step(dve.tensor_tensor(og_o[1], og_o[0], og_o[1], ALU.add))
                    dve.tensor_tensor(acc, og_o[1], og_o[2], ALU.add).then_inc(comb_made, 1)
                    dve.wait_ge(comb_made, t * 2 + b + 1)
                    step(dve.tensor_copy(W[:, 0:4], W[:, 4:8]))
                    dve.tensor_copy(W[:, 0:4], W[:, 4:8]).then_inc(og_used, 1)
                    cols = bass.ds(t * 256 + SAMPLE + P * b, P)
                    low(HL[:, 0:4, cols], psum[:, 6 + b, :].rearrange("p (k c) -> p k c", c=P), HH[:, 0:4, cols])

            for layer in range(2):
                if layer == 1:
                    u.skip(2, 2, 2, 2, 2, 4)
                    dve.wait_ge(x_made, 16 + 8)
                    dve.wait_ge(lo_made, lo.at)
                    dve.wait_ge(free[0], UNITS_AT[W_QC] // 2 + 1)
                    dve.memset(qc_st[:, :], 0.0).then_inc(zeroed, 1)
                    attend(0, H_C)
                    dve.memset(HH[:, :, PADS:T].bitcast(F32), 0.0)
                    dve.memset(HL[:, :, PADS:T].bitcast(F32), 0.0)
                    dve.wait_ge(s_mm, N_A_STEPS + N_C_STEPS)
                    step(dve.memset(qc_st[:, :], 0.0))
                    QS = qc_st[:, :].rearrange("p (n j h q) -> p n j h q", n=NB, j=2, h=16)
                    for j in range(2):
                        for o in range(2):
                            for par in range(2):
                                src = XA[64 * par:64 * par + 64, 4 * j + 2 * o:4 * j + 2 * o + 2, 0:SAMPLE]
                                h = 8 * j + 4 * o + par
                                out = QS[64 * o:64 * o + 64, :, j, h:h + 3:2, :]
                                ins = dve.tensor_scalar(out.rearrange("p n y q -> p y n q"), src.rearrange("p y (n q) -> p y n q", n=NB),
                                                        HEAD_DIM ** -0.5, None, ALU.mult)
                                if not (j and o and par):
                                    step(ins)
                    ins.then_inc(qb_made, 1)
                    dve.wait_ge(ss_mm, 9)
                    S = tiles(cs_s, 4)
                    step(dve.tensor_tensor(S, psum[:, 0:4, 0:2 * SKC], tiles(cm_sb, 4), ALU.add))
                    step(dve.tensor_reduce(cstat[:, 0:8], tiles(cs_s, NB), AX, ALU.max, negate=True))
                    dve.tensor_scalar(cstat[:, 0:8], cstat[:, 0:8], nsink[:, 16:17], None, ALU.min).then_inc(ss_max, 1)
                    dve.wait_ge(ss_exp, 5)
                    step(dve.tensor_tensor(cstat[:, 8:16], cstat[:, 8:16], cstat[:, 16:24], ALU.add))
                    step(dve.reciprocal(cstat[:, 24:32], cstat[:, 8:16]))
                    S8 = tiles(cs_s, NB)
                    dve.tensor_tensor(S8, S8, cstat[:, 24:32].unsqueeze(2).broadcast_to([P, NB, SKC]), ALU.mult).then_inc(ss_norm, 1)
                    dve.wait_ge(spv_mm, 1)
                    OC = tiles(ocs, 8)
                    O = psum[:, 0:2, :].rearrange("p b (n c) -> p (b n) c", n=4)
                    for j in range(2):
                        for o in range(2):
                            for par in range(2):
                                src = O[64 * o:64 * o + 64, :, j * 64 + o * 32 + par * 8:j * 64 + o * 32 + 32]
                                for y in range(2):
                                    ins = dve.tensor_copy(
                                        OC[64 * par:64 * par + 64, 4 * j + 2 * o + y, :].rearrange("p (n q) -> p n q", n=NB),
                                        src[:, :, y * 16:y * 16 + 8])
                                    if not (j and o and par and y):
                                        step(ins)
                    ins.then_inc(spv_taken, 1)
                    low(HL[:, :, 0:SAMPLE], OC, HH[:, :, 0:SAMPLE])
                u.skip(2, 2, 2, 2)
                residual(layer, 1)
                normalise(layer, 2)
                dve.wait_ge(x_out, 16 + 32 * layer)
                step(dve.memset(XA, 0.0))

                def ff_up(h):
                    for m in range(2):
                        u.skip_half(m)
                        dve.wait_ge(free[m], u.free[m].at)
                        dve.tensor_tensor(TMP[:, m, :], TMP[:, m, :], TMP[:, m, :], ALU.mult).then_inc(scaled, 1)
                    for m in range(2):
                        low(HIDL[h][:, m, :], TMP[:, m, :], HIDH[h][:, m, :])

                def ff_down():
                    for m in range(8):
                        if m < 2:
                            dve.wait_ge(free[m % 2], u.free[m % 2].at)
                        u.wait(dve, m == 7)
                        dve.tensor_tensor(chunked(XA[:, m, :]), chunked(XA[:, m, :]), UNIT[m % 2], ALU.add).then_inc(free[m % 2], 1)
                        u.free[m % 2].add()

                ff_up(0)
                with turns(dve, 7, {lo: 4, hi: 4, **u.per(2, 8, 2, 8)}):
                    ff_up(1)
                    ff_down()
                    ff_up(0)
                    ff_down()
                ff_up(1)
                ff_down()
                ff_down()
                residual(layer, 3)
                u.skip(0 + 8)
                u.done.add()
                normalise(layer, 4)
                for m in range(8):
                    if m % 2 == 0:
                        u.skip(2)
                    dve.wait_ge(free[m % 2], u.free[m % 2].at)
                    step(dve.tensor_tensor(TMP[:, m % 2, :], TMP[:, m % 2, :], XD[:, m, :], ALU.mult))
                    dve.tensor_tensor(XA[:, m, :], XA[:, m, :], TMP[:, m % 2, :], ALU.add).then_inc(x_made, 1)
                if layer == 0:
                    normalise(1, 0)


def _layouts(i):
    import numpy as np
    f = lambda name: np.asarray(i[name])

    def ktiles(w):
        return w.reshape(-1, P, w.shape[1]).transpose(1, 0, 2)

    def feature_major(sample, prompt):
        t = np.zeros((sample.shape[-1], T), sample.dtype)
        t[:, :SAMPLE] = sample.reshape(SAMPLE, -1).T
        t[:, SAMPLE:PADS] = prompt.reshape(SEQ, -1).T
        return ktiles(t)

    out = {"xT": feature_major(f("x_sample"), f("x_prompt"))}
    wall = np.zeros((N_SLOTS, P, SLOT), f("w_ff1").dtype)

    def put(slot, w):
        w = ktiles(w).reshape(P, -1)
        wall[slot, :, :w.shape[1]] = w
        return slot + 1

    def columns(slot, w):
        for c in range(0, w.shape[1], 256):
            slot = put(slot, w[:, c:c + 256])
        return slot

    w_in = f("w_in_ab")[0]
    columns(W_U, w_in[:, 9 * 512:])
    columns(W_QKV, w_in[:, :9 * 512])
    put(W_GLU, f("w_glu")[0])
    columns(W_OUT[0], f("w_out_ab")[0])
    columns(W_QC, f("w_in_c")[0])
    columns(W_OUT[1], f("w_out_c")[0])
    for layer in range(2):
        w1, w2, s = f("w_ff1")[layer], f("w_ff2")[layer], W_FF[layer]
        up = [w1[:, 256 * k:256 * k + 256] for k in range(FF_BLOCKS)]
        down = [w2[256 * k:256 * k + 256] for k in range(FF_BLOCKS)]
        s = put(s, up[0])
        for k in range(1, FF_BLOCKS):
            s = put(s, up[k])
            s = put(s, down[k - 1])
        put(s, down[-1])
        wall[W_PLE[layer]] = feature_major(f("p_sample")[layer], f("p_prompt")[layer]).reshape(P, -1)
        put(W_PLE[layer] + 1, f("w_ple")[layer])
        columns(W_GATE[layer], f("w_ple_gate")[layer])
    out["wall"] = wall

    tri = np.arange(P)[:, None] - np.arange(P)[None, :]
    consts = np.zeros((P, 5 * P), np.float32)
    consts[:, 0:P] = np.eye(P)
    consts[:, P:2 * P] = 1
    consts[:, 2 * P:3 * P] = np.where(tri <= 0, 0, -1e30)
    consts[:, 3 * P:4 * P] = np.where(tri >= 0, 0, -1e30)
    half = np.arange(P) % 2
    consts[:, 4 * P:5 * P] = np.where((tri >= 0) & (half[:, None] == half[None, :]), 0, -1e30)
    out["consts"] = consts
    params = np.zeros((P, N_PARAM), np.float32)
    gains = np.stack([f("g_" + g) for g in GAINS], 1)
    params[:, 0:80] = gains.reshape(2, 5, KC, P).transpose(3, 0, 1, 2).reshape(P, 80)
    params[:, C_GLU:C_GLU + 4] = f("b_glu")[0].reshape(4, P).T
    params[:, C_D:C_D + 4] = f("ssm_d")[0].reshape(4, P).T
    params[:, C_SINK:C_SINK + 16] = f("sinks_c")[0][None, :]
    params[:, C_SINKROW] = np.repeat(f("sinks_c")[0], NS)
    params[:, C_EPS] = EPS
    out["params"] = params

    s = np.tile(np.arange(NS), 2 * H_A)[:, None]
    b = np.repeat(np.arange(2), 64)[:, None]
    t = np.arange(SAMPLE)[None, :]
    smask = np.zeros((4, P, SK), bool)
    for z in range(4):
        new = [(t // NS == 2 * z + b) & (t % NS <= s) & ((s - t % NS) % d == 0) for d in DILATION]
        r1, r4 = np.arange(128)[None, :], np.arange(512)[None, :]
        smask[z] = np.concatenate([r1 >= s, *new, (r4 >= s) & ((r4 - s) % 4 == 0), (np.arange(512)[None, :] % 8 == s)], 1)
    out["smask"] = np.where(smask, 0, -1e30).astype(np.float32)
    sc_ = np.tile(np.arange(NS), H_C)[:, None]
    cm = [np.concatenate([np.arange(P)[None, :] >= sc_, (t // NS == n) & (t % NS <= sc_)], 1) for n in range(NB)]
    out["cmask"] = np.where(np.concatenate(cm, 1), 0, -1e30).astype(np.float32)

    def states(x):
        return x.reshape(ST, P, *x.shape[2:]).swapaxes(0, 1)

    dt = np.repeat(f("ssm_log_dt")[0][:, None], 64, 1)
    out["ssm"] = np.stack([states(f("ssm_a_re")[0]), states(f("ssm_a_im")[0]), states(dt)], 1).reshape(P, 3 * ST)
    h0 = [states(f(k)[0].transpose(1, 2, 0)) for k in ("state_b_re", "state_b_im")]
    out["h0"] = np.stack(h0, 1).reshape(P, -1)
    bm, cm_ = np.zeros((4, P, 4, 2, P), np.float32), np.zeros((4, P, 4, 2, P), np.float32)
    for g in range(32):
        blk, gl = divmod(g, 8)
        tile, part = divmod(gl, 2)
        for c, (kb, kc) in enumerate((("ssm_b_re", "ssm_c_re"), ("ssm_b_im", "ssm_c_im"))):
            bm[blk, 16 * gl:16 * gl + 16, tile, c, 64 * part:64 * part + 64] = f(kb)[0, g].T
            cm_[blk, 64 * part:64 * part + 64, tile, c, 16 * gl:16 * gl + 16] = f(kc)[0, g].T
    out["bmat"], out["cmat"] = bm.reshape(4, P, 1024), cm_.reshape(4, P, 1024)

    def keys(c):
        n, r = c.shape[:2]
        return c.reshape(n, r, -1, P).transpose(0, 3, 2, 1).reshape(n, P, -1)

    for g, name in enumerate(("cache_a1_kv", "cache_a2_kv", "cache_a3_kv")):
        c = f(name)[0]
        out[f"kt{g}"], out[f"v{g}"] = keys(c[:, 0]), c[:, 1].reshape(NB, ROWS[g], 512)
    c = f("cache_c_kv")[0]
    out["ktc"], out["vc"] = keys(c[:, 0]), c[:, 1].reshape(NB, ROWS_C, 256)
    return out


_OUTS = {"yT": (P, KC, T), "st_s": (P, 2 * ST * NB), "st_p": (P, 2 * ST),
         **{f"okp{g}": (P, 4, r) for g, r in enumerate(ROWS)}, **{f"ovp{g}": (r, 512) for g, r in enumerate(ROWS)},
         **{f"oks{g}": (NB, P, 4, r - NS) for g, r in enumerate(ROWS)},
         **{f"ovs{g}": (NB, r - NS, 512) for g, r in enumerate(ROWS)},
         **{f"oks_new{g}": (P, 4, SAMPLE) for g in range(3)}, **{f"ovs_new{g}": (SAMPLE, 512) for g in range(3)},
         "okc_p": (P, 2, ROWS_C), "ovc_p": (ROWS_C, 256), "okc_s": (NB, P, 2, ROWS_C - NS),
         "ovc_s": (NB, ROWS_C - NS, 256), "okc_new": (P, 2, SAMPLE), "ovc_new": (SAMPLE, 256)}


def kernel(**inputs):
    import numpy as np
    import concourse.bacc as bacc
    from concourse.bass_utils import run_bass_kernel_spmd as run

    nc = bacc.Bacc("TRN2", target_bir_lowering=False, num_devices=1)
    arrays, a = {}, {}
    for name, x in _layouts(inputs).items():
        x = np.ascontiguousarray(x)
        arrays[f"in_{name}"] = x
        a[name] = nc.dram_tensor(f"in_{name}", x.shape, mybir.dt.from_np(x.dtype), kind="ExternalInput").ap()
    for name, shape in _OUTS.items():
        a[name] = nc.dram_tensor(f"out_{name}", shape, F32, kind="ExternalOutput").ap()
    for name in ("kt", "v", "okp", "ovp", "oks", "ovs", "oks_new", "ovs_new"):
        a[name] = [a[f"{name}{g}"] for g in range(3)]
    build(nc, a)
    r = run(nc, [arrays], core_ids=[0]).results[0]
    o = {name: r[f"out_{name}"] for name in _OUTS}

    y = o["yT"].transpose(2, 1, 0).reshape(T, D_MODEL)
    outs = [y[SAMPLE:PADS].reshape(1, SEQ, D_MODEL), y[:SAMPLE].reshape(NB, NS, D_MODEL)]

    def prompt(k, v, heads):
        k = k.transpose(2, 1, 0).reshape(v.shape)
        return np.stack([k, v]).reshape(1, 1, 2, -1, heads, HEAD_DIM)

    def sample(k, k_new, v, v_new, heads):
        k = k.transpose(0, 3, 2, 1).reshape(v.shape)
        k_new = k_new.transpose(2, 1, 0).reshape(NB, NS, -1)
        k = np.concatenate([k, k_new], 1)
        v = np.concatenate([v, v_new.reshape(NB, NS, -1)], 1)
        return np.stack([k, v], 1).reshape(1, NB, 2, -1, heads, HEAD_DIM)

    for g in range(3):
        outs.append(prompt(o[f"okp{g}"], o[f"ovp{g}"], H_A))
        outs.append(sample(o[f"oks{g}"], o[f"oks_new{g}"], o[f"ovs{g}"], o[f"ovs_new{g}"], H_A))
    st_p = o["st_p"].reshape(P, 2, ST).transpose(1, 2, 0).reshape(2, 1, 1, 32, N_STATE)
    st_s = o["st_s"].reshape(P, 2, ST, NB).transpose(1, 3, 2, 0).reshape(2, 1, NB, 32, N_STATE)
    outs += [st_p[0], st_s[0], st_p[1], st_s[1]]
    outs.append(prompt(o["okc_p"], o["ovc_p"], 4))
    outs.append(sample(o["okc_s"], o["okc_new"], o["ovc_s"], o["ovc_new"], 4))
    return tuple(outs)
```

```python
from contextlib import ExitStack, contextmanager

import concourse.bass as bass
from concourse import mybir
from concourse.alu_op_type import AluOpType as ALU

F32 = mybir.dt.float32
F32R = mybir.dt.float32r
ACT = mybir.ActivationFunctionType
AX = mybir.AxisListType.X

P = 128
D_MODEL = 1024
KC = D_MODEL // P
HEAD_DIM = 64
N_STATE = 64
H_A = 8
H_C = 16
NB, NS = 8, 8
SAMPLE = NB * NS
SEQ = 1024
T = SAMPLE + SEQ + 4
CH = T // 3
PADS = SAMPLE + SEQ
DILATION = (1, 4, 16)
ROWS = (128, 512, 1024)
SEEN = (128, 512, 512)
ROWS_C = 128
ST = 16
SLOT = 2 * T
FF_BLOCKS = 16
EPS = 1e-6
ROW = 528
GAINS = ("pre_mix", "post_mix", "pre_ffn", "post_ffn", "ple")
SK = 128 + 3 * SAMPLE + 512 + 512
SKC = ROWS_C + SAMPLE

S5_STEPS = 45
W_U, W_QKV, W_GLU, W_OUT = 0, 2, 20, (21, 69)
W_FF, W_PLE, W_GATE = (25, 73), (57, 105), (59, 107)
W_QC, W_KC, W_VC, N_SLOTS = 63, 67, 68, 111

C_GLU, C_D, C_SINK, C_SINKROW, C_EPS, N_PARAM = 80, 84, 88, 104, 105, 106

V_ARE, V_AIM, V_DT, V_X, V_R, V_TH, V_K, V_COS, V_SIN, V_ABR, V_ABI, V_CR, V_CI, V_T1, V_T2, V_T3 = range(16)
V_POW = 16
N_VEC = V_POW + 20


UNITS = ([2] * 2 + ([2] * 4 + [4] * 2) * 3 + [4] + [2] * 4 + [2] + [2, 8] * 15 + [8] + [0, 8] + [2] * 4
         + [2] * 5 + [4] + [2] * 4 + [2] + [2, 8] * 15 + [8] + [0, 8] + [2] * 4)
assert len(UNITS) == N_SLOTS
UNITS_AT = [sum(UNITS[:s]) for s in range(N_SLOTS + 1)]
LO_GLU = 8 + 4 + 4
LO_MIXED_A = LO_GLU + 9
LO_MIXED_C = LO_MIXED_A + 8 + 2 * FF_BLOCKS + 8 + 8 + 9


class Count:

    def __init__(self, sem):
        self.sem, self.base, self.extra = sem, 0, 0

    @property
    def at(self):
        return self.base + self.extra

    def add(self, n=1):
        self.extra += n
        return self.at


@contextmanager
def turns(eng, n, per):
    start = {c: c.at for c in per}
    with eng.Fori(0, n) as i:
        for c, k in per.items():
            c.base, c.extra = start[c] + i * k, 0
        yield i
    for c, k in per.items():
        assert c.extra == k, (c.sem, c.extra, k)
        c.base, c.extra = start[c] + n * k, 0


def build(nc, a):
    x_keep = nc.dram_tensor("x_keep", (P, KC, T), F32).ap()
    og = nc.dram_tensor("og", (3, SEQ, ROW), F32).ap()
    qk_keep = nc.dram_tensor("qk_keep", (P, 3, 8, SAMPLE), F32).ap()
    v_keep = nc.dram_tensor("v_keep", (SAMPLE, 3, 512), F32).ap()

    with ExitStack() as ctx:
        def region(name, cols, *stages):
            made = []
            for stage in stages:
                with ExitStack() as s:
                    for n, c, dt in stage:
                        made.append(s.enter_context(nc.sbuf_tensor(n, [P, c], dt)))
                    assert sum(c for _, c, _ in stage) <= cols, (name, stage)
            whole = ctx.enter_context(nc.sbuf_tensor(name, [P, cols], F32))
            return whole, *made

        def sb(name, cols, dt=F32):
            return ctx.enter_context(nc.sbuf_tensor(name, [P, cols], dt))

        def sem(name):
            return ctx.enter_context(nc.semaphore(name))

        w_raw = sb("w_raw", SLOT)
        w_hi = [sb(f"w_hi{i}", SLOT, F32R) for i in range(2)]
        w_lo = [sb(f"w_lo{i}", SLOT, F32R) for i in range(2)]
        ident, ones, mask, param = sb("ident", P), sb("ones", P), sb("mask", 3 * P), sb("param", N_PARAM)
        oas = sb("oas", 4 * SAMPLE)
        nsink = sb("nsink", 17)
        (_, tmp, rs, q_st, sm, pr, pt, o_st, stat, vs_new, ks_new, sstat, sc, r_blk, hs_re, hs_im, h0, bt, last,
         og_in, c_acc, c_w, ktc_sb, vc_in, cm_sb) = region(
            "region_e", 5680,
            [("tmp", 2 * T, F32), ("rs", T, F32)],
            [("q_st", 1024, F32), ("sm", 1024, F32), ("pr", 1024, F32), ("pt", 1024, F32),
             ("o_st", ROW, F32), ("stat", 128, F32)],
            [("vs_new", 3 * 512, F32), ("ks_new", 12 * SAMPLE, F32), ("sstat", 16, F32)],
            [("sc", N_VEC * ST, F32), ("r_blk", 8, F32), ("hs_re", 1024, F32), ("hs_im", 1024, F32),
             ("h0", 2 * ST * NB, F32), ("bt", 2048, F32), ("last", 16, F32)],
            [("og_in", 2 * 3 * ROW, F32), ("c_acc", 1024, F32), ("c_w", 128, F32)],
            [("ktc_sb", 2048, F32), ("vc_in", 2048, F32), ("cm_sb", NB * SKC, F32)])
        (_, hid_hi0, hid_hi1, hid_lo0, hid_lo1, xd, v_sb, u_sb, zb_, kc_sb, vc_sb, qc_st, on_c) = region(
            "region_d", 9 * 512 + 4 * T,
            [("hid_hi0", 2 * T, F32R), ("hid_hi1", 2 * T, F32R), ("hid_lo0", 2 * T, F32R), ("hid_lo1", 2 * T, F32R)],
            [("xd", KC * T, F32)],
            [("v_sb", 9 * 512, F32), ("u_sb", 4 * T, F32)],
            [("zb", 4 * T, F32)],
            [("kc_sb", 2 * T, F32), ("vc_sb", 9 * 256, F32), ("qc_st", 2048, F32), ("on_c", 1024, F32)])
        hid_hi, hid_lo = (hid_hi0, hid_hi1), (hid_lo0, hid_lo1)
        (xa, z_hi, z_lo, sp_t, qb, qs, tr2, ti2, tr3, ti3, sr1, si1, b_blk1, c_blk1,
         cs_s, cs_t, ocs, cstat) = region(
            "xa", KC * T,
            [("z_hi", 4 * T, F32R), ("z_lo", 4 * T, F32R)],
            [("sp_t", 12 * P, F32), ("qb", 960, F32), ("qs", 12 * SAMPLE, F32)],
            [(n, SEQ, F32) for n in ("tr2", "ti2", "tr3", "ti3", "sr1", "si1", "b_blk1", "c_blk1")],
            [("cs_s", NB * SKC, F32), ("cs_t", 2048, F32), ("ocs", 512, F32), ("cstat", 64, F32)])
        (_, h_hi, h_lo, kt_sb0, kt_sb1, va, s_sb, sm_sb, b_blk0, c_blk0, tr0, ti0, tr1, ti1, gr, gi, xt1, xt2,
         xs1, xs2, sr0, si0, sj, tp) = region(
            "region_bc", 2 * KC * T,
            [("h_hi", KC * T, F32R), ("h_lo", KC * T, F32R)],
            [("kt_sb0", 4 * sum(SEEN), F32), ("kt_sb1", 4 * sum(SEEN), F32), ("va", 9 * 512, F32), ("s_sb", SK, F32),
             ("sm_sb", SK, F32)],
            [("b_blk0", 1024, F32), ("c_blk0", 1024, F32)]
            + [(n, SEQ, F32) for n in ("tr0", "ti0", "tr1", "ti1", "gr", "gi", "xt1", "xt2", "xs1", "xs2", "sr0", "si0", "sj")]
            + [("tp", 2048, F32)])
        kt_sb = (kt_sb0, kt_sb1)
        tr, ti = (tr0, tr1, tr2, tr3), (ti0, ti1, ti2, ti3)
        sr, si = (sr0, sr1), (si0, si1)
        b_blk, c_blk = (b_blk0, b_blk1), (c_blk0, c_blk1)
        psum = ctx.enter_context(nc.psum_tensor("psum", [P, 8, 512], F32))

        raw_in, hi_made, split, slot_done = sem("raw_in"), sem("hi_made"), sem("split"), sem("slot_done")
        full, free = sem("full"), (sem("free0"), sem("free1"))
        const_in = sem("const_in")
        x_half, x_in, x_out, x_made = sem("x_half"), sem("x_in"), sem("x_out"), sem("x_made")
        sq_made, sq_used, sums_read, inv_made = sem("sq_made"), sem("sq_used"), sem("sums_read"), sem("inv_made")
        part_made, part_added, whole_sum = sem("part_made"), sem("part_added"), sem("whole_sum")
        scaled, hi_act, lo_made = sem("scaled"), sem("hi_act"), sem("lo_made")
        dve_own, act_own = sem("dve_own"), sem("act_own")
        q_ready, s_mm, s_masked, max_made, exp_made = (sem(n) for n in ("q_ready", "s_mm", "s_masked", "max_made", "exp_made"))
        pt_mm, pt_taken, pv_mm, o_made, o_out = (sem(n) for n in ("pt_mm", "pt_taken", "pv_mm", "o_made", "o_out"))
        turned, zeroed = sem("turned"), sem("zeroed")
        ss_max, vec_arg = sem("ss_max"), sem("vec_arg")
        out_done, kept = sem("out_done"), sem("kept")
        sx_in, kv_used, mask_in = sem("sx_in"), sem("kv_used"), sem("mask_in")
        k_in, v_in = (sem("k_in0"), sem("k_in1")), (sem("v_in0"), sem("v_in1"))
        qb_made, ss_mm, ss_masked, ss_exp, ss_norm = (sem(n) for n in ("qb_made", "ss_mm", "ss_masked", "ss_exp", "ss_norm"))
        st_mm, st_taken, spv_mm, spv_taken = (sem(n) for n in ("st_mm", "st_taken", "spv_mm", "spv_taken"))
        ssm_in, b_in, b_used, blk_in, vec_act, vec_dve, bu_mm, bu_used = (
            sem(n) for n in ("ssm_in", "b_in", "b_used", "blk_in", "vec_act", "vec_dve", "bu_mm", "bu_used"))
        powers_made, level_prod, level_made, xs_made, sr_made, si_made, pool_own = (
            sem(n) for n in ("powers_made", "level_prod", "level_made", "xs_made", "sr_made",
                             "si_made", "pool_own"))
        hs_made, ys_mm, h_used, y_made, state_out = (
            sem(n) for n in ("hs_made", "ys_mm", "h_used", "y_made", "state_out"))
        w_dif, w_exp, comb_made = sem("w_dif"), sem("w_exp"), sem("comb_made")
        og_loaded = (sem("og_loaded0"), sem("og_loaded1"))

        def tiles(t, n):
            return t[:, :].rearrange("p (n c) -> p n c", n=n)

        XA, XD, TMP = tiles(xa, KC), tiles(xd, KC), tiles(tmp, 2)
        HH, HL = tiles(h_hi, KC), tiles(h_lo, KC)
        HIDH, HIDL = [tiles(t, 2) for t in hid_hi], [tiles(t, 2) for t in hid_lo]
        U, ZB, ZH, ZL = tiles(u_sb, 4), tiles(zb_, 4), tiles(z_hi, 4), tiles(z_lo, 4)
        V, VC, KCT = tiles(v_sb, 9), tiles(vc_sb, 9), tiles(kc_sb, 2)
        G = param[:, 0:80].rearrange("p (l k c) -> p l k c", l=2, k=5)
        QST, QCST = tiles(q_st, 8), tiles(qc_st, 16)
        UNIT = [psum[:, 3 * s:3 * s + 3, 0:CH] for s in range(2)]

        def chunked(ap):
            return ap.rearrange("p (c n) -> p c n", c=3)


        def prompt_cols(g, i):
            if g == 0:
                return lambda x: x[:, :, bass.ds(SAMPLE + i * P, P)]
            if g == 1:
                return lambda x: x[:, :, bass.ds(SAMPLE + i[1] * 512 + i[0], P, 4)]
            return lambda x: x[:, :, bass.ds(SAMPLE + i, P, 8)]

        def key_cols(g, i, nk):
            if nk == 1:
                return prompt_cols(g, i)
            if g == 0:
                return lambda x: x[:, :, bass.ds(SAMPLE - P + i * P, 2 * P)]
            return lambda x: x[:, :, bass.ds(SAMPLE + i[0], 2 * P, 4)]

        def value_tile(g, i):
            return 2 * i[0] + i[1] if g == 1 else i

        def over_tiles(eng, g, per_tile, tile):
            if g == 1:
                def pair(i, first, last):
                    tile((i, 0), 1, None if first else ((i - 1, 1), 2), ((i, 1), 2))
                    tile((i, 1), 2, ((i, 0), 1), None if last else ((i + 1, 0), 1))

                pair(0, True, False)
                with turns(eng, 2, {c: 2 * k for c, k in per_tile.items()}) as i:
                    pair(i + 1, False, False)
                pair(3, False, True)
            else:
                nk = 2 - g // 2
                tile(0, 1, None, (1, nk))
                if g == 0:
                    tile(1, 2, (0, 1), (2, 2))
                first = 2 - g // 2
                with turns(eng, 7 - first, per_tile) as i:
                    tile(i + first, nk, (i + (first - 1), nk), (i + (first + 1), nk))
                tile(7, nk, (6, nk), None)

        class Units:

            def __init__(self):
                self.full, self.done, self.free = Count(full), Count(slot_done), (Count(free[0]), Count(free[1]))

            def wait(self, eng, last):
                c = self.done if last else self.full
                eng.wait_ge(c.sem, c.add())

            def skip(self, *slots):
                for n in slots:
                    self.full.add(n - 1)
                    self.done.add()
                    self.free[0].add(n // 2)
                    self.free[1].add(n // 2)

            def skip_half(self, m):
                (self.done if m else self.full).add()
                self.free[m].add()

            def per(self, *slots):
                n = sum(slots)
                return {self.full: n - len(slots), self.done: len(slots), self.free[0]: n // 2, self.free[1]: n // 2}

            def all_free(self, eng):
                eng.wait_ge(free[0], self.free[0].at)
                eng.wait_ge(free[1], self.free[1].at)

        block = ctx.enter_context(nc.Block())
        N_A_STEPS, N_C_STEPS = 3 * 8 * 4, 8 * 8

        @block.sync
        def _(sp):
            spl, stored, units = Count(split), Count(out_done), Units()
            made, oout, keeps = Count(o_made), Count(o_out), Count(kept)
            xin, xout, xm = Count(x_in), Count(x_out), Count(x_made)
            fed = [0]

            def feed(slot, first=False):
                if not first:
                    sp.wait_ge(split, spl.add())
                src = a["wall"][bass.ds(slot, 1), :, :].rearrange("a p n -> p (a n)")
                sp.dma_start(w_raw[:, :], src).then_inc(raw_in, 16)

            def feed_to(end):
                n = end - fed[0]
                if not fed[0]:
                    feed(0, first=True)
                    n, fed[0] = n - 1, 1
                if n > 0:
                    with turns(sp, n, {spl: 1}) as i:
                        feed(i + fed[0])
                fed[0] = end

            def store(dst, src):
                sp.dma_start(dst, src).then_inc(out_done, 16)
                stored.add(16)

            c = a["consts"]
            sp.dma_start(XA[:, 0:4, :], a["xT"][:, 0:4, :]).then_inc(x_half, 16)
            sp.dma_start(XA[:, 4:8, :], a["xT"][:, 4:8, :]).then_inc(x_in, 16)
            sp.dma_start(ident[:, :], c[:, 0:P]).then_inc(const_in, 16)
            sp.dma_start(ones[:, :], c[:, P:2 * P]).then_inc(const_in, 16)
            sp.dma_start(mask[:, :], c[:, 2 * P:5 * P]).then_inc(const_in, 16)
            sp.dma_start(param[:, :], a["params"]).then_inc(const_in, 16)
            xin.add(16)
            feed_to(11)

            def load_keys(n, b):
                o = 0
                for g in range(3):
                    c = 4 * SEEN[g]
                    src = a["kt"][g].rearrange("n p (j r) -> n p j r", j=4)[bass.ds(n, 1), :, :, 0:SEEN[g]]
                    sp.dma_start(kt_sb[b][:, o:o + c].rearrange("p (j r) -> p j r", j=4), src.rearrange("n p j r -> (n p) j r"))\
                        .then_inc(k_in[b], 16)
                    o += c

            def load_values(n, b):
                vb = (va, v_sb)[b]
                sp.dma_start(vb[:, 0:512], a["v"][0][bass.ds(n, 1), :, :].rearrange("n p c -> p (n c)")).then_inc(v_in[b], 16)
                for c in range(4):
                    sp.dma_start(vb[:, 512 * (1 + c):512 * (2 + c)],
                                 a["v"][1][bass.ds(n, 1), P * c:P * c + P, :].rearrange("n p c -> p (n c)"))\
                        .then_inc(v_in[b], 16)
                    for h in range(2):
                        src = a["v"][2].rearrange("n (i s) c -> s n i c", s=16)[2 * c + h, bass.ds(n, 1), :, :]
                        sp.dma_start(vb[64 * h:64 * h + 64, 512 * (5 + c):512 * (6 + c)],
                                     src.rearrange("n i c -> (n i) c")).then_inc(v_in[b], 16)

            def load_mask(z):
                sp.dma_start(sm_sb[:, :], a["smask"][bass.ds(z, 1), :, :].rearrange("z p c -> p (z c)")).then_inc(mask_in, 16)

            units.skip(2, 2)
            for g in range(3):
                units.skip(2, 2, 2, 2, 4, 4)
                units.all_free(sp)
                w = min(ROWS[g], SEQ)
                store(a["okp"][g], XA[:, 4:8, PADS - w:PADS])
                if g == 0:
                    store(a["ovp"][g], V[:, 7, :])
                elif g == 1:
                    for phase in range(4):
                        store(a["ovp"][g].rearrange("(n r) c -> r n c", r=4)[phase], V[:, 2 * phase + 1, :])
                else:
                    for t in range(8):
                        store(a["ovp"][g].rearrange("(n r) c -> r n c", r=8)[t], V[:, t, :])
                store(a["oks_new"][g], XA[:, 4:8, 0:SAMPLE])
                store(a["ovs_new"][g], V[0:SAMPLE, 8, :])
                sp.dma_start(qk_keep[:, g, :, :], XA[:, :, 0:SAMPLE]).then_inc(kept, 16)
                sp.dma_start(v_keep[:, g, :], V[0:SAMPLE, 8, :]).then_inc(kept, 16)
                keeps.add(32)

                def tile(i, nk, before, after, g=g):
                    sp.wait_ge(o_made, made.add())
                    row = og[g]
                    if g == 0:
                        sp.dma_start(row[bass.ds(i * P, P), :], o_st[:, 0:ROW]).then_inc(o_out, 16)
                        oout.add(16)
                    elif g == 1:
                        dst = row.rearrange("(h n r) c -> h r n c", h=2, r=4)[i[1], bass.ds(i[0], 1), :, :]
                        sp.dma_start(dst.rearrange("r n c -> (r n) c"), o_st[:, 0:ROW]).then_inc(o_out, 16)
                        oout.add(16)
                    else:
                        dst = row.rearrange("(n r) c -> r n c", r=8)[bass.ds(i, 1), :, :]
                        sp.dma_start(dst.rearrange("r n c -> (r n) c"), o_st[:, 0:ROW]).then_inc(o_out, 16)
                        oout.add(16)

                if g < 2:
                    over_tiles(sp, g, {made: 1, oout: 16}, tile)
                else:
                    for t in range(8):
                        tile(t, 1, None, None)
                        if t in (0, 2):
                            load_keys(t // 2, t // 2)
                        elif t == 4:
                            load_mask(0)
                            load_values(0, 0)
                sp.wait_ge(out_done, stored.at)
                feed_to((17, 23, 23)[g])

            sp.wait_ge(kept, keeps.at)
            sp.wait_ge(o_out, oout.at)
            sp.wait_ge(pv_mm, N_A_STEPS)
            sp.dma_start(tiles(qs, 3).rearrange("p g (j t) -> p g j t", j=4), qk_keep[:, :, 0:4, :]).then_inc(sx_in, 16)
            sp.dma_start(tiles(ks_new, 3).rearrange("p g (j t) -> p g j t", j=4),
                         qk_keep[:, :, 4:8, :]).then_inc(sx_in, 16)
            sp.dma_start(vs_new[0:SAMPLE, :], v_keep.rearrange("t g c -> t (g c)")).then_inc(sx_in, 16)
            used, smm, masked = Count(kv_used), Count(ss_mm), Count(ss_masked)
            load_values(1, 1)

            def next_keys(z):
                for b in range(2):
                    sp.wait_ge(ss_mm, smm.add())
                    load_keys(z * 2 + b, b)
                sp.wait_ge(ss_masked, masked.add())
                load_mask(z)

            def next_values(z):
                for b in range(2):
                    sp.wait_ge(kv_used, used.add())
                    load_values(z * 2 + b, b)

            next_keys(1)
            with turns(sp, 2, {used: 2, smm: 2, masked: 1}) as z:
                next_keys(z + 2)
                next_values(z + 1)
            next_values(3)

            sp.wait_ge(kv_used, 8)
            sp.wait_ge(ss_norm, 4)
            sp.wait_ge(spv_taken, 4)
            sp.dma_start(sc[:, 0:3 * ST], a["ssm"]).then_inc(ssm_in, 16)
            sp.dma_start(h0[:, :], a["h0"]).then_inc(ssm_in, 16)
            for b in range(4):
                sp.dma_start((b_blk + c_blk)[b][:, :], a["bmat"][b]).then_inc(b_in, 16)
            for z in range(2):
                if z == 0:
                    sp.wait_ge(b_used, 1)
                else:
                    sp.wait_ge(h_used, 8)
                for k in range(2):
                    for t, m in ((b_blk[k], "bmat"), (c_blk[k], "cmat")):
                        sp.dma_start(t[:, :], a[m][z * 2 + k]).then_inc(blk_in, 16)
            sp.wait_ge(state_out, 1)
            store(a["st_s"], h0[:, :])
            store(a["st_p"], sc[:, V_T1 * ST:(V_T2 + 1) * ST])

            sp.wait_ge(out_done, stored.at)
            sp.wait_ge(lo_made, LO_GLU)
            ogu = Count(comb_made)
            for t in range(2):
                sp.dma_start(tiles(og_in, 2)[:, t, :].rearrange("p (g c) -> p g c", g=3),
                             og[:, P * t:P * t + P, :].rearrange("g p c -> p g c")).then_inc(og_loaded[t], 16)
            with turns(sp, 3, {ogu: 2}) as t:
                for b in range(2):
                    sp.wait_ge(comb_made, ogu.add())
                    sp.dma_start(tiles(og_in, 2)[:, b, :].rearrange("p (g c) -> p g c", g=3),
                                 og[:, bass.ds(t * 256 + 256 + P * b, P), :].rearrange("g p c -> p g c"))\
                        .then_inc(og_loaded[b], 16)

            for layer in range(2):
                if layer == 0:
                    sp.wait_ge(lo_made, LO_MIXED_A)
                    sp.dma_start(XD, a["xT"]).then_inc(x_in, 16)
                else:
                    sp.wait_ge(lo_made, LO_MIXED_C)
                    sp.wait_ge(x_out, xout.at)
                    sp.dma_start(XD, x_keep).then_inc(x_in, 16)
                xin.add(16)
                feed_to(W_OUT[layer] + 7)
                sp.wait_ge(x_made, xm.add(8))
                sp.dma_start(x_keep, XA).then_inc(x_out, 16)
                xout.add(16)

                def copy_batch(n, layer=layer):
                    s = bass.ds(n, 1)
                    for g in ((2,) if layer == 0 else (0, 1)):
                        r = ROWS[g]
                        src = a["kt"][g].rearrange("n p (j r) -> n p j r", j=4)
                        store(a["oks"][g][s], src[s] if g == 2 else src[s, :, :, NS:r])
                        store(a["ovs"][g][s, 0:r - NS, :], a["v"][g][s, NS:r, :])
                    if layer == 1:
                        store(a["okc_s"][s, :, :, 0:ROWS_C - NS],
                              a["ktc"].rearrange("n p (j r) -> n p j r", j=2)[s, :, :, NS:ROWS_C])
                        store(a["ovc_s"][s, 0:ROWS_C - NS, :], a["vc"][s, NS:ROWS_C, :])

                n_copies = 16 * (2 if layer == 0 else 6)
                base = fed[0]
                with turns(sp, 7, {spl: 4, stored: n_copies}) as i:
                    for k in range(4):
                        feed(i * 4 + base + k)
                    copy_batch(i)
                fed[0] += 28
                copy_batch(7)
                feed_to(W_PLE[layer] + 3)
                sp.wait_ge(slot_done, W_PLE[layer])
                sp.wait_ge(x_out, xout.at)
                sp.dma_start(XD, x_keep).then_inc(x_in, 16)
                xin.add(16)
                xm.add(8)
                if layer == 0:
                    feed_to(W_GATE[0] + 7)
                    sp.wait_ge(x_made, xm.add(8))
                    sp.dma_start(x_keep, XA).then_inc(x_out, 16)
                    xout.add(16)
                    feed_to(W_VC + 4)
                    sp.wait_ge(slot_done, W_VC + 1)
                    sp.wait_ge(free[0], UNITS_AT[W_VC + 1] // 2)
                    sp.wait_ge(free[1], UNITS_AT[W_VC + 1] // 2)
                    store(a["okc_p"], KCT[:, :, PADS - ROWS_C:PADS])
                    store(a["ovc_p"], VC[:, 7, :])
                    store(a["okc_new"], KCT[:, :, 0:SAMPLE])
                    store(a["ovc_new"], VC[0:SAMPLE, 8, :])
                    sp.wait_ge(o_made, made.add(8))
                    sp.dma_start(ktc_sb[:, :].rearrange("p (n c) -> p n c", n=NB), a["ktc"].rearrange("n p c -> p n c")).then_inc(sx_in, 16)
                    sp.dma_start(vc_in[:, :].rearrange("p (n c) -> p n c", n=NB), a["vc"].rearrange("n p c -> p n c")).then_inc(sx_in, 16)
                    sp.dma_start(cm_sb[:, :], a["cmask"]).then_inc(sx_in, 16)
                    sp.wait_ge(out_done, stored.at)
                else:
                    feed_to(N_SLOTS)
                    sp.wait_ge(x_made, xm.add(8))
                    store(a["yT"], XA)
            sp.wait_ge(out_done, stored.at)
            sp.wait_ge(x_out, xout.at)
            sp.wait_ge(o_out, oout.at)
            sp.wait_ge(kept, keeps.at)

        @block.gpsimd
        def _(pool):
            raw, hi, done = Count(raw_in), Count(hi_made), Count(slot_done)

            def split_slot(b, wait_free=True):
                pool.wait_ge(raw_in, raw.add(16))
                if wait_free:
                    pool.wait_ge(slot_done, done.add())
                pool.tensor_tensor(w_hi[b][:, :], w_raw[:, :], ones[:, 0:1].broadcast_to([P, SLOT]), ALU.mult).then_inc(hi_made, 1)
                pool.wait_ge(hi_made, hi.add())
                pool.tensor_tensor(w_lo[b][:, :], w_raw[:, :], w_hi[b][:, :].bitcast(F32), ALU.subtract).then_inc(split, 1)

            pool.wait_ge(const_in, 64)
            split_slot(0, wait_free=False)
            split_slot(1, wait_free=False)
            with turns(pool, W_GLU // 2, {raw: 32, hi: 2, done: 2}):
                split_slot(0)
                split_slot(1)

            prod, xsm, hus, pown, sim = (Count(s) for s in (level_prod, xs_made, h_used, pool_own, si_made))

            def level(t, k):
                n = 1 << k
                pool.wait_ge(level_prod, prod.add())
                pool.tensor_tensor(tr[t][:, n:2 * n], tp[:, 0:n], tp[:, 512:512 + n], ALU.subtract)
                pool.tensor_tensor(ti[t][:, n:2 * n], tp[:, 1024:1024 + n], tp[:, 1536:1536 + n], ALU.add).then_inc(level_made, 1)

            def block_of(tables):
                for t in range(4):
                    S = si[t % 2]
                    pool.wait_ge(xs_made, xsm.add())
                    pool.wait_ge(h_used, hus.at if t < 2 else hus.add())
                    pool.tensor_tensor(S[:, :], xs1[:, :], ti[t][:, :], ALU.mult)
                    if t < tables:
                        level((t + 2) % 4, 6)
                    pool.wait_ge(si_made, sim.at)
                    sim.add()
                    pool.tensor_tensor(sj[:, :], xs2[:, :], tr[t][:, :], ALU.mult).then_inc(pool_own, 1)
                    if t < tables:
                        level((t + 2) % 4, 7)
                    pool.wait_ge(pool_own, pown.add())
                    pool.tensor_tensor(S[:, :], S[:, :], sj[:, :], ALU.add).then_inc(si_made, 1)
                    if t < tables:
                        level((t + 2) % 4, 8)
                    if t < tables:
                        level((t + 2) % 4, 9)
                hus.add(2)

            for t in range(2):
                for k in range(6, 10):
                    level(t, k)
            with turns(pool, 3, {prod: 16, xsm: 4, hus: 4, pown: 4, sim: 4}):
                block_of(4)
            block_of(2)

            with turns(pool, (N_SLOTS - W_GLU - 3) // 2, {raw: 32, hi: 2, done: 2}):
                split_slot(0)
                split_slot(1)
            split_slot(0)

        @block.tensor
        def _(pe):
            u, spl = Units(), Count(split)
            sqm, rms, lo, added = Count(sq_made), Count(sums_read), Count(lo_made), Count(part_added)
            n_q, n_s, n_mask, n_exp, n_ptt, n_pt, n_pv, n_o = (
                Count(s) for s in (q_ready, s_mm, s_masked, exp_made, pt_taken, pt_mm, pv_mm, o_made))

            def late(sem_, value):
                if not (isinstance(value, int) and value <= 0):
                    pe.wait_ge(sem_, value)

            def sums():
                pe.wait_ge(free[0], u.free[0].at)
                for kc in range(KC):
                    pe.wait_ge(sq_made, sqm.add())
                    for c in range(3):
                        mm = pe.matmul(UNIT[0][:, c, :], ones[:, :], TMP[:, kc % 2, c * CH:(c + 1) * CH],
                                       start=kc == 0, stop=kc == KC - 1)
                    mm.then_inc(sq_used, 1)
                pe.wait_ge(sums_read, rms.add())

            def whole_sums():
                pe.wait_ge(part_added, added.add(8))
                pe.wait_ge(free[0], u.free[0].at)
                for c in range(3):
                    mm = pe.matmul(UNIT[0][:, c, :], ones[:, :], rs[:, c * CH:(c + 1) * CH], start=True, stop=True)
                mm.then_inc(whole_sum, 1)
                pe.wait_ge(sums_read, rms.add())

            def halves(slot, kcs):
                return [t[slot % 2][:, 0:2048].rearrange("p (k c) -> p k c", k=kcs) for t in (w_hi, w_lo)]

            def slot_ready():
                pe.wait_ge(split, spl.add())

            def features(slot, XH, XL, kcs=KC, n_units=2, done=1, arriving=False):
                WH, WL = halves(slot, kcs)
                for m in range(n_units):
                    cols = slice(m * P, m * P + P)
                    s = m % 2
                    late(free[s], u.free[s].at)
                    u.free[s].add()
                    for kc in range(kcs):
                        if arriving and m == 0:
                            pe.wait_ge(lo_made, lo.add())
                        for w, x in ((WH, XH), (WL, XH), (WH, XL)):
                            first, last = kc == 0 and w is WH and x is XH, kc == kcs - 1 and x is XL
                            for c in range(3):
                                mm = pe.matmul(UNIT[s][:, c, :], w[:, kc, cols], x[:, kc, c * CH:(c + 1) * CH],
                                               start=first, stop=last)
                    if m == n_units - 1:
                        mm.then_inc(slot_done, done)
                        u.done.add(done)
                    else:
                        mm.then_inc(full, 1)
                        u.full.add()

            def values(slot, g):
                WH, WL = halves(slot, KC)
                for n, tt in enumerate(((0, 1, 2), (3, 4, 5), (6, 7), (8,))):
                    s = n % 2
                    pe.wait_ge(free[s], u.free[s].at)
                    u.free[s].add()
                    for c, t in enumerate(tt):
                        pick = (lambda x: x[:, :, 0:P]) if t == 8 else prompt_cols(g, divmod(t, 2) if g == 1 else t)
                        XH, XL = pick(HH), pick(HL)
                        for kc in range(KC):
                            for x, w in ((XH, WH), (XH, WL), (XL, WH)):
                                mm = pe.matmul(psum[:, 3 * s + c, 0:256], x[:, kc], w[:, kc, :],
                                               start=kc == 0 and x is XH and w is WH, stop=kc == KC - 1 and x is XL)
                    if n == 3:
                        mm.then_inc(slot_done, 1)
                        u.done.add()
                    else:
                        mm.then_inc(full, 1)
                        u.full.add()

            def slot_pairs(n, first, XH, XL, arriving=False):
                if arriving:
                    for k in range(2):
                        slot_ready()
                        features(first + k, XH, XL, arriving=k == 0)
                    n -= 1
                with turns(pe, n, {spl: 2, **u.per(2, 2)}):
                    for k in range(2):
                        slot_ready()
                        features(first + k, XH, XL)

            def attend(g, heads, keys, vals):
                steps, per_kv = heads // 2, 1 if heads == H_A else 4
                staged = QST if heads == H_A else QCST

                def tile(i, nk, before, after):
                    K = key_cols(g, i, nk)(keys)

                    def scores(k):
                        pe.wait_ge(q_ready, n_q.add())
                        m = n_mask.add()
                        late(s_masked, m - 2)
                        for hh in range(2):
                            h = 2 * k + hh
                            kt = h // 2 if per_kv == 1 else h // 8
                            mm = pe.matmul(psum[:, k % 2, hh * 256:hh * 256 + nk * P], staged[:, h, :], K[:, kt],
                                           start=True, stop=True)
                        mm.then_inc(s_mm, 1)

                    def turn(k, nk):
                        pe.wait_ge(exp_made, n_exp.add())
                        m = n_ptt.add()
                        late(pt_taken, m - 2)
                        for hh in range(2):
                            for kb in range(nk):
                                o = (k % 2) * 512 + hh * 256 + kb * P
                                mm = pe.transpose(psum[:, 2 + k % 2, hh * 256 + kb * P:hh * 256 + kb * P + P],
                                                  pr[:, o:o + P], ident[:, :])
                        mm.then_inc(pt_mm, 1)

                    def weigh(k, i, nk):
                        if k == 0:
                            late(o_made, n_o.add() - 1)
                        pe.wait_ge(pt_taken, n_pv.add())
                        for hh in range(2):
                            h = 2 * k + hh
                            c = (h // per_kv) * HEAD_DIM
                            for kb in range(nk):
                                t = value_tile(g, i) - (nk - 1 - kb)
                                o = (k % 2) * 512 + hh * 256 + kb * P
                                mm = pe.matmul(psum[:, 4 + h // 8, (h % 8) * HEAD_DIM:(h % 8 + 1) * HEAD_DIM],
                                               pt[:, o:o + P], vals[:, bass.ds(t, 1), c:c + HEAD_DIM],
                                               start=kb == 0, stop=kb == nk - 1)
                        mm.then_inc(pv_mm, 1)

                    def outputs_turned():
                        pe.wait_ge(o_made, n_o.at)
                        pe.wait_ge(lo_made, lo.at)
                        for k in range(KC):
                            mm = pe.transpose(psum[:, 6 + k // 4, (k % 4) * P:(k % 4 + 1) * P],
                                              on_c[:, k * P:(k + 1) * P], ident[:, :])
                        mm.then_inc(turned, 1)
                        lo.add()

                    for k in range(steps):
                        scores(k)
                        if k >= 2:
                            turn(k - 2, nk)
                        elif before:
                            turn(steps - 2 + k, before[1])
                        if k >= 3:
                            if k == 3 and before and heads == H_C:
                                outputs_turned()
                            weigh(k - 3, i, nk)
                        elif before:
                            weigh(steps - 3 + k, *before)
                    if not after:
                        turn(steps - 2, nk)
                        weigh(steps - 3, i, nk)
                        turn(steps - 1, nk)
                        weigh(steps - 2, i, nk)
                        weigh(steps - 1, i, nk)
                        if heads == H_C:
                            outputs_turned()

                per = {n_q: steps, n_mask: steps, n_exp: steps, n_ptt: steps, n_pv: steps, n_o: 1}
                if heads == H_C:
                    per[lo] = 1
                over_tiles(pe, g, per, tile)
                pe.wait_ge(o_made, n_o.at)

            pe.wait_ge(const_in, 64)
            whole_sums()
            for k in range(2):
                slot_ready()
                features(W_U + k, HH, HL, arriving=k == 0)
            for g in range(3):
                slot_pairs(2, W_QKV + 6 * g, HH, HL)
                for k in range(2):
                    slot_ready()
                    values(W_QKV + 6 * g + 4 + k, g)
                u.all_free(pe)
                attend(g, H_A, XA[:, 4:8, :], V)

            pe.wait_ge(sx_in, 48)
            pe.wait_ge(o_made, n_o.at)
            KSN, VSN = tiles(ks_new, 12), tiles(vs_new, 3)
            QB, PT = qb[:, :].rearrange("p (g c) -> p g c", g=3), tiles(sp_t, 12)
            qbm, kin, vin, ssm_, sse, stt_, spt_ = Count(qb_made), [Count(s) for s in k_in], [Count(s) for s in v_in], Count(ss_masked), Count(ss_norm), Count(st_taken), Count(spv_taken)
            def pair_scores():
                for b in range(2):
                    KT_ = kt_sb[b]
                    pe.wait_ge(qb_made, qbm.add())
                    pe.wait_ge(k_in[b], kin[b].add(48))
                    if b == 0:
                        late(ss_masked, ssm_.add() - 1)
                    rows = slice(64 * b, 64 * b + 64)

                    def score(out, g, keys):
                        for j in range(4):
                            mm = pe.matmul(out, QB[:, g, j * 64:j * 64 + 64], keys[j], start=j == 0, stop=j == 3)
                        return mm

                    off = 0
                    for g in range(3):
                        kk = KT_[:, off:off + 4 * SEEN[g]].rearrange("p (j r) -> p j r", j=4)
                        off += 4 * SEEN[g]
                        score(psum[rows, g, 0:SEEN[g]], g, [kk[:, j, :] for j in range(4)])
                        mm = score(psum[rows, 0, P + 64 * g:P + 64 * g + 64], g, [KSN[:, 4 * g + j, :] for j in range(4)])
                    mm.then_inc(ss_mm, 1)

            def pair_turned():
                pe.wait_ge(ss_norm, sse.add())
                pe.wait_ge(st_taken, stt_.add() - 1)
                for n in range(9):
                    o = 0 if n == 0 else 320 + (n - 1) * P
                    out = psum[:, 4 + n // 4, (n % 4) * P:(n % 4 + 1) * P] if n < 8 else psum[:, 3, 384:512]
                    pe.transpose(out, s_sb[:, o:o + P], ident[:, :])
                for g in range(3):
                    mm = pe.transpose(psum[0:64, 3, g * P:g * P + P], s_sb[:, P + 64 * g:P + 64 * g + 64], ident[:, :])
                mm.then_inc(st_mm, 1)
                pe.wait_ge(st_taken, stt_.at)

            def pair_outputs():
                pe.wait_ge(spv_taken, spt_.add() - 1)
                for b in range(2):
                    pe.wait_ge(v_in[b], vin[b].add(208))
                    vb = tiles((va, v_sb)[b], 9)
                    for j in range(4):
                        out = psum[:, 6, b * 64 + j * 16:b * 64 + j * 16 + 16]
                        cols = slice(b * 64 + j * 16, b * 64 + j * 16 + 16)
                        for g in range(3):
                            pe.matmul(out, VSN[0:64, g, j * P:(j + 1) * P], PT[0:64, g, cols], start=g == 0, stop=False)
                        for n in range(9):
                            mm = pe.matmul(out, vb[:, n, j * P:(j + 1) * P], PT[:, 3 + n, cols], start=False, stop=n == 8)
                    mm.then_inc(kv_used, 1)

            pair_scores()
            with turns(pe, 3, {qbm: 2, kin[0]: 48, kin[1]: 48, vin[0]: 208, vin[1]: 208, ssm_: 1, sse: 1, stt_: 1, spt_: 1}):
                pair_turned()
                pair_scores()
                pair_outputs()
            pair_turned()
            pair_outputs()

            pe.wait_ge(spv_taken, 4)
            bi, vd, ym, srm, sim, bus, hus = (Count(s) for s in (blk_in, vec_dve, y_made, sr_made, si_made, bu_used, h_used))
            def by_tile(t):
                return t[:, :].rearrange("p (t c s) -> p t c s", t=4, c=2)

            pe.wait_ge(b_in, 64)
            for b in range(4):
                B = by_tile((b_blk + c_blk)[b])
                for c in range(2):
                    for t in range(4):
                        mm = pe.matmul(psum[:, b, c * 256 + t * 64:c * 256 + t * 64 + 64], B[:, t, c, :],
                                       U[:, b:b + 1, 0:SAMPLE], start=True, stop=True)
            mm.then_inc(b_used, 1)
            HSR, HSI = tiles(hs_re, 16), tiles(hs_im, 16)
            with turns(pe, 2, {bi: 64, vd: 1, ym: 2, srm: 8, sim: 8, bus: 8}) as z:
                pe.wait_ge(blk_in, bi.add(64))

                def inputs(k):
                    b, t = divmod(k, 4)
                    pe.wait_ge(bu_used, bus.add())
                    for c in range(2):
                        for n in range(2):
                            mm = pe.matmul(psum[:, 2 * c + n, :], by_tile(b_blk[b])[:, t, c, :],
                                           U[:, bass.ds(z * 2 + b, 1), SAMPLE + n * 512:SAMPLE + n * 512 + 512],
                                           start=True, stop=True)
                    mm.then_inc(bu_mm, 1)

                def outputs(k):
                    b, t = divmod(k, 4)
                    if t == 0:
                        pe.wait_ge(y_made, ym.at)
                        ym.add()
                    pe.wait_ge(sr_made, srm.add())
                    pe.wait_ge(si_made, sim.add())
                    for n in range(2):
                        for c, H in ((0, sr[t % 2]), (1, si[t % 2])):
                            mm = pe.matmul(psum[:, 4 + n, :], by_tile(c_blk[b])[:, t, c, :], H[:, n * 512:n * 512 + 512],
                                           start=t == 0 and c == 0, stop=t == 3 and c == 1, skip_group_check=True)
                    mm.then_inc(h_used, 1)

                inputs(0)
                pe.wait_ge(hs_made, 1)
                pe.wait_ge(y_made, ym.at)
                for b in range(2):
                    for t in range(4):
                        for c, H in ((0, HSR), (1, HSI)):
                            mm = pe.matmul(psum[:, 6, b * SAMPLE:(b + 1) * SAMPLE], by_tile(c_blk[b])[:, t, c, :],
                                           H[:, bass.ds(z * 8 + b * 4 + t, 1), :],
                                           start=t == 0 and c == 0, stop=t == 3 and c == 1)
                mm.then_inc(ys_mm, 1)
                inputs(1)
                pe.wait_ge(vec_dve, vd.add())
                for k in range(8):
                    if k < 6:
                        inputs(k + 2)
                    outputs(k)

            pe.wait_ge(lo_made, lo.add(4))
            slot_ready()
            features(W_GLU, ZH, ZL, kcs=4, n_units=4)
            lo.add(4)

            cmb = Count(comb_made)
            lo.add()
            with turns(pe, 4, {cmb: 2, lo: 2}):
                for b in range(2):
                    pe.wait_ge(comb_made, cmb.add())
                    m = lo.add()
                    pe.wait_ge(lo_made, m - 2)
                    for k in range(4):
                        mm = pe.transpose(psum[:, 6 + b, k * P:k * P + P], c_acc[:, b * 512 + k * P:b * 512 + k * P + P],
                                          ident[:, :])
                    mm.then_inc(turned, 1)

            for layer in range(2):
                if layer == 1:
                    slot_pairs(2, W_QC, HH, HL, arriving=True)
                    slot_ready()
                    features(W_KC, HH, HL)
                    slot_ready()
                    values(W_VC, 0)
                    u.all_free(pe)
                    attend(0, H_C, KCT, VC)
                    pe.wait_ge(sx_in, 48 + 48)
                    pe.wait_ge(qb_made, 9)
                    QS = qc_st[:, :].rearrange("p (n j c) -> p n j c", n=NB, j=2)
                    KS, VS = ktc_sb[:, :].rearrange("p (n j r) -> p n j r", n=NB, j=2), tiles(vc_in, NB)
                    for n in range(NB):
                        o = (n % 2) * SKC
                        for out, keys in ((psum[:, n // 2, o:o + P], [KS[:, n, j] for j in range(2)]),
                                          (psum[:, n // 2, o + P:o + SKC], [KCT[:, j, 0:SAMPLE] for j in range(2)])):
                            for j in range(2):
                                mm = pe.matmul(out, QS[:, n, j, :], keys[j], start=j == 0, stop=j == 1)
                    mm.then_inc(ss_mm, 1)
                    pe.wait_ge(ss_norm, 5)
                    pe.wait_ge(lo_made, lo.at)
                    S, PTC = tiles(cs_s, NB), tiles(cs_t, 16)
                    for n in range(NB):
                        pe.transpose(psum[:, 4 + n // 4, (n % 4) * P:(n % 4 + 1) * P], S[:, n, 0:P], ident[:, :])
                        mm = pe.transpose(psum[0:64, 6 + n // 4, (n % 4) * P:(n % 4 + 1) * P], S[:, n, P:SKC], ident[:, :])
                    mm.then_inc(st_mm, 1)
                    pe.wait_ge(st_taken, 5)
                    for n in range(NB):
                        for j in range(2):
                            out = psum[:, n // 4, (n % 4) * P + j * 64:(n % 4) * P + j * 64 + 64]
                            pe.matmul(out, VS[:, n, j * P:j * P + P], PTC[:, n, j * 64:j * 64 + 64], start=True, stop=False)
                            mm = pe.matmul(out, VC[0:SAMPLE, 8, j * P:j * P + P], PTC[0:64, 8 + n, j * 64:j * 64 + 64],
                                           start=False, stop=True)
                    mm.then_inc(spv_mm, 1)
                    lo.add()
                pe.wait_ge(lo_made, lo.at)
                slot_pairs(2, W_OUT[layer], HH, HL)
                whole_sums()
                sums()
                up = W_FF[layer]

                def ff_up(slot, arriving=False):
                    slot_ready()
                    features(slot, HH, HL, arriving=arriving)
                    lo.add(2)

                def ff_down(slot, h):
                    slot_ready()
                    pe.wait_ge(lo_made, lo.at - (0 if slot == up + 31 else 2))
                    features(slot, HIDH[h], HIDL[h], kcs=2, n_units=8)

                ff_up(up, arriving=True)
                with turns(pe, 7, {spl: 4, lo: 4, **u.per(2, 8, 2, 8)}):
                    ff_up(up + 1)
                    ff_down(up + 2, 0)
                    ff_up(up + 3)
                    ff_down(up + 4, 1)
                ff_up(up + 29)
                ff_down(up + 30, 0)
                ff_down(up + 31, 1)
                whole_sums()
                slot_ready()
                slot_ready()
                s = W_PLE[layer] % 2
                PH, PL = (t[s][:, :].rearrange("p (k c) -> p k c", k=2) for t in (w_hi, w_lo))
                features(W_PLE[layer] + 1, PH, PL, kcs=2, n_units=8, done=2)
                sums()
                slot_pairs(2, W_GATE[layer], HH, HL, arriving=True)
                if layer == 0:
                    sums()

        OUT_G = (64, 64 + 112, 64 + 112 + 176)
        OUT_S5 = OUT_G[2] + 32


        @block.scalar
        def _(act):
            u, squ, lo, scl, rd = Units(), Count(sq_used), Count(lo_made), Count(scaled), Count(sums_read)
            xm, own = Count(x_made), Count(act_own)
            n_s, n_max, n_ptx, n_pt, n_pv, n_o, n_sc = (Count(s) for s in (s_mm, max_made, pt_mm, pt_mm, pv_mm, o_made, w_dif))
            n_turn, n_out = Count(turned), Count(o_out)

            def late(sem_, value):
                if not (isinstance(value, int) and value <= 0):
                    act.wait_ge(sem_, value)

            def squares(ready):
                for kc in range(KC):
                    ready(kc)
                    late(sq_used, squ.add() - 2)
                    act.activation(TMP[:, kc % 2, :], XA[:, kc, :], ACT.Square).then_inc(sq_made, 1)
                act.wait_ge(sq_used, squ.at)
                inverse_rms()

            def inverse_rms():
                act.activation(chunked(rs[:, :]), UNIT[0], ACT.Ln, bias=param[:, C_EPS:C_EPS + 1],
                               scale=1.0 / D_MODEL).then_inc(sums_read, 1)
                act.wait_ge(sums_read, rd.add())
                act.activation(rs[:, :], rs[:, :], ACT.Exp, scale=-0.5).then_inc(inv_made, 1)

            def part(kc, half):
                late(part_added, parts.add() - 2)
                act.activation(TMP[:, half, :], XA[:, kc, :], ACT.Square)\
                    .then_inc(part_made, 1)

            def whole():
                act.wait_ge(whole_sum, wholes.add())
                inverse_rms()

            parts, wholes = Count(part_added), Count(whole_sum)

            def high(dst, src, ready, n):
                act.wait_ge(ready, n)
                act.activation(dst, src, ACT.Copy).then_inc(hi_act, 1)

            def norm_highs():
                for kc in range(KC):
                    high(HH[:, kc, :], TMP[:, kc % 2, :], scaled, scl.add())
                lo.add(8)

            def take(dst, m, last, func=ACT.Copy, **kw):
                u.wait(act, last)
                act.activation(chunked(dst), UNIT[m % 2], func, **kw).then_inc(free[m % 2], 1)
                u.free[m % 2].add()

            def take_pairs(n, buf, first=0):
                with turns(act, n, u.per(2, 2)) as i:
                    for k in range(4):
                        take(buf[:, bass.ds(i * 4 + k + first, 1), :].rearrange("p a t -> p (a t)"), k, k % 2 == 1)

            def take_values(buf, cols):
                for n, (t, k) in enumerate(((0, 3), (3, 3), (6, 2), (8, 1))):
                    rows = slice(0, SAMPLE) if n == 3 else slice(0, P)
                    u.wait(act, n == 3)
                    s = n % 2
                    act.activation(buf[rows, t:t + k, cols], psum[rows, 3 * s:3 * s + k, 0:256], ACT.Copy).then_inc(free[s], 1)
                    u.free[s].add()

            def attend(g, heads):
                steps = heads // 2

                staged = QST if heads == H_A else QCST

                def stage(i, k):
                    late(s_mm, n_s.add() - steps)
                    for par in range(2):
                        rows = 64 * (par if heads == H_A else (k // 2) % 2)
                        q = prompt_cols(g, i)(XA[:, k:k + 1, :])[64 * par:64 * par + 64]
                        mm = act.activation(staged[rows:rows + 64, 2 * k + par:2 * k + par + 1, :], q, ACT.Copy,
                                            scale=HEAD_DIM ** -0.5)
                    mm.then_inc(q_ready, 1)

                def tile(i, nk, before, after):
                    if not before:
                        for k in range(steps):
                            stage(i, k)

                    def exps(k):
                        act.wait_ge(max_made, n_max.add())
                        late(pt_mm, n_ptx.add() - 2)
                        for hh in range(2):
                            h = 2 * k + hh
                            o = (k % 2) * 512 + hh * 256
                            mm = act.activation(pr[:, o:o + nk * P], sm[:, o:o + nk * P], ACT.Exp, bias=stat[:, h:h + 1],
                                                accum_out=stat[:, 16 + h:17 + h])
                        mm.then_inc(exp_made, 1)

                    def turned_out(k, nk):
                        act.wait_ge(pt_mm, n_pt.add())
                        late(pv_mm, n_pv.add() - 2)
                        o = (k % 2) * 512
                        act.activation(pt[:, o:o + 512].rearrange("p (h c) -> p h c", h=2)[:, :, 0:nk * P],
                                       psum[:, 2 + k % 2, :].rearrange("p (h c) -> p h c", h=2)[:, :, 0:nk * P],
                                       ACT.Copy).then_inc(pt_taken, 1)

                    def outputs_high(i):
                        high(HH[:, :, bass.ds(i * P + SAMPLE, P)],
                             psum[:, 6:8, :].rearrange("p b (k c) -> p (b k) c", c=P), turned, n_turn.add())

                    for k in range(steps):
                        exps(k)
                        if k >= 2:
                            turned_out(k - 2, nk)
                        elif before:
                            turned_out(steps - 2 + k, before[1])
                        if k == 4 and before and heads == H_C:
                            outputs_high(before[0])
                        if k and after:
                            stage(after[0], k - 1)
                    if heads == H_C:
                        act.wait_ge(w_dif, n_sc.add())
                        act.activation(stat[:, 48:64], stat[:, 32:48], ACT.Exp).then_inc(w_exp, 1)
                    if after:
                        stage(after[0], steps - 1)
                    else:
                        turned_out(steps - 2, nk)
                        turned_out(steps - 1, nk)
                        if heads == H_C:
                            outputs_high(i)

                per = {n_s: steps, n_max: steps, n_ptx: steps, n_pt: steps, n_pv: steps}
                if heads == H_C:
                    per |= {n_sc: 1, n_turn: 1}
                over_tiles(act, g, per, tile)

            for kc in range(KC):
                act.wait_ge(*((x_half, 16) if kc < 4 else (x_in, 16)))
                part(kc, kc % 2)
            act.wait_ge(const_in, 64)
            whole()
            norm_highs()
            for m in range(4):
                take(U[:, m, :], m, m % 2 == 1)
            act.wait_ge(lo_made, lo.at)
            act.wait_ge(zeroed, 1)
            for g in range(3):
                if g:
                    act.wait_ge(out_done, OUT_G[g - 1])
                    act.wait_ge(kept, 32 * g)
                take_pairs(2, XA)
                for k in range(2):
                    take_values(V, slice(256 * k, 256 * k + 256))
                u.all_free(act)
                attend(g, H_A)

            smx, stm, kvu = Count(ss_max), Count(st_mm), Count(kv_used)
            PT = tiles(sp_t, 12)
            with turns(act, 4, {smx: 1, stm: 1, kvu: 2}):
                act.wait_ge(ss_max, smx.add())
                act.activation(s_sb[:, :], s_sb[:, :], ACT.Exp, bias=sstat[:, 0:1], accum_out=sstat[:, 1:2]).then_inc(ss_exp, 1)
                act.wait_ge(st_mm, stm.add())
                act.wait_ge(kv_used, kvu.at)
                kvu.add(2)
                act.activation(PT[0:64, 0:3, :], psum[0:64, 3, 0:384].rearrange("p (g c) -> p g c", g=3), ACT.Copy)
                act.activation(PT[:, 3:11, :], psum[:, 4:6, :].rearrange("p b (n c) -> p (b n) c", c=P), ACT.Copy)
                act.activation(PT[:, 11, :], psum[:, 3, 384:512], ACT.Copy).then_inc(st_taken, 1)

            def vec(v):
                return sc[:, v * ST:(v + 1) * ST]

            act.wait_ge(ssm_in, 32)
            act.activation(vec(V_DT), vec(V_DT), ACT.Exp).then_inc(vec_act, 1)
            act.wait_ge(vec_arg, 1)
            act.activation(vec(V_R), vec(V_X), ACT.Exp)
            act.activation(vec(V_SIN), vec(V_K), ACT.Sin)
            act.activation(vec(V_COS), vec(V_COS), ACT.Sin).then_inc(vec_act, 1)

            BT, TP = bt[:, :].rearrange("p (c t l) -> p c t l", c=2, t=ST), tiles(tp, 4)
            SC = tiles(sc, N_VEC)
            srm, sim, lev = (Count(s) for s in (sr_made, si_made, level_made))

            def table(n, t):
                R_, I_ = tr[t], ti[t]
                act.activation(R_[:, 0:64], BT[:, 0, bass.ds(n, 1), :].rearrange("p a l -> p (a l)"), ACT.Copy)
                act.activation(I_[:, 0:64], BT[:, 1, bass.ds(n, 1), :].rearrange("p a l -> p (a l)"), ACT.Copy)\
                    .then_inc(act_own, 1)
                act.wait_ge(act_own, own.add())
                for k in range(6, 10):
                    m = 1 << k
                    act.wait_ge(level_made, lev.at)
                    lev.add()
                    wr, wi = SC[:, V_POW + 2 * k, bass.ds(n, 1)], SC[:, V_POW + 2 * k + 1, bass.ds(n, 1)]
                    for q, (src, w) in enumerate(((R_, wr), (I_, wi), (I_, wr), (R_, wi))):
                        mm = act.activation(TP[:, q, 0:m], src[:, 0:m], ACT.Copy, scale=w)
                    mm.then_inc(level_prod, 1)

            act.wait_ge(powers_made, 1)
            table(0, 0)
            table(1, 1)
            table(2, 2)
            table(3, 3)
            with turns(act, 3, {srm: 4, sim: 4, lev: 16, own: 4}) as b:
                for t in range(4):
                    act.wait_ge(sr_made, srm.add())
                    act.wait_ge(si_made, sim.add())
                    table(b * 4 + 4 + t, t)
            act.wait_ge(y_made, 4)
            act.wait_ge(zeroed, 2)
            for m in range(4):
                act.activation(ZB[:, m, :], ZB[:, m, :], ACT.Gelu_apprx_tanh).then_inc(act_own, 1)
                high(ZH[:, m, :], ZB[:, m, :], act_own, own.add())
            lo.add(4)
            act.wait_ge(out_done, OUT_S5)
            for m in range(4):
                if m >= 2:
                    act.wait_ge(lo_made, lo.at + m - 1)
                take(TMP[:, m % 2, :], m, m == 3, ACT.Sigmoid, bias=param[:, C_GLU + m:C_GLU + m + 1])
                if m:
                    high(HH[:, 3 + m, :], TMP[:, (m - 1) % 2, :], scaled, scl.add())
            high(HH[:, 7, :], TMP[:, 1, :], scaled, scl.add())
            lo.add(4)

            high(HH[:, 0:4, 0:SAMPLE], tiles(oas, 4), spv_taken, 4)
            lo.add()
            with turns(act, 4, {n_sc: 2, n_turn: 2}) as t:
                for b in range(2):
                    act.wait_ge(w_dif, n_sc.add())
                    act.activation(c_w[:, b * 64 + 32:b * 64 + 56], c_w[:, b * 64 + 8:b * 64 + 32], ACT.Exp).then_inc(w_exp, 1)
                for b in range(2):
                    high(HH[:, 0:4, bass.ds(t * 256 + SAMPLE + P * b, P)],
                         psum[:, 6 + b, :].rearrange("p (k c) -> p k c", c=P), turned, n_turn.add())
            lo.add(8)

            for layer in range(2):
                if layer == 1:
                    act.wait_ge(x_out, 32)
                    take_pairs(2, XA)
                    for m in range(2):
                        take(KCT[:, m, :], m, m == 1)
                    take_values(VC, slice(0, 256))
                    u.all_free(act)
                    act.wait_ge(zeroed, 3)
                    attend(0, H_C)
                    lo.add(8)
                    for n in range(NB):
                        act.wait_ge(ss_max, 5)
                        mm = act.activation(tiles(cs_s, NB)[:, n, :], tiles(cs_s, NB)[:, n, :], ACT.Exp,
                                            bias=cstat[:, n:n + 1], accum_out=cstat[:, 8 + n:9 + n])
                    act.activation(cstat[:, 16:24], cstat[:, 0:8], ACT.Exp,
                                   bias=param[:, C_SINKROW:C_SINKROW + 1]).then_inc(ss_exp, 1)
                    act.wait_ge(st_mm, 5)
                    PTC = tiles(cs_t, 16)
                    act.activation(PTC[:, 0:8, :], psum[:, 4:6, :].rearrange("p b (n c) -> p (b n) c", c=P), ACT.Copy)
                    act.activation(PTC[0:64, 8:16, :], psum[0:64, 6:8, :].rearrange("p b (n c) -> p (b n) c", c=P),
                                   ACT.Copy).then_inc(st_taken, 1)
                    high(HH[:, :, 0:SAMPLE], tiles(ocs, 8), spv_taken, 5)
                    lo.add()
                act.wait_ge(lo_made, lo.at)
                for m in range(8):
                    take(XA[:, m, :], m, m % 2 == 1)
                    act.wait_ge(free[m % 2], u.free[m % 2].at)
                    part(m, m % 2)
                whole()

                def ready_r(kc):
                    act.wait_ge(free[kc % 2], u.free[kc % 2].at - 3 + kc // 2)

                def ready_x(kc):
                    act.wait_ge(x_made, xm.add())

                squares(ready_x)
                norm_highs()

                def ff_up(h):
                    for m in range(2):
                        act.wait_ge(lo_made, lo.at - 1 + m)
                        take(TMP[:, m, :], m, m == 1, ACT.Relu)
                    for m in range(2):
                        high(HIDH[h][:, m, :], TMP[:, m, :], scaled, scl.add())
                    lo.add(2)

                ff_up(0)
                with turns(act, 7, {lo: 4, scl: 4, **u.per(2, 8, 2, 8)}):
                    ff_up(1)
                    u.skip(8)
                    ff_up(0)
                    u.skip(8)
                ff_up(1)
                u.skip(8, 8)
                act.wait_ge(lo_made, lo.at)
                for kc in range(KC):
                    ready_r(kc)
                    part(kc, kc % 2)
                whole()
                for m in range(8):
                    act.wait_ge(x_made, xm.at + m + 1)
                    if m == 7:
                        u.done.add()
                    take(XD[:, m, :], m, m == 7)
                squares(ready_x)
                norm_highs()
                act.wait_ge(lo_made, lo.at)
                for m in range(8):
                    if m >= 2:
                        act.wait_ge(x_made, xm.at + m - 1)
                    take(TMP[:, m % 2, :], m, m % 2 == 1, ACT.Sigmoid)
                if layer == 0:
                    act.wait_ge(x_made, xm.at + 8)
                    squares(ready_x)
                    norm_highs()

        @block.vector
        def _(dve):
            u, lo, hi, inv_, own = Units(), Count(lo_made), Count(hi_act), Count(inv_made), Count(dve_own)
            xin = Count(x_in)
            xin.add(16)
            n_s, n_exp, n_pv, n_out, n_we, n_turn = (Count(s) for s in (s_mm, exp_made, pv_mm, o_out, w_exp, turned))

            def step(ins):
                ins.then_inc(dve_own, 1)
                dve.wait_ge(dve_own, own.add())

            def late(sem_, value):
                if not (isinstance(value, int) and value <= 0):
                    dve.wait_ge(sem_, value)

            def copy(dst, src):
                return dve.tensor_scalar(dst, src, 1.0, None, ALU.mult)

            def low(dst, src, high_):
                dve.wait_ge(hi_act, hi.add())
                dve.tensor_tensor(dst, src, high_.bitcast(F32), ALU.subtract).then_inc(lo_made, 1)
                lo.add()

            def clear_rs():
                dve.wait_ge(lo_made, lo.at)
                step(dve.memset(rs[:, :], 0.0))

            def add_part(half):
                dve.wait_ge(part_made, pm.add())
                dve.tensor_tensor(rs[:, :], rs[:, :], TMP[:, half, :], ALU.add).then_inc(part_added, 1)
                dve.wait_ge(part_added, pa.add())

            pm, pa = Count(part_made), Count(part_added)

            def inverse():
                dve.wait_ge(inv_made, inv_.add())

            def normalise(layer, kind):
                inverse()
                first = lo.at
                for kc in range(KC + 1):
                    if kc < KC:
                        if kc >= 2:
                            dve.wait_ge(lo_made, first + kc - 1)
                        dve.scalar_tensor_tensor(TMP[:, kc % 2, :], XA[:, kc, :], G[:, layer, kind, kc:kc + 1], rs[:, :],
                                                 ALU.mult, ALU.mult).then_inc(scaled, 1)
                    if kc:
                        low(HL[:, kc - 1, :], TMP[:, (kc - 1) % 2, :], HH[:, kc - 1, :])

            def residual(layer, kind):
                inverse()
                dve.wait_ge(x_in, xin.add(16))
                for kc in range(KC + 1):
                    if kc < KC:
                        dve.scalar_tensor_tensor(XA[:, kc, :], XA[:, kc, :], G[:, layer, kind, kc:kc + 1], rs[:, :],
                                                 ALU.mult, ALU.mult).then_inc(dve_own, 1)
                        own.add()
                    if kc:
                        dve.wait_ge(dve_own, own.at - (1 if kc < KC else 0))
                        dve.tensor_tensor(XA[:, kc - 1, :], XA[:, kc - 1, :], XD[:, kc - 1, :], ALU.add).then_inc(x_made, 1)

            def attend(g, heads):
                steps = heads // 2

                def sums_done(last):
                    sums = stat[:, 16:16 + heads]
                    if heads == H_C:
                        dve.wait_ge(w_exp, n_we.add())
                        step(dve.tensor_tensor(sums, sums, stat[:, 48:64], ALU.add))
                    else:
                        dve.wait_ge(exp_made, last)
                        late(o_out, n_out.at)
                        dve.tensor_copy(o_st[:, 512:520], sums)
                        dve.tensor_copy(o_st[:, 520:528], stat[:, 0:8])
                    step(dve.reciprocal(stat[:, 64:64 + heads], sums))

                def outputs():
                    dve.wait_ge(pv_mm, n_pv.add(steps))
                    inv = stat[:, 64:64 + heads].unsqueeze(2).broadcast_to([P, heads, HEAD_DIM])
                    if heads == H_A:
                        dst, n = o_st[:, 0:512], n_out.add(16)
                    else:
                        late(turned, n_turn.at)
                        n_turn.add()
                        dst = on_c[:, :]
                    dve.tensor_tensor(dst.rearrange("p (h d) -> p h d", h=heads),
                                      psum[:, 4:4 + heads // 8, :].rearrange("p b (h d) -> p (b h) d", h=8), inv, ALU.mult)\
                        .then_inc(o_made, 1)

                def outputs_low(i):
                    low(HL[:, :, bass.ds(i * P + SAMPLE, P)], psum[:, 6:8, :].rearrange("p b (k c) -> p (b k) c", c=P),
                        HH[:, :, bass.ds(i * P + SAMPLE, P)])

                def tile(i, nk, before, after):
                    for k in range(steps):
                        dve.wait_ge(s_mm, n_s.add())
                        done = n_exp.at
                        late(exp_made, n_exp.add() - 2)
                        out = sm[:, (k % 2) * 512:(k % 2) * 512 + 512].rearrange("p (h c) -> p h c", h=2)[:, :, 0:nk * P]
                        m = mask[:, 2 * P:3 * P] if g == 2 else mask[:, 2 * P - nk * P:2 * P]
                        dve.tensor_tensor(out, psum[:, k % 2, :].rearrange("p (h c) -> p h c", h=2)[:, :, 0:nk * P],
                                          m.unsqueeze(1).broadcast_to([P, 2, nk * P]), ALU.add).then_inc(s_masked, 1)
                        if k == 0 and before:
                            sums_done(done)
                        dve.wait_ge(s_masked, n_mk.add())
                        red = dve.tensor_reduce(stat[:, 2 * k:2 * k + 2], out, AX, ALU.max, negate=True)
                        if heads == H_C:
                            step(red)
                            red = dve.tensor_tensor(stat[:, 2 * k:2 * k + 2], stat[:, 2 * k:2 * k + 2],
                                                    nsink[:, 2 * k:2 * k + 2], ALU.min)
                        red.then_inc(max_made, 1)
                        if k == 2 and before:
                            outputs()
                        if k == 5 and before:
                            outputs_low(before[0])
                    if heads == H_C:
                        dve.wait_ge(max_made, n_s.at)
                        dve.tensor_tensor(stat[:, 32:48], param[:, C_SINK:C_SINK + 16], stat[:, 0:16], ALU.add).then_inc(w_dif, 1)
                    if not after:
                        sums_done(n_exp.at)
                        outputs()
                        if heads == H_C:
                            outputs_low(i)

                per = {n_s: steps, n_exp: steps, n_mk: steps, n_pv: steps}
                if heads == H_A:
                    per[n_out] = 16
                else:
                    per |= {own: steps + 2, n_we: 1, n_turn: 1, hi: 1, lo: 1}
                if heads == H_A:
                    per[own] = 1
                over_tiles(dve, g, per, tile)

            n_mk = Count(s_masked)

            step(dve.memset(rs[:, :], 0.0))
            for kc in range(KC):
                add_part(kc % 2)
            dve.wait_ge(const_in, 64)
            dve.tensor_scalar(nsink[:, :], param[:, C_SINK:C_SINK + 17], -1.0, None, ALU.mult)
            normalise(0, 0)
            dve.wait_ge(lo_made, lo.at)
            dve.memset(QST, 0.0).then_inc(zeroed, 1)
            u.skip(2, 2)
            for g in range(3):
                u.skip(2, 2, 2, 2, 4, 4)
                attend(g, H_A)

            smk, mi, ssm_, sse, spv, stt_ = (Count(ss_masked), Count(mask_in), Count(ss_mm), Count(ss_exp), Count(kv_used), Count(st_mm))
            QSF, QB = qs[:, :].rearrange("p (g j t) -> p g j t", g=3, j=4), qb[:, :].rearrange("p (g c) -> p g c", g=3)
            dve.wait_ge(sx_in, 48)
            dve.wait_ge(pv_mm, N_A_STEPS)
            step(dve.memset(qb[:, :], 0.0))
            OAS = tiles(oas, 4)
            def pair_queries(z):
                for b in range(2):
                    late(ss_mm, ssm_.at)
                    for par in range(2):
                        rows = slice(64 * par, 64 * par + 64)
                        out = QB[rows].rearrange("p g (j c) -> p g j c", c=80)[:, :, :, 8 * par:8 * par + 8]
                        ins = dve.tensor_scalar(out, QSF[rows, :, :, bass.ds(z * 16 + b * 8, 8)], HEAD_DIM ** -0.5, None, ALU.mult)
                    ins.then_inc(qb_made, 1)
                    ssm_.add()

            def pair_softmax():
                dve.wait_ge(ss_mm, ssm_.at)
                dve.wait_ge(mask_in, mi.add(16))
                late(st_mm, stt_.at)
                stt_.add()
                dve.tensor_tensor(s_sb[:, 0:320], psum[:, 0, 0:320], sm_sb[:, 0:320], ALU.add)
                dve.tensor_tensor(s_sb[:, 320:SK].rearrange("p (b c) -> p b c", b=2), psum[:, 1:3, :],
                                  sm_sb[:, 320:SK].rearrange("p (b c) -> p b c", b=2), ALU.add).then_inc(ss_masked, 1)
                dve.wait_ge(ss_masked, smk.add())
                dve.tensor_reduce(sstat[:, 0:1], s_sb[:, :], AX, ALU.max, negate=True).then_inc(ss_max, 1)
                dve.wait_ge(ss_exp, sse.add())
                step(dve.reciprocal(sstat[:, 2:3], sstat[:, 1:2]))
                dve.tensor_scalar(s_sb[:, :], s_sb[:, :], sstat[:, 2:3], None, ALU.mult).then_inc(ss_norm, 1)

            def pair_taken(z):
                dve.wait_ge(kv_used, spv.add(2))
                for par in range(2):
                    rows = slice(64 * par, 64 * par + 64)
                    src = psum[rows, 6, 0:128].rearrange("p (b j c) -> p b j c", b=2, j=4)[:, :, :, 8 * par:8 * par + 8]
                    out = OAS[rows, :, bass.ds(z * 16, 16)].rearrange("p j (b q) -> p b j q", b=2)
                    ins = copy(out, src)
                    if par == 0:
                        step(ins)
                ins.then_inc(spv_taken, 1)

            pair_queries(0)
            pair_softmax()
            with turns(dve, 3, {ssm_: 2, mi: 16, own: 2, smk: 1, sse: 1, spv: 2, stt_: 1}) as z:
                pair_queries(z + 1)
                pair_softmax()
                pair_taken(z)
            pair_taken(3)

            def vec(v, n=1):
                return sc[:, v * ST:(v + n) * ST]

            def vv(out, x, y, op):
                step(dve.tensor_tensor(vec(out), vec(x), vec(y), op))

            def vs(out, x, s1, op0, s2=None, op1=None):
                step(dve.tensor_scalar(vec(out), vec(x), s1, s2, op0, op1) if op1 else
                     dve.tensor_scalar(vec(out), vec(x), s1, None, op0))

            PI, ROUND = 3.1415925, 12582912.0
            dve.wait_ge(ssm_in, 32)
            dve.wait_ge(vec_act, 1)
            vv(V_X, V_ARE, V_DT, ALU.mult)
            vv(V_TH, V_AIM, V_DT, ALU.mult)
            vs(V_T1, V_TH, 1 / 6.283185307179586, ALU.mult)
            vs(V_T1, V_T1, ROUND, ALU.add)
            vs(V_T1, V_T1, -ROUND, ALU.add)
            step(dve.scalar_tensor_tensor(vec(V_K), vec(V_T1), -6.28125, vec(V_TH), ALU.mult, ALU.add))
            step(dve.scalar_tensor_tensor(vec(V_K), vec(V_T1), -1.9353071795864769e-3, vec(V_K), ALU.mult, ALU.add))
            vs(V_COS, V_K, 1.5707963267948966, ALU.add)
            vs(V_T1, V_COS, PI, ALU.is_gt)
            step(dve.scalar_tensor_tensor(vec(V_COS), vec(V_T1), -6.283185307179586, vec(V_COS), ALU.mult, ALU.add))
            vs(V_COS, V_COS, -PI, ALU.max, PI, ALU.min)
            dve.tensor_scalar(vec(V_K), vec(V_K), -PI, PI, ALU.max, ALU.min).then_inc(vec_arg, 1)
            dve.wait_ge(vec_act, 2)
            vv(V_ABR, V_R, V_COS, ALU.mult)
            vv(V_ABI, V_R, V_SIN, ALU.mult)
            vv(V_T1, V_ARE, V_ARE, ALU.mult)
            vv(V_T2, V_AIM, V_AIM, ALU.mult)
            vv(V_T1, V_T1, V_T2, ALU.add)
            step(dve.reciprocal(vec(V_T1), vec(V_T1)))
            vs(V_T2, V_ABR, -1.0, ALU.add)
            vv(V_CR, V_T2, V_ARE, ALU.mult)
            vv(V_T3, V_ABI, V_AIM, ALU.mult)
            vv(V_CR, V_CR, V_T3, ALU.add)
            vv(V_CR, V_CR, V_T1, ALU.mult)
            vv(V_CI, V_ABI, V_ARE, ALU.mult)
            vv(V_T3, V_T2, V_AIM, ALU.mult)
            vv(V_CI, V_CI, V_T3, ALU.subtract)
            vv(V_CI, V_CI, V_T1, ALU.mult)
            step(dve.tensor_copy(vec(V_POW), vec(V_COS)))
            step(dve.tensor_copy(vec(V_POW + 1), vec(V_SIN)))
            for k in range(10):
                w = V_POW + 2 * k
                if k:
                    vv(V_T1, w - 2, w - 2, ALU.mult)
                    vv(V_T2, w - 1, w - 1, ALU.mult)
                    vv(w, V_T1, V_T2, ALU.subtract)
                    vv(w + 1, w - 2, w - 1, ALU.mult)
                    vs(w + 1, w + 1, 2.0, ALU.mult)
                vv(V_T1, w, w, ALU.mult)
                vv(V_T2, w + 1, w + 1, ALU.mult)
                vv(V_T1, V_T1, V_T2, ALU.add)
                vs(V_T1, V_T1, -0.5, ALU.mult, 1.5, ALU.add)
                vv(w, w, V_T1, ALU.mult)
                vv(w + 1, w + 1, V_T1, ALU.mult)

            SC = tiles(sc, N_VEC)
            SC4 = SC.rearrange("p v (b t) -> p v b t", b=4)
            HS4 = [t[:, :].rearrange("p (b t n) -> p b t n", b=4, t=4) for t in (hs_re, hs_im)]
            HF = [t[:, :].rearrange("p (tn s) -> p tn s", s=NS) for t in (hs_re, hs_im)]
            BT = bt[:, :].rearrange("p (c t l) -> p c t l", c=2, t=ST)

            def tt(out, x, y, op):
                step(dve.tensor_tensor(out, x, y, op))

            def wide(v, n):
                return SC[:, v, :].unsqueeze(2).broadcast_to([P, ST, n])

            def wide4(v):
                return SC4[:, v].unsqueeze(3).broadcast_to([P, 4, 4, SAMPLE])

            def x16(t, n):
                return t[:, 0:ST * n].rearrange("p (t n) -> p t n", t=ST)

            dve.memset(BT[:, 0, :, 0:1], 1.0)
            step(dve.memset(BT[:, 1, :, 0:1], 0.0))
            for k in range(6):
                n = 1 << k
                wr, wi = wide(V_POW + 2 * k, n), wide(V_POW + 2 * k + 1, n)
                er, ei = BT[:, 0, :, 0:n], BT[:, 1, :, 0:n]
                dve.tensor_tensor(x16(xt1, n), er, wr, ALU.mult)
                dve.tensor_tensor(x16(xt2, n), ei, wi, ALU.mult)
                dve.tensor_tensor(x16(gr, n), er, wi, ALU.mult)
                tt(x16(gi, n), ei, wr, ALU.mult)
                dve.tensor_tensor(BT[:, 0, :, n:2 * n], x16(xt1, n), x16(xt2, n), ALU.subtract)
                if k < 5:
                    tt(BT[:, 1, :, n:2 * n], x16(gr, n), x16(gi, n), ALU.add)
                else:
                    dve.tensor_tensor(BT[:, 1, :, n:2 * n], x16(gr, n), x16(gi, n), ALU.add).then_inc(powers_made, 1)
                    dve.wait_ge(powers_made, 1)

            dve.wait_ge(b_used, 1)
            br, bi_ = (psum[:, 0:4, 256 * c:256 * c + 256].rearrange("p b (t n) -> p b t n", t=4) for c in range(2))
            x1, x2 = (t[:, :].rearrange("p (b t n) -> p b t n", b=4, t=4) for t in (xt1, xt2))
            tt(x1, br, wide4(V_CR), ALU.mult)
            tt(x2, bi_, wide4(V_CI), ALU.mult)
            tt(HS4[0], x1, x2, ALU.subtract)
            tt(x1, br, wide4(V_CI), ALU.mult)
            dve.tensor_tensor(x2, bi_, wide4(V_CR), ALU.mult).then_inc(bu_used, 1)
            dve.wait_ge(bu_used, 1)
            tt(HS4[1], x1, x2, ALU.add)
            dve.tensor_copy(x16(gr, NB), wide(V_ABR, NB))
            step(dve.tensor_copy(x16(gi, NB), wide(V_ABI, NB)))
            NH = ST * NB
            abr, abi, t1, t2, t3, t4 = gr[:, 0:NH], gi[:, 0:NH], *(xt1[:, NH * i:NH * i + NH] for i in range(4))

            def advance(pr_, pi_, cr_, ci_):
                dve.tensor_tensor(t1, pr_, abr, ALU.mult)
                dve.tensor_tensor(t2, pi_, abi, ALU.mult)
                dve.tensor_tensor(t3, pr_, abi, ALU.mult)
                tt(t4, pi_, abr, ALU.mult)
                dve.tensor_tensor(t1, t1, t2, ALU.subtract)
                tt(t3, t3, t4, ALU.add)
                dve.tensor_tensor(cr_, cr_, t1, ALU.add)
                tt(ci_, ci_, t3, ALU.add)

            advance(h0[:, 0:NH], h0[:, NH:2 * NH], HF[0][:, :, 0], HF[1][:, :, 0])
            for s in range(1, NS):
                advance(HF[0][:, :, s - 1], HF[1][:, :, s - 1], HF[0][:, :, s], HF[1][:, :, s])
            for c in range(2):
                step(dve.tensor_copy(h0[:, c * NH:(c + 1) * NH], HF[c][:, :, NS - 1]))
            dve.tensor_scalar(hs_im[:, :], hs_im[:, :], -1.0, None, ALU.mult).then_inc(hs_made, 1)
            bi, bum, ysm, hus, lev, xsm, srm, pown = (
                Count(s) for s in (blk_in, bu_mm, ys_mm, h_used, level_made, xs_made, sr_made, pool_own))

            def x4(t):
                return t[:, 0:4 * P].rearrange("p (t n) -> p t n", t=4)

            with turns(dve, 2, {own: S5_STEPS, bi: 64, bum: 8, ysm: 1, hus: 8, lev: 32, xsm: 8, srm: 8, pown: 8}) as z:
                step(copy(r_blk[:, :], SC[:, V_R, bass.ds(z * 8, 8)]))
                dve.wait_ge(blk_in, bi.add(64))
                dve.wait_ge(ys_mm, ysm.add())
                for b in range(2):
                    cre, cim = (c_blk[b][:, :].rearrange("p (t c s) -> p t c s", t=4, c=2)[:, :, c, :] for c in range(2))
                    fr, fi = (SC[:, v, bass.ds(z * 8 + b * 4, 4)].unsqueeze(2).broadcast_to([P, 4, P]) for v in (V_CR, V_CI))
                    dve.tensor_tensor(x4(gr), cre, fr, ALU.mult)
                    dve.tensor_tensor(x4(gi), cim, fi, ALU.mult)
                    dve.tensor_tensor(x4(xt1), cre, fi, ALU.mult)
                    tt(x4(xt2), cim, fr, ALU.mult)
                    dve.tensor_tensor(cre, x4(gr), x4(gi), ALU.subtract)
                    ins = dve.scalar_tensor_tensor(cim, x4(xt1), -1.0, x4(xt2), ALU.mult, ALU.subtract)
                    if b == 0:
                        step(ins)
                ins.then_inc(vec_dve, 1)
                dve.wait_ge(vec_dve, z + 1)

                def skip_path(b, tokens, y):
                    return dve.scalar_tensor_tensor(ZB[:, bass.ds(z * 2 + b, 1), tokens], U[:, bass.ds(z * 2 + b, 1), tokens],
                                                    param[:, bass.ds(z * 2 + (b + C_D), 1)], y, ALU.mult, ALU.add)

                def finish(b):
                    dve.wait_ge(h_used, z * 8 + 4 * (b + 1))
                    skip_path(b, slice(SAMPLE, PADS), psum[:, 4:6, :].rearrange("p (a b) c -> p a (b c)", a=1)).then_inc(y_made, 1)

                for b in range(2):
                    skip_path(b, slice(0, SAMPLE), psum[:, 6:7, b * SAMPLE:(b + 1) * SAMPLE])
                for k in range(8):
                    t = k % 4
                    TR, TI = tr[t], ti[t]
                    dve.wait_ge(level_made, lev.add(4))
                    dve.wait_ge(bu_mm, bum.add())
                    ur, ui = psum[:, 0:2, :].rearrange("p b c -> p (b c)"), psum[:, 2:4, :].rearrange("p b c -> p (b c)")
                    dve.tensor_tensor(xt1[:, :], ur, TR[:, :], ALU.mult)
                    step(dve.tensor_tensor(xt2[:, :], ui, TI[:, :], ALU.mult))
                    tt(gr[:, :], xt1[:, :], xt2[:, :], ALU.add)
                    dve.tensor_tensor(xt1[:, :], ui, TR[:, :], ALU.mult)
                    dve.tensor_tensor(xt2[:, :], ur, TI[:, :], ALU.mult).then_inc(bu_used, 1)
                    dve.wait_ge(bu_used, z * 8 + k + 2)
                    tt(gi[:, :], xt1[:, :], xt2[:, :], ALU.subtract)
                    dve.wait_ge(pool_own, pown.at)
                    pown.add()
                    r = r_blk[:, k:k + 1].broadcast_to([P, SEQ])
                    dve.tensor_tensor_scan(xs1[:, :], r, gr[:, :], 0.0, ALU.mult, ALU.add)
                    dve.tensor_tensor_scan(xs2[:, :], r, gi[:, :], 0.0, ALU.mult, ALU.add).then_inc(xs_made, 1)
                    dve.wait_ge(xs_made, xsm.add())
                    dve.wait_ge(h_used, hus.at if k < 2 else hus.add())
                    dve.tensor_tensor(xt1[:, :], xs1[:, :], TR[:, :], ALU.mult)
                    step(dve.tensor_tensor(xt2[:, :], xs2[:, :], TI[:, :], ALU.mult))
                    dve.tensor_tensor(sr[t % 2][:, :], xt1[:, :], xt2[:, :], ALU.subtract).then_inc(sr_made, 1)
                    dve.wait_ge(sr_made, srm.add())
                    dve.tensor_copy(last[:, k:k + 1], sr[t % 2][:, SEQ - 1:SEQ])
                    if k:
                        dve.wait_ge(si_made, z * 8 + k)
                        step(dve.tensor_copy(last[:, 7 + k:8 + k], si[(k - 1) % 2][:, SEQ - 1:SEQ]))
                    if k == 5:
                        finish(0)
                hus.add(2)
                dve.wait_ge(si_made, z * 8 + 8)
                step(dve.tensor_copy(last[:, 15:16], si[1][:, SEQ - 1:SEQ]))
                copy(SC[:, V_X, bass.ds(z * 8, 8)], last[:, 0:8])
                step(copy(SC[:, V_TH, bass.ds(z * 8, 8)], last[:, 8:16]))
                finish(1)
            dve.memset(ZB[:, :, PADS:T], 0.0).then_inc(zeroed, 1)
            vv(V_T1, V_X, V_CR, ALU.mult)
            vv(V_T2, V_TH, V_CI, ALU.mult)
            vv(V_T1, V_T1, V_T2, ALU.subtract)
            vv(V_T2, V_X, V_CI, ALU.mult)
            vv(V_T3, V_TH, V_CR, ALU.mult)
            dve.tensor_tensor(vec(V_T2), vec(V_T2), vec(V_T3), ALU.add).then_inc(state_out, 1)
            for m in range(4):
                low(ZL[:, m, :], ZB[:, m, :], ZH[:, m, :])

            for m in range(4):
                dve.wait_ge(free[m % 2], UNITS_AT[W_GLU] // 2 + m // 2 + 1)
                dve.tensor_tensor(TMP[:, m % 2, :], TMP[:, m % 2, :], ZB[:, m, :], ALU.mult).then_inc(scaled, 1)
                low(HL[:, 4 + m, :], TMP[:, m % 2, :], HH[:, 4 + m, :])
            u.skip(4)

            dve.memset(HH[:, 0:4, PADS:T].bitcast(F32), 0.0)
            dve.memset(HL[:, 0:4, PADS:T].bitcast(F32), 0.0)
            low(HL[:, 0:4, 0:SAMPLE], tiles(oas, 4), HH[:, 0:4, 0:SAMPLE])
            ogl = [Count(s) for s in og_loaded]
            with turns(dve, 4, {ogl[0]: 16, ogl[1]: 16, own: 18, n_we: 2, hi: 2, lo: 2}) as t:
                for b in range(2):
                    IN = og_in[:, b * 3 * ROW:(b + 1) * 3 * ROW].rearrange("p (g c) -> p g c", g=3)
                    W = c_w[:, b * 64:b * 64 + 64]
                    acc = c_acc[:, b * 512:b * 512 + 512].rearrange("p (h d) -> p h d", h=8)
                    og_o = [IN[:, g, 0:512].rearrange("p (h d) -> p h d", h=8) for g in range(3)]
                    dve.wait_ge(og_loaded[b], ogl[b].add(16))
                    nm, ls = IN[:, :, 520:528], IN[:, :, 512:520]
                    tt(W[:, 0:8], nm[:, 0], nm[:, 1], ALU.min)
                    tt(W[:, 0:8], W[:, 0:8], nm[:, 2], ALU.min)
                    E = W[:, 32:56].rearrange("p (g h) -> p g h", g=3)
                    D = W[:, 8:32].rearrange("p (g h) -> p g h", g=3)
                    dve.tensor_tensor(D, W[:, 0:8].unsqueeze(1).broadcast_to([P, 3, 8]), nm, ALU.subtract).then_inc(w_dif, 1)
                    dve.wait_ge(w_exp, n_we.add())
                    tt(E, E, ls, ALU.mult)
                    tt(W[:, 0:8], E[:, 0], E[:, 1], ALU.add)
                    tt(W[:, 0:8], W[:, 0:8], E[:, 2], ALU.add)
                    step(dve.reciprocal(W[:, 56:64], W[:, 0:8]))
                    tt(D, E, W[:, 56:64].unsqueeze(1).broadcast_to([P, 3, 8]), ALU.mult)
                    for g in range(3):
                        ins = dve.tensor_tensor(og_o[g], og_o[g], D[:, g].unsqueeze(2).broadcast_to([P, 8, HEAD_DIM]), ALU.mult)
                    step(ins)
                    step(dve.tensor_tensor(og_o[1], og_o[0], og_o[1], ALU.add))
                    dve.tensor_tensor(acc, og_o[1], og_o[2], ALU.add).then_inc(comb_made, 1)
                for b in range(2):
                    cols = bass.ds(t * 256 + SAMPLE + P * b, P)
                    low(HL[:, 0:4, cols], psum[:, 6 + b, :].rearrange("p (k c) -> p k c", c=P), HH[:, 0:4, cols])

            for layer in range(2):
                if layer == 1:
                    u.skip(2, 2, 2, 2, 2, 4)
                    dve.wait_ge(x_made, 16 + 8)
                    dve.wait_ge(lo_made, lo.at)
                    dve.wait_ge(free[0], UNITS_AT[W_QC] // 2 + 1)
                    dve.memset(qc_st[:, :], 0.0).then_inc(zeroed, 1)
                    attend(0, H_C)
                    dve.memset(HH[:, :, PADS:T].bitcast(F32), 0.0)
                    dve.memset(HL[:, :, PADS:T].bitcast(F32), 0.0)
                    dve.wait_ge(s_mm, N_A_STEPS + N_C_STEPS)
                    step(dve.memset(qc_st[:, :], 0.0))
                    QS = qc_st[:, :].rearrange("p (n j h q) -> p n j h q", n=NB, j=2, h=16)
                    for j in range(2):
                        for o in range(2):
                            for par in range(2):
                                src = XA[64 * par:64 * par + 64, 4 * j + 2 * o:4 * j + 2 * o + 2, 0:SAMPLE]
                                h = 8 * j + 4 * o + par
                                out = QS[64 * o:64 * o + 64, :, j, h:h + 3:2, :]
                                ins = dve.tensor_scalar(out.rearrange("p n y q -> p y n q"), src.rearrange("p y (n q) -> p y n q", n=NB),
                                                        HEAD_DIM ** -0.5, None, ALU.mult)
                                if not (j and o and par):
                                    step(ins)
                    ins.then_inc(qb_made, 1)
                    dve.wait_ge(ss_mm, 9)
                    S = tiles(cs_s, 4)
                    step(dve.tensor_tensor(S, psum[:, 0:4, 0:2 * SKC], tiles(cm_sb, 4), ALU.add))
                    step(dve.tensor_reduce(cstat[:, 0:8], tiles(cs_s, NB), AX, ALU.max, negate=True))
                    dve.tensor_scalar(cstat[:, 0:8], cstat[:, 0:8], nsink[:, 16:17], None, ALU.min).then_inc(ss_max, 1)
                    dve.wait_ge(ss_exp, 5)
                    step(dve.tensor_tensor(cstat[:, 8:16], cstat[:, 8:16], cstat[:, 16:24], ALU.add))
                    step(dve.reciprocal(cstat[:, 24:32], cstat[:, 8:16]))
                    S8 = tiles(cs_s, NB)
                    dve.tensor_tensor(S8, S8, cstat[:, 24:32].unsqueeze(2).broadcast_to([P, NB, SKC]), ALU.mult).then_inc(ss_norm, 1)
                    dve.wait_ge(spv_mm, 1)
                    OC = tiles(ocs, 8)
                    O = psum[:, 0:2, :].rearrange("p b (n c) -> p (b n) c", n=4)
                    for j in range(2):
                        for o in range(2):
                            for par in range(2):
                                src = O[64 * o:64 * o + 64, :, j * 64 + o * 32 + par * 8:j * 64 + o * 32 + 32]
                                for y in range(2):
                                    ins = dve.tensor_copy(
                                        OC[64 * par:64 * par + 64, 4 * j + 2 * o + y, :].rearrange("p (n q) -> p n q", n=NB),
                                        src[:, :, y * 16:y * 16 + 8])
                                    if not (j and o and par and y):
                                        step(ins)
                    ins.then_inc(spv_taken, 1)
                    low(HL[:, :, 0:SAMPLE], OC, HH[:, :, 0:SAMPLE])
                clear_rs()
                with turns(dve, 2, {pm: 4, pa: 4}):
                    for k in range(4):
                        add_part(k % 2)
                u.skip(2, 2, 2, 2)
                residual(layer, 1)
                normalise(layer, 2)
                dve.wait_ge(x_out, 16 + 32 * layer)
                step(dve.memset(XA, 0.0))
                clear_rs()

                def ff_up(h):
                    for m in range(2):
                        u.skip_half(m)
                        dve.wait_ge(free[m], u.free[m].at)
                        dve.tensor_tensor(TMP[:, m, :], TMP[:, m, :], TMP[:, m, :], ALU.mult).then_inc(scaled, 1)
                    for m in range(2):
                        low(HIDL[h][:, m, :], TMP[:, m, :], HIDH[h][:, m, :])

                def ff_down(add_parts=False):
                    for m in range(8):
                        if m < 2:
                            dve.wait_ge(free[m % 2], u.free[m % 2].at)
                        u.wait(dve, m == 7)
                        dve.tensor_tensor(chunked(XA[:, m, :]), chunked(XA[:, m, :]), UNIT[m % 2], ALU.add).then_inc(free[m % 2], 1)
                        u.free[m % 2].add()
                        if add_parts and m:
                            add_part((m - 1) % 2)
                    if add_parts:
                        add_part(1)

                ff_up(0)
                with turns(dve, 7, {lo: 4, hi: 4, **u.per(2, 8, 2, 8)}):
                    ff_up(1)
                    ff_down()
                    ff_up(0)
                    ff_down()
                ff_up(1)
                ff_down()
                ff_down(add_parts=True)
                residual(layer, 3)
                u.skip(8)
                u.done.add()
                normalise(layer, 4)
                for m in range(8):
                    if m % 2 == 0:
                        u.skip(2)
                    dve.wait_ge(free[m % 2], u.free[m % 2].at)
                    step(dve.tensor_tensor(TMP[:, m % 2, :], TMP[:, m % 2, :], XD[:, m, :], ALU.mult))
                    dve.tensor_tensor(XA[:, m, :], XA[:, m, :], TMP[:, m % 2, :], ALU.add).then_inc(x_made, 1)
                if layer == 0:
                    normalise(1, 0)


def _layouts(i):
    import numpy as np
    f = lambda name: np.asarray(i[name])

    def ktiles(w):
        return w.reshape(-1, P, w.shape[1]).transpose(1, 0, 2)

    def feature_major(sample, prompt):
        t = np.zeros((sample.shape[-1], T), sample.dtype)
        t[:, :SAMPLE] = sample.reshape(SAMPLE, -1).T
        t[:, SAMPLE:PADS] = prompt.reshape(SEQ, -1).T
        return ktiles(t)

    out = {"xT": feature_major(f("x_sample"), f("x_prompt"))}
    wall = np.zeros((N_SLOTS, P, SLOT), f("w_ff1").dtype)

    def put(slot, w):
        w = ktiles(w).reshape(P, -1)
        wall[slot, :, :w.shape[1]] = w
        return slot + 1

    def columns(slot, w):
        for c in range(0, w.shape[1], 256):
            slot = put(slot, w[:, c:c + 256])
        return slot

    w_in = f("w_in_ab")[0]
    columns(W_U, w_in[:, 9 * 512:])
    columns(W_QKV, w_in[:, :9 * 512])
    put(W_GLU, f("w_glu")[0])
    columns(W_OUT[0], f("w_out_ab")[0])
    columns(W_QC, f("w_in_c")[0])
    columns(W_OUT[1], f("w_out_c")[0])
    for layer in range(2):
        w1, w2, s = f("w_ff1")[layer], f("w_ff2")[layer], W_FF[layer]
        up = [w1[:, 256 * k:256 * k + 256] for k in range(FF_BLOCKS)]
        down = [w2[256 * k:256 * k + 256] for k in range(FF_BLOCKS)]
        s = put(s, up[0])
        for k in range(1, FF_BLOCKS):
            s = put(s, up[k])
            s = put(s, down[k - 1])
        put(s, down[-1])
        wall[W_PLE[layer]] = feature_major(f("p_sample")[layer], f("p_prompt")[layer]).reshape(P, -1)
        put(W_PLE[layer] + 1, f("w_ple")[layer])
        columns(W_GATE[layer], f("w_ple_gate")[layer])
    out["wall"] = wall

    tri = np.arange(P)[:, None] - np.arange(P)[None, :]
    consts = np.zeros((P, 5 * P), np.float32)
    consts[:, 0:P] = np.eye(P)
    consts[:, P:2 * P] = 1
    consts[:, 2 * P:3 * P] = np.where(tri <= 0, 0, -1e30)
    consts[:, 3 * P:4 * P] = np.where(tri >= 0, 0, -1e30)
    half = np.arange(P) % 2
    consts[:, 4 * P:5 * P] = np.where((tri >= 0) & (half[:, None] == half[None, :]), 0, -1e30)
    out["consts"] = consts
    params = np.zeros((P, N_PARAM), np.float32)
    gains = np.stack([f("g_" + g) for g in GAINS], 1)
    params[:, 0:80] = gains.reshape(2, 5, KC, P).transpose(3, 0, 1, 2).reshape(P, 80)
    params[:, C_GLU:C_GLU + 4] = f("b_glu")[0].reshape(4, P).T
    params[:, C_D:C_D + 4] = f("ssm_d")[0].reshape(4, P).T
    params[:, C_SINK:C_SINK + 16] = f("sinks_c")[0][None, :]
    params[:, C_SINKROW] = np.repeat(f("sinks_c")[0], NS)
    params[:, C_EPS] = EPS
    out["params"] = params

    s = np.tile(np.arange(NS), 2 * H_A)[:, None]
    b = np.repeat(np.arange(2), 64)[:, None]
    t = np.arange(SAMPLE)[None, :]
    smask = np.zeros((4, P, SK), bool)
    for z in range(4):
        new = [(t // NS == 2 * z + b) & (t % NS <= s) & ((s - t % NS) % d == 0) for d in DILATION]
        r1, r4 = np.arange(128)[None, :], np.arange(512)[None, :]
        smask[z] = np.concatenate([r1 >= s, *new, (r4 >= s) & ((r4 - s) % 4 == 0), (np.arange(512)[None, :] // 64 == s)], 1)
    out["smask"] = np.where(smask, 0, -1e30).astype(np.float32)
    sc_ = np.tile(np.arange(NS), H_C)[:, None]
    cm = [np.concatenate([np.arange(P)[None, :] >= sc_, (t // NS == n) & (t % NS <= sc_)], 1) for n in range(NB)]
    out["cmask"] = np.where(np.concatenate(cm, 1), 0, -1e30).astype(np.float32)

    def states(x):
        return x.reshape(ST, P, *x.shape[2:]).swapaxes(0, 1)

    dt = np.repeat(f("ssm_log_dt")[0][:, None], 64, 1)
    out["ssm"] = np.stack([states(f("ssm_a_re")[0]), states(f("ssm_a_im")[0]), states(dt)], 1).reshape(P, 3 * ST)
    h0 = [states(f(k)[0].transpose(1, 2, 0)) for k in ("state_b_re", "state_b_im")]
    out["h0"] = np.stack(h0, 1).reshape(P, -1)
    bm, cm_ = np.zeros((4, P, 4, 2, P), np.float32), np.zeros((4, P, 4, 2, P), np.float32)
    for g in range(32):
        blk, gl = divmod(g, 8)
        tile, part = divmod(gl, 2)
        for c, (kb, kc) in enumerate((("ssm_b_re", "ssm_c_re"), ("ssm_b_im", "ssm_c_im"))):
            bm[blk, 16 * gl:16 * gl + 16, tile, c, 64 * part:64 * part + 64] = f(kb)[0, g].T
            cm_[blk, 64 * part:64 * part + 64, tile, c, 16 * gl:16 * gl + 16] = f(kc)[0, g].T
    out["bmat"], out["cmat"] = bm.reshape(4, P, 1024), cm_.reshape(4, P, 1024)

    def keys(c):
        n, r = c.shape[:2]
        return c.reshape(n, r, -1, P).transpose(0, 3, 2, 1).reshape(n, P, -1)

    for g, name in enumerate(("cache_a1_kv", "cache_a2_kv", "cache_a3_kv")):
        c = f(name)[0]
        k = keys(c[:, 0])
        if g == 2:
            k = k.reshape(NB, P, 4, 64, 16).swapaxes(3, 4).reshape(NB, P, -1)
        out[f"kt{g}"], out[f"v{g}"] = k, c[:, 1].reshape(NB, ROWS[g], 512)
    c = f("cache_c_kv")[0]
    out["ktc"], out["vc"] = keys(c[:, 0]), c[:, 1].reshape(NB, ROWS_C, 256)
    return out


_OUTS = {"yT": (P, KC, T), "st_s": (P, 2 * ST * NB), "st_p": (P, 2 * ST),
         **{f"okp{g}": (P, 4, r) for g, r in enumerate(ROWS)}, **{f"ovp{g}": (r, 512) for g, r in enumerate(ROWS)},
         **{f"oks{g}": (NB, P, 4, r if g == 2 else r - NS) for g, r in enumerate(ROWS)},
         **{f"ovs{g}": (NB, r - NS, 512) for g, r in enumerate(ROWS)},
         **{f"oks_new{g}": (P, 4, SAMPLE) for g in range(3)}, **{f"ovs_new{g}": (SAMPLE, 512) for g in range(3)},
         "okc_p": (P, 2, ROWS_C), "ovc_p": (ROWS_C, 256), "okc_s": (NB, P, 2, ROWS_C - NS),
         "ovc_s": (NB, ROWS_C - NS, 256), "okc_new": (P, 2, SAMPLE), "ovc_new": (SAMPLE, 256)}


def kernel(**inputs):
    import numpy as np
    import concourse.bacc as bacc
    from concourse.bass_utils import run_bass_kernel_spmd as run

    nc = bacc.Bacc("TRN2", target_bir_lowering=False, num_devices=1)
    arrays, a = {}, {}
    for name, x in _layouts(inputs).items():
        x = np.ascontiguousarray(x)
        arrays[f"in_{name}"] = x
        a[name] = nc.dram_tensor(f"in_{name}", x.shape, mybir.dt.from_np(x.dtype), kind="ExternalInput").ap()
    for name, shape in _OUTS.items():
        a[name] = nc.dram_tensor(f"out_{name}", shape, F32, kind="ExternalOutput").ap()
    for name in ("kt", "v", "okp", "ovp", "oks", "ovs", "oks_new", "ovs_new"):
        a[name] = [a[f"{name}{g}"] for g in range(3)]
    build(nc, a)
    r = run(nc, [arrays], core_ids=[0]).results[0]
    o = {name: r[f"out_{name}"] for name in _OUTS}

    y = o["yT"].transpose(2, 1, 0).reshape(T, D_MODEL)
    outs = [y[SAMPLE:PADS].reshape(1, SEQ, D_MODEL), y[:SAMPLE].reshape(NB, NS, D_MODEL)]

    def prompt(k, v, heads):
        k = k.transpose(2, 1, 0).reshape(v.shape)
        return np.stack([k, v]).reshape(1, 1, 2, -1, heads, HEAD_DIM)

    def sample(k, k_new, v, v_new, heads):
        k = k.transpose(0, 3, 2, 1).reshape(v.shape)
        k_new = k_new.transpose(2, 1, 0).reshape(NB, NS, -1)
        k = np.concatenate([k, k_new], 1)
        v = np.concatenate([v, v_new.reshape(NB, NS, -1)], 1)
        return np.stack([k, v], 1).reshape(1, NB, 2, -1, heads, HEAD_DIM)

    for g in range(3):
        outs.append(prompt(o[f"okp{g}"], o[f"ovp{g}"], H_A))
        if g == 2:
            o["oks2"] = o["oks2"].reshape(NB, P, 4, 16, 64).swapaxes(3, 4).reshape(NB, P, 4, -1)[..., NS:]
        outs.append(sample(o[f"oks{g}"], o[f"oks_new{g}"], o[f"ovs{g}"], o[f"ovs_new{g}"], H_A))
    st_p = o["st_p"].reshape(P, 2, ST).transpose(1, 2, 0).reshape(2, 1, 1, 32, N_STATE)
    st_s = o["st_s"].reshape(P, 2, ST, NB).transpose(1, 3, 2, 0).reshape(2, 1, NB, 32, N_STATE)
    outs += [st_p[0], st_s[0], st_p[1], st_s[1]]
    outs.append(prompt(o["okc_p"], o["ovc_p"], 4))
    outs.append(sample(o["okc_s"], o["okc_new"], o["ovc_s"], o["ovc_new"], 4))
    return tuple(outs)
```
